# Optimizing a Trainium2 kernel written in Bass

```python
import math
import jax
import jax.numpy as jnp
from jax import lax
import numpy as np

D_MODEL = 1024
BATCH = 1
SEQ = 512
DEPTH = 1
DEC_BATCH = 8
DEC_SEQ = 1
PAST_LEN = 4096
PAGE_SIZE = 128

D_RNN = D_MODEL
RG_BLOCKS = 16
RG_BW = D_RNN // RG_BLOCKS
CONV_W = 4
RG_C = 8.0
GLA_HEADS = 4
GLA_DK = D_MODEL // 2
GLA_DV = D_MODEL
GLA_DKH = GLA_DK // GLA_HEADS
GLA_DVH = GLA_DV // GLA_HEADS
GLA_RANK = 16
GLA_TAU = 16.0
GLA_CHUNK = 64
N_GROUPS = 4
EXP_PER_GROUP = 8
N_EXPERTS = N_GROUPS * EXP_PER_GROUP
D_EXPERT = 512
TOP_K = 2
MOE_BLOCK = 128
ALPHA = (2.0 * DEPTH) ** 0.25
BETA = (8.0 * DEPTH) ** -0.25
LN_EPS = 1e-5
RMS_EPS = 1e-6
N_IN = 2 * D_RNN + 2 * GLA_DK + 2 * GLA_DV + GLA_RANK + 2 * D_MODEL

kernel_name = 'hawk_gla_hiermoe_deepnorm_adaln_step'

F32 = jnp.float32

def _ln(x):
    xf = x.astype(F32)
    mu = jnp.mean(xf, -1, keepdims=True)
    var = jnp.mean(jnp.square(xf - mu), -1, keepdims=True)
    return (xf - mu) * lax.rsqrt(var + LN_EPS)

def layer_norm(x, g, b):
    return (_ln(x) * g.astype(F32) + b.astype(F32)).astype(x.dtype)

def modulate(x, shift, scale):
    return (_ln(x) * (1.0 + scale.astype(F32)) + shift.astype(F32)).astype(x.dtype)

def causal_conv(x, buf, w, b):
    T = x.shape[1]
    xp = jnp.concatenate([buf.astype(x.dtype), x], axis=1)
    y = b
    for i in range(CONV_W):
        y = y + xp[:, i:i + T] * w[i]
    return y, xp[:, -(CONV_W - 1):]

def _lin_combine(left, right):
    a1, b1 = left
    a2, b2 = right
    return a1 * a2, a2 * b1 + b2

def rg_lru(x, h0, wa, ba, wx, bx, lam):
    B, T, _ = x.shape
    xf = x.astype(F32)
    xb = xf.reshape(B, T, RG_BLOCKS, RG_BW)
    r = jax.nn.sigmoid(jnp.einsum('btnc,ncd->btnd', xb, wa.astype(F32)).reshape(B, T, D_RNN) + ba.astype(F32))
    i = jax.nn.sigmoid(jnp.einsum('btnc,ncd->btnd', xb, wx.astype(F32)).reshape(B, T, D_RNN) + bx.astype(F32))
    log_a = -RG_C * r * jax.nn.softplus(-lam.astype(F32))
    a = jnp.exp(log_a)
    u = jnp.sqrt(-jnp.expm1(2.0 * log_a)) * (i * xf)
    u = u.at[:, 0].add(a[:, 0] * h0.astype(F32))
    _, h = lax.associative_scan(_lin_combine, (a, u), axis=1)
    return h, h[:, -1]

def gla_chunked(q, k, v, la, S0):
    B, H, T, dk = q.shape
    dv = v.shape[-1]
    pad = (-T) % GLA_CHUNK
    if pad:
        pw = ((0, 0), (0, 0), (0, pad), (0, 0))
        q, k, v, la = jnp.pad(q, pw), jnp.pad(k, pw), jnp.pad(v, pw), jnp.pad(la, pw)
    n = (T + pad) // GLA_CHUNK
    C = GLA_CHUNK
    qc = q.reshape(B, H, n, C, dk)
    kc = k.reshape(B, H, n, C, dk)
    vc = v.reshape(B, H, n, C, dv)
    bcum = jnp.cumsum(la.reshape(B, H, n, C, dk), axis=3)
    btot = bcum[:, :, :, -1, :]
    q_in = qc * jnp.exp(bcum)
    k_in = kc * jnp.exp(-bcum)
    tri = jnp.tril(jnp.ones((C, C), dtype=bool))
    attn = jnp.where(tri, jnp.einsum('bhnik,bhnjk->bhnij', q_in, k_in), 0.0)
    intra = jnp.einsum('bhnij,bhnjv->bhniv', attn, vc)
    k_out = kc * jnp.exp(btot[:, :, :, None, :] - bcum)
    dS = jnp.einsum('bhnjk,bhnjv->bhnkv', k_out, vc)

    def step(S, inp):
        dec, ds = inp
        return S * dec[..., None] + ds, S

    S_fin, S_starts = lax.scan(step, S0, (jnp.moveaxis(jnp.exp(btot), 2, 0), jnp.moveaxis(dS, 2, 0)))
    S_starts = jnp.moveaxis(S_starts, 0, 2)
    inter = jnp.einsum('bhnik,bhnkv->bhniv', q_in, S_starts)
    o = (intra + inter).reshape(B, H, n * C, dv)[:, :, :T]
    return o, S_fin

def gla_recurrent(q, k, v, la, S0):
    def step(S, inp):
        qt, kt, vt, lat = inp
        S = S * jnp.exp(lat)[..., None] + kt[..., :, None] * vt[..., None, :]
        return S, jnp.einsum('bhk,bhkv->bhv', qt, S)

    mv = lambda t: jnp.moveaxis(t, 2, 0)
    S_fin, o = lax.scan(step, S0, (mv(q), mv(k), mv(v), mv(la)))
    return jnp.moveaxis(o, 0, 2), S_fin

def hier_moe(h, w_grp, b_grp, w_exp, b_exp, we_gate, we_up, we_down):
    N, D = h.shape
    grp_logits = (h @ w_grp + b_grp).astype(F32)
    grp_p = jax.nn.softmax(grp_logits, axis=-1)
    g_sel = jnp.argmax(grp_logits, axis=-1)
    g_w = jnp.take_along_axis(grp_p, g_sel[:, None], axis=-1)[:, 0]
    exp_logits = (h @ w_exp + b_exp).astype(F32).reshape(N, N_GROUPS, EXP_PER_GROUP)
    sel_logits = jnp.take_along_axis(exp_logits, g_sel[:, None, None], axis=1)[:, 0]
    top_v, top_i = lax.top_k(sel_logits, TOP_K)
    e_w = jax.nn.softmax(top_v, axis=-1) * g_w[:, None]
    e_id = g_sel[:, None] * EXP_PER_GROUP + top_i
    A = N * TOP_K
    flat_e = e_id.reshape(A)
    flat_w = e_w.reshape(A)
    flat_tok = jnp.repeat(jnp.arange(N, dtype=jnp.int32), TOP_K)
    order = jnp.argsort(flat_e)
    se, stok, sw = flat_e[order], flat_tok[order], flat_w[order]
    counts = jnp.bincount(flat_e, length=N_EXPERTS)
    starts = jnp.cumsum(counts) - counts
    pcounts = (counts + MOE_BLOCK - 1) // MOE_BLOCK * MOE_BLOCK
    pends = jnp.cumsum(pcounts)
    pstarts = pends - pcounts
    dest = pstarts[se] + jnp.arange(A) - starts[se]
    n_blocks = -(-(A + N_EXPERTS * (MOE_BLOCK - 1)) // MOE_BLOCK)
    P = n_blocks * MOE_BLOCK
    x_buf = jnp.zeros((P, D), h.dtype).at[dest].set(h[stok])
    tok_buf = jnp.zeros((P,), jnp.int32).at[dest].set(stok)
    w_buf = jnp.zeros((P,), F32).at[dest].set(sw)
    blk_e = jnp.minimum(jnp.searchsorted(pends, jnp.arange(n_blocks) * MOE_BLOCK, side='right'), N_EXPERTS - 1)

    def expert_block(args):
        xb, e = args
        return (jax.nn.silu(xb @ we_gate[e]) * (xb @ we_up[e])) @ we_down[e]

    y_buf = lax.map(expert_block, (x_buf.reshape(n_blocks, MOE_BLOCK, D), blk_e)).reshape(P, D)
    return jax.ops.segment_sum(y_buf * w_buf[:, None].astype(y_buf.dtype), tok_buf, num_segments=N)

def trunk_layer(x, c, conv_buf, h0, S0, p, chunked):
    B, T, _ = x.shape
    mod = jax.nn.silu(c) @ p['w_mod'] + p['b_mod']
    sh1, sc1, g1, sh2, sc2, g2 = [m[:, None, :] for m in jnp.split(mod, 6, axis=-1)]
    hmix = modulate(x, sh1, sc1)
    proj = jnp.einsum('btd,dn->btn', hmix, p['w_in']) + p['b_in']
    widths = [D_RNN, D_RNN, GLA_DK, GLA_DK, GLA_DV, GLA_DV, GLA_RANK, D_MODEL]
    offs = [int(o) for o in np.cumsum(widths)]
    rx, ry, q, k, v, gg, alr, gate_a, gate_b = jnp.split(proj, offs, axis=-1)
    xc, conv_new = causal_conv(rx, conv_buf, p['conv_w'], p['conv_b'])
    hr, h_last = rg_lru(xc, h0, p['rg_wa'], p['rg_ba'], p['rg_wx'], p['rg_bx'], p['rg_lambda'])
    y_a = hr.astype(x.dtype) * jax.nn.gelu(ry)
    la = jax.nn.log_sigmoid((alr @ p['gla_wa2'] + p['gla_ba']).astype(F32)) / GLA_TAU

    def heads(t, dh):
        return t.reshape(B, T, GLA_HEADS, dh).transpose(0, 2, 1, 3).astype(F32)

    qh = heads(q, GLA_DKH) * (GLA_DKH ** -0.5)
    kh, vh, lah = heads(k, GLA_DKH), heads(v, GLA_DVH), heads(la, GLA_DKH)
    gla_fn = gla_chunked if chunked else gla_recurrent
    o, S_new = gla_fn(qh, kh, vh, lah, S0.astype(F32))
    o = o * lax.rsqrt(jnp.mean(jnp.square(o), -1, keepdims=True) + RMS_EPS) * p['gla_norm_g'].astype(F32)
    o = o.transpose(0, 2, 1, 3).reshape(B, T, GLA_DV).astype(x.dtype)
    y_b = o * jax.nn.silu(gg)
    merged = jax.nn.sigmoid(gate_a) * (y_a @ p['p_a']) + jax.nn.sigmoid(gate_b) * (y_b @ p['p_b'])
    mix = merged @ p['w_o']
    x = layer_norm(ALPHA * x + g1 * mix, p['ln1_g'], p['ln1_b'])
    hf = modulate(x, sh2, sc2).reshape(B * T, D_MODEL)
    ff = hier_moe(hf, p['w_grp'], p['b_grp'], p['w_exp'], p['b_exp'],
                  p['we_gate'], p['we_up'], p['we_down']).reshape(B, T, D_MODEL)
    x = layer_norm(ALPHA * x + g2 * ff, p['ln2_g'], p['ln2_b'])
    return x, conv_new.astype(x.dtype), h_last.astype(x.dtype), S_new.astype(x.dtype)

def setup_inputs(seed: int = 0) -> dict:
    key = jax.random.key(seed)
    ks = iter(jax.random.split(key, 48))
    L = DEPTH

    def nrm(shape, scale):
        return jax.random.normal(next(ks), shape, F32) * scale

    u = jax.random.uniform(next(ks), (L, D_RNN), F32, minval=0.9, maxval=0.999)
    a0 = u ** (1.0 / RG_C)
    rg_lambda = jnp.log(a0) - jnp.log1p(-a0)
    return {
        'x_prompt': nrm((BATCH, SEQ, D_MODEL), 1.0),
        'x_sample': nrm((DEC_BATCH, DEC_SEQ, D_MODEL), 1.0),
        'state_conv': nrm((L, DEC_BATCH, CONV_W - 1, D_RNN), 1.0),
        'state_rglru': nrm((L, DEC_BATCH, D_RNN), 0.5),
        'state_gla': nrm((L, DEC_BATCH, GLA_HEADS, GLA_DKH, GLA_DVH), 0.5),
        'c_prompt': nrm((BATCH, D_MODEL), 1.0),
        'c_sample': nrm((DEC_BATCH, D_MODEL), 1.0),
        'w_mod': nrm((L, D_MODEL, 6 * D_MODEL), D_MODEL ** -0.5),
        'b_mod': nrm((L, 6 * D_MODEL), 0.02),
        'w_in': nrm((L, D_MODEL, N_IN), D_MODEL ** -0.5),
        'b_in': nrm((L, N_IN), 0.02),
        'conv_w': nrm((L, CONV_W, D_RNN), CONV_W ** -0.5),
        'conv_b': nrm((L, D_RNN), 0.02),
        'rg_wa': nrm((L, RG_BLOCKS, RG_BW, RG_BW), RG_BW ** -0.5),
        'rg_ba': nrm((L, D_RNN), 0.02),
        'rg_wx': nrm((L, RG_BLOCKS, RG_BW, RG_BW), RG_BW ** -0.5),
        'rg_bx': nrm((L, D_RNN), 0.02),
        'rg_lambda': rg_lambda,
        'gla_wa2': nrm((L, GLA_RANK, GLA_DK), GLA_RANK ** -0.5),
        'gla_ba': nrm((L, GLA_DK), 0.02),
        'gla_norm_g': 1.0 + nrm((L, GLA_DVH), 0.02),
        'p_a': nrm((L, D_RNN, D_MODEL), BETA * D_RNN ** -0.5),
        'p_b': nrm((L, GLA_DV, D_MODEL), BETA * GLA_DV ** -0.5),
        'w_o': nrm((L, D_MODEL, D_MODEL), BETA * D_MODEL ** -0.5),
        'ln1_g': 1.0 + nrm((L, D_MODEL), 0.02),
        'ln1_b': nrm((L, D_MODEL), 0.02),
        'w_grp': nrm((L, D_MODEL, N_GROUPS), D_MODEL ** -0.5),
        'b_grp': nrm((L, N_GROUPS), 0.01),
        'w_exp': nrm((L, D_MODEL, N_EXPERTS), D_MODEL ** -0.5),
        'b_exp': nrm((L, N_EXPERTS), 0.01),
        'we_gate': nrm((L, N_EXPERTS, D_MODEL, D_EXPERT), D_MODEL ** -0.5),
        'we_up': nrm((L, N_EXPERTS, D_MODEL, D_EXPERT), D_MODEL ** -0.5),
        'we_down': nrm((L, N_EXPERTS, D_EXPERT, D_MODEL), BETA * D_EXPERT ** -0.5),
        'ln2_g': 1.0 + nrm((L, D_MODEL), 0.02),
        'ln2_b': nrm((L, D_MODEL), 0.02),
    }

def reference(x_prompt, x_sample, state_conv, state_rglru, state_gla, c_prompt, c_sample,
              w_mod, b_mod, w_in, b_in, conv_w, conv_b, rg_wa, rg_ba, rg_wx, rg_bx, rg_lambda,
              gla_wa2, gla_ba, gla_norm_g, p_a, p_b, w_o, ln1_g, ln1_b,
              w_grp, b_grp, w_exp, b_exp, we_gate, we_up, we_down, ln2_g, ln2_b):
    yp, ys = x_prompt, x_sample
    bp = x_prompt.shape[0]
    conv_p, rg_p, gla_p, conv_s, rg_s, gla_s = [], [], [], [], [], []
    for l in range(DEPTH):
        prm = {
            'w_mod': w_mod[l], 'b_mod': b_mod[l], 'w_in': w_in[l], 'b_in': b_in[l],
            'conv_w': conv_w[l], 'conv_b': conv_b[l], 'rg_wa': rg_wa[l], 'rg_ba': rg_ba[l],
            'rg_wx': rg_wx[l], 'rg_bx': rg_bx[l], 'rg_lambda': rg_lambda[l],
            'gla_wa2': gla_wa2[l], 'gla_ba': gla_ba[l], 'gla_norm_g': gla_norm_g[l],
            'p_a': p_a[l], 'p_b': p_b[l], 'w_o': w_o[l], 'ln1_g': ln1_g[l], 'ln1_b': ln1_b[l],
            'w_grp': w_grp[l], 'b_grp': b_grp[l], 'w_exp': w_exp[l], 'b_exp': b_exp[l],
            'we_gate': we_gate[l], 'we_up': we_up[l], 'we_down': we_down[l],
            'ln2_g': ln2_g[l], 'ln2_b': ln2_b[l],
        }
        zc = jnp.zeros((bp, CONV_W - 1, D_RNN), x_prompt.dtype)
        zh = jnp.zeros((bp, D_RNN), x_prompt.dtype)
        zs = jnp.zeros((bp, GLA_HEADS, GLA_DKH, GLA_DVH), x_prompt.dtype)
        yp, cp, hp, sp = trunk_layer(yp, c_prompt, zc, zh, zs, prm, True)
        ys, cs, hs, ss = trunk_layer(ys, c_sample, state_conv[l], state_rglru[l], state_gla[l], prm, False)
        conv_p.append(cp); rg_p.append(hp); gla_p.append(sp)
        conv_s.append(cs); rg_s.append(hs); gla_s.append(ss)
    new_conv_p = jnp.stack(conv_p, 0)
    new_rglru_p = jnp.stack(rg_p, 0)
    new_gla_p = jnp.stack(gla_p, 0)
    new_conv_s = jnp.stack(conv_s, 0)
    new_rglru_s = jnp.stack(rg_s, 0)
    new_gla_s = jnp.stack(gla_s, 0)
    return (yp, ys, new_conv_p, new_rglru_p, new_gla_p, new_conv_s, new_rglru_s, new_gla_s)


_drawn_inputs = setup_inputs


def setup_inputs(seed=0):
    import zlib

    import numpy as np

    out = dict(_drawn_inputs(seed))
    spreads = {}
    factors = {'rg_ba': 8.0,
     'rg_bx': 6.866,
     'gla_ba': 5.612,
     'gla_norm_g': 33.748,
     'b_grp': 7.373,
     'b_exp': 21.875,
     'ln2_g': 22.772,
     'ln2_b': 22.91}
    for name, (base, spread) in spreads.items():
        noise = np.random.default_rng([zlib.crc32(name.encode()), seed]).standard_normal(out[name].shape)
        drawn = base * np.exp(spread * noise) if base else spread * noise
        out[name] = jnp.asarray(drawn.astype(out[name].dtype))
    for name, factor in factors.items():
        out[name] = (out[name] * factor).astype(out[name].dtype)
    return out
```

```python
from contextlib import ExitStack

import concourse.bass as bass
from concourse import mybir

F32 = mybir.dt.float32
I32 = mybir.dt.int32
ACT = mybir.ActivationFunctionType
ALU = mybir.AluOpType
AX = mybir.AxisListType.X

P = 128
D = 1024
KD = D // P
T = 512
NS = 8
NT = T + NS
HALF = NT // 2
TILES = 5
CONV = 4
HEADS = 4
DKH = 128
DVH = 256
CH = 64
NCH = T // CH
RANK = 16
TAU = 16.0
NG = 4
EPG = 8
NE = NG * EPG
DE = 512
CAP = 64
PAIRS = 2 * NT
NBLK = 48
TW = NBLK + 2
SPLITS = 9
OOB = 1 << 20
ALPHA = 2.0 ** 0.25
LN_EPS = 1e-5
RMS_EPS = 1e-6
BIG = 1e30
WT = KD * 512

R_C = 0
R_CONVST = 9
R_H0 = 33
R_CONVW = 41
R_CONVB = 45
R_BA = 46
R_BX = 47
R_LAM = 48
R_BIN = 49
R_MISC = 56
ROWS = 57


def plan_jobs():
    jobs = [("pack", 0)] + [("xt", i) for i in range(TILES)]
    jobs += [("mod", m) for m in range(6)] + [("modT", 0)] + [("mod", m) for m in range(6, 12)]
    for g in range(2):
        jobs += [("rx", c) for c in range(4 * g, 4 * g + 4)]
        for c in range(4 * g, 4 * g + 4):
            jobs += [("ry", c), ("ra", c), ("ri", c)]
    jobs += [("qk", c) for c in range(8)] + [("al", 0)] + [("la", c) for c in range(HEADS)]
    for c in range(8):
        jobs.append(("v", c))
        if c:
            jobs.append(("vt", c - 1))
    jobs.append(("vt", 7))
    jobs += [("kt", i) for i in range(4)]
    for n in range(NCH):
        jobs += [("ds", n), ("vb", n), ("os", n)]
    jobs += [("ss", 0), ("ss", 1), ("gg", 0), ("ss", 2), ("gg", 1), ("ss", 3)]
    jobs += [("gg", c) for c in range(2, 8)]
    for a, b in (("ga", "pa"), ("gb", "pb")):
        for g in range(2):
            jobs += [(a, c) for c in range(4 * g, 4 * g + 4)] + [(b, c) for c in range(4 * g, 4 * g + 4)]
    jobs += [("bc", v) for v in range(4)] + [("rlT", 0), ("hlT", 0)]
    for i in range(TILES):
        jobs.append(("wo", i))
        if i >= 1:
            jobs += [("ht", i - 1), ("lg", i - 1)]
    jobs += [("ht", 4), ("lg", 4), ("rk", 0)]
    return jobs


JOBS = plan_jobs()
INDEX = {job: n for n, job in enumerate(JOBS)}
WTILES = ([("w_mod", m * 512) for m in range(12)]
          + [("w_in", c) for c in (0, 1024, 512, 1536, 2048, 2560, 3072, 3584, 4096, 4608)]
          + [("w_in", 5136), ("p_a", 0), ("w_in", 5136 + 512), ("p_a", 512)]
          + [("w_in", 6160), ("p_b", 0), ("w_in", 6160 + 512), ("p_b", 512)]
          + [("w_o", 0), ("w_o", 512)])
MOD_TILES = 12


def ring_slot(t):
    return t % 3 if t < MOD_TILES else t % 2


def ring_plan():
    last, turns, plan = {}, {}, []
    for t in range(len(WTILES)):
        s = ring_slot(t)
        turns[s] = turns.get(s, 0) + 1
        plan.append((s, last.get(s), turns[s]))
        last[s] = t
    return plan


RING = ring_plan()


def build(nc, t, outs):
    (y_prompt, y_sample, new_conv_p, new_rg_p, new_gla_p, new_conv_s, new_rg_s, new_gla_s) = outs
    hf_dram = nc.dram_tensor("hf_scratch", (NT, D), F32, kind="Internal").ap()
    table_dram = nc.dram_tensor("table_scratch", (CAP * TW, 2), I32, kind="Internal").ap()
    pair_dram = nc.dram_tensor("pair_scratch", (PAIRS, D), F32, kind="Internal").ap()

    with ExitStack() as ctx:
        sem_names = {}

        def sem(name):
            sem_names[name] = ctx.enter_context(nc.semaphore(name))
            return sem_names[name]

        MEM = 53100
        mem = ctx.enter_context(nc.sbuf_tensor("mem", [P, MEM], F32))
        ps = ctx.enter_context(nc.psum_tensor("ps", [P, 8, 512], F32))

        def area(at, *shape):
            n = 1
            for s in shape:
                n *= s
            v = mem[:, at:at + n]
            if len(shape) == 2:
                v = v.rearrange("p (a b) -> p a b", b=shape[1])
            if len(shape) == 3:
                v = v.rearrange("p (a b c) -> p a b c", b=shape[1], c=shape[2])
            return v

        ring = [area(s * WT, KD, 512) for s in range(6)]
        B = 3 * WT
        hT = area(B, KD, NT)
        O = area(B + 4160, KD, NT)
        TB = B + 8320
        xn = [area(TB + 1024 * j, D) for j in range(2)]
        packrows = area(TB + 2048, D)
        v_tok = area(2 * WT, 4, D)
        bd = [area(2 * WT + 1024 * j, KD, P) for j in range(2)]
        x_tok = area(6 * WT, TILES, D)
        mod_sb = area(6 * WT + 5120, 6 * D)
        A0 = 6 * WT + 5120 + 6144
        A = area(A0, KD, NT)
        Q = area(A0 + 4160, KD, NT)
        Z0 = A0 + 8320
        Z = area(Z0, KD, NT)
        L = area(Z0, HEADS, NT)
        K2 = area(Z0 + 2080, HEADS, NT)
        EX = area(TB, HEADS, NT)
        rg = {n: [area(Z0 + (2 * i + j) * NT, NT) for j in range(2)]
              for i, n in enumerate(("xc", "r", "i", "a"))}
        rg["th"] = [area(TB + j * NT, NT) for j in range(2)]
        rg["sq"] = [area(TB + (2 + j) * NT, NT) for j in range(2)]
        vf = [area(Z0 + j * NT, NT) for j in range(2)]
        S = [area(Z0, HEADS, DVH), area(Z0 + 1040, HEADS, DVH)]
        kout_tok = area(Z0 + 2080, 4, 512)
        st = [area(TB + 1024 * j, HEADS, DVH) for j in range(2)]
        attm = [area(TB + 2048 + 256 * j, HEADS, CH) for j in range(2)]
        sq = [area(TB + 1040 * j, 2, NT) for j in range(2)]
        rms = [area(Z0 + 2080 + NT * j, NT) for j in range(2)]
        gt = [area(Z0 + 3120 + NT * j, NT) for j in range(2)]
        bc = area(A0, 4, D)
        lnp = area(A0 + 4160, 2, D)
        hf = [area(A0 + 4160 + 2048 + 1024 * j, D) for j in range(2)]
        lt = [area(B + 4160 + 1024 * j, D) for j in range(2)]
        hfT = [area(B + 1024 * j, KD, P) for j in range(2)]
        xT = [area(Z0 + 512 * j, KD, CAP) for j in range(2)]
        sg = [area(Z0 + 1024 + 512 * j, DE) for j in range(2)]
        act = [area(Z0 + 2048 + 512 * j, DE) for j in range(2)]
        acT = [area(Z0 + 3072 + 256 * j, 4, CAP) for j in range(2)]
        xg = [area(A0 + 4160 + 1024 * j, D) for j in range(2)]
        yb = [area(A0 + 4160 + 2048 + 1024 * j, D) for j in range(2)]
        ln2 = area(0, 2, D)
        yp = [area(WT + 2048 * i, 2, D) for i in range(TILES)]
        ft = [area(4 * WT + 1024 * j, D) for j in range(TILES)]
        small = [Z0 + 4160]

        def keep(*shape):
            n = 1
            for s in shape:
                n *= s
            v = area(small[0], *shape)
            small[0] += n
            assert small[0] <= MEM, small[0]
            return v

        ident = keep(P)
        ones = keep(P)
        upper = keep(P)
        maskT = keep(CH)
        sel8 = keep(P)
        fp = keep(KD, ROWS)
        cs = keep(KD, 9)
        modT = keep(16, 9)
        alpha_w = keep(KD, RANK)
        route_w = keep(KD, NG + NE)
        route_b = keep(NG + NE)
        lam = keep(6, 8)
        rl = keep(KD, 11)
        hl = keep(KD, 9)
        tmp8 = keep(4, 8)
        qs = keep(HEADS, NS)
        ela = keep(HEADS, NS)
        dec = keep(HEADS, NCH)
        bt = keep(HEADS, NCH)
        stats = keep(2, 6)
        mv = keep(4)
        wpair = keep(TILES, 2)
        wa2 = area(2 * WT + 2048, 512)
        al = area(2 * WT + 2560, NT)
        scan_mask = area(2 * WT + 3080, NT)
        v_samp = area(2 * WT, D)
        v_samp = keep(D)
        rt = [TB]

        def rtmp(*shape):
            n = 1
            for s in shape:
                n *= s
            v = area(rt[0], *shape)
            rt[0] += n
            assert rt[0] <= TB + 3968
            return v

        LG = rtmp(TILES, NG + NE)
        j4 = rtmp(NG)
        j32 = rtmp(NE)
        m64 = rtmp(SPLITS)
        g_eq = rtmp(TILES, NG)
        g_e = rtmp(TILES, NG)
        g_m = rtmp(12, TILES)
        ml = rtmp(TILES, NE)
        e_eq = rtmp(TILES, NE)
        OH = rtmp(TILES, 2, NE)
        M = rtmp(TILES, NE)
        rank = rtmp(TILES, NE)
        cnt = rtmp(4, NE)
        many = rtmp(NE, SPLITS)
        prod = rtmp(TILES, 2, NE)
        r1 = rtmp(TILES, 2)
        b1 = rtmp(TILES, 2)
        q1 = rtmp(TILES, 2)
        ge = rtmp(TILES * 2, SPLITS - 1)
        blk_f = rtmp(NBLK)
        iota_i = rtmp(64)
        addr_f = rtmp(TILES, 2)
        addr_i = keep(TILES, 2).bitcast(I32)
        payload = keep(TILES, 2, 2).bitcast(I32)
        blk_i = keep(NBLK + 1).bitcast(I32)
        idx = area(Z0 + 3584, TW, 2).bitcast(I32)
        gidx = [area(Z0 + 3700 + j, 1).bitcast(I32) for j in range(2)]
        sidx = [area(Z0 + 3702 + j, 1).bitcast(I32) for j in range(2)]
        oobt = area(2 * WT, TW * 2).bitcast(I32)
        outrow = area(2 * WT + 1024, 2, D)

        job_done = sem("job_done")
        slot_free = [sem(f"slot_free{s}") for s in range(3)]
        w_in_slot = [sem(f"w_in_slot{s}") for s in range(3)]
        w_used = sem("w_used")
        rows_clear = sem("rows_clear")
        pack_in = sem("pack_in")
        x_in = sem("x_in")
        bmod_in = sem("bmod_in")
        small_in = sem("small_in")
        bd_clear = sem("bd_clear")
        bd_in = sem("bd_in")
        consts = sem("consts")
        pool_step = sem("pool_step")
        act_step = sem("act_step")
        dve_step = sem("dve_step")
        xn_ready = sem("xn_ready")
        rstd_q = sem("rstd_q")
        rstd_a = sem("rstd_a")
        cs_ready = sem("cs_ready")
        x_tr = sem("x_tr")
        modT_ready = sem("modT_ready")
        hT_act = sem("hT_act")
        hT_dve = sem("hT_dve")
        lam_q = sem("lam_q")
        lam_a = sem("lam_a")
        lam_ready = sem("lam_ready")
        rx_ready = sem("rx_ready")
        ry_ready = sem("ry_ready")
        xc_ready = sem("xc_ready")
        gates_ready = sem("gates_ready")
        th_ready = sem("th_ready")
        sqrt_ready = sem("sqrt_ready")
        ya_ready = sem("ya_ready")
        qk_ready = sem("qk_ready")
        al_ready = sem("al_ready")
        lax_ready = sem("lax_ready")
        nabs_ready = sem("nabs_ready")
        log_ready = sem("log_ready")
        bcum_ready = sem("bcum_ready")
        e1_ready = sem("e1_ready")
        dexp_q = sem("dexp_q")
        e2_ready = sem("e2_ready")
        gla_in_ready = sem("gla_in_ready")
        vf_ready = sem("vf_ready")
        vt_ready = sem("vt_ready")
        kt_ready = sem("kt_ready")
        at_done = sem("at_done")
        attm_ready = sem("attm_ready")
        o_done = sem("o_done")
        o_copied = sem("o_copied")
        s_ready = sem("s_ready")
        st_in = [sem(f"st_in{j}") for j in range(2)]
        st_ready = sem("st_ready")
        st_out = [sem(f"st_out{j}") for j in range(2)]
        os_copied = sem("os_copied")
        sq_ready = sem("sq_ready")
        var_ready = sem("var_ready")
        rms_ready = sem("rms_ready")
        gt_ready = sem("gt_ready")
        yb_ready = sem("yb_ready")
        sig_ready = sem("sig_ready")
        z_ready = sem("z_ready")
        s_out = sem("s_out")
        outs_ready = sem("outs_ready")
        lnp_in = sem("lnp_in")
        hf_ready = sem("hf_ready")
        hf_out = [sem(f"hf_out{j}") for j in range(2)]
        hfT_ready = sem("hfT_ready")
        ge_q = sem("ge_q")
        ge_a = sem("ge_a")
        m_ready = sem("m_ready")
        iotas = sem("iotas")
        addr_ready = sem("addr_ready")
        table_clear = sem("table_clear")
        oob_ready = sem("oob_ready")
        table_filled = sem("table_filled")
        blocks_ready = sem("blocks_ready")
        pair = lambda name: [sem(f"{name}{j}") for j in range(2)]
        we_in = [sem(f"we_in{s}") for s in range(6)]
        xg_clear = sem("xg_clear")
        idx_copied = sem("idx_copied")
        xg_in = pair("xg_in")
        moved = pair("moved")
        xt_done = pair("xt_done")
        xT_ready = pair("xT_ready")
        gu_done = pair("gu_done")
        sg_ready = pair("sg_ready")
        act_ready = pair("act_ready")
        tr_done = pair("tr_done")
        acT_ready = pair("acT_ready")
        dn_done = pair("dn_done")
        y_ready = pair("y_ready")
        started = sem("started")
        scattered = sem("scattered")
        pe_turns = sem("pe_turns")
        pool_turns = sem("pool_turns")
        ln2_in = sem("ln2_in")
        yp_in = [sem(f"yp_in{i}") for i in range(TILES)]
        yw_ready = sem("yw_ready")
        fin_q = sem("fin_q")
        fin_a = sem("fin_a")
        norm_ready = sem("norm_ready")
        y_out_ready = sem("y_out_ready")
        out_sem = sem("out_sem")
        STARTS_AT_ONE = [s for l in (xt_done, xT_ready, gu_done, act_ready, tr_done, acT_ready, dn_done, y_ready)
                         for s in l]

        def rows(i):
            return P if i < 4 else NS

        def slot_banks(job):
            s = 2 * (INDEX[job] % 3)
            return ps[:, s:s + 2, :]

        def two_halves(job):
            return slot_banks(job)[:, :, 0:HALF]

        def halves(v):
            return v.rearrange("p (h n) -> p h n", h=2)

        def await_job(eng, job):
            eng.wait_ge(job_done, INDEX[job] + 1)

        def freed(job):
            return slot_free[INDEX[job] % 3]

        block = ctx.enter_context(nc.Block())

        @block.sync
        def _(sp):
            sp.dma_start(x_tok[0:NS, 4, :], t["x_sample"].rearrange("b o d -> (b o) d")).then_inc(x_in, 16)
            sp.dma_start(x_tok[:, 0:4, :], t["x_prompt"][0].rearrange("(i p) d -> p i d", p=P)).then_inc(x_in, 16)

            def load_tile(n):
                name, col = WTILES[n]
                s, before, _ = RING[n]
                if before is not None:
                    sp.wait_ge(w_used, before + 1)
                sp.dma_start(ring[s], t[name][0][:, col:col + 512].rearrange("(k p) n -> p k n", p=P))\
                  .then_inc(w_in_slot[s], 16)

            for n in range(MOD_TILES + 8):
                load_tile(n)

            def load_state(b):
                if b >= 2:
                    sp.wait_ge(st_out[b % 2], 16 * (b // 2))
                    sp.wait_ge(job_done, INDEX[("os", b - 2)] + 1)
                else:
                    sp.wait_ge(job_done, INDEX[("kt", 3)] + 1)
                    sp.wait_ge(kt_ready, 1)
                sp.dma_start(st[b % 2], t["state_gla"][0, b].rearrange("h k v -> k h v")).then_inc(st_in[b % 2], 16)

            load_tile(MOD_TILES + 8)
            load_state(0)
            load_state(1)
            for b in range(NS):
                sp.wait_ge(st_ready, b + 1)
                sp.dma_start(new_gla_s[0, b].rearrange("h k v -> k h v"), st[b % 2]).then_inc(st_out[b % 2], 16)
                if b + 2 < NS:
                    load_state(b + 2)
            sp.wait_ge(s_ready, NCH)
            sp.dma_start(new_gla_p[0, 0].rearrange("h k v -> k h v"), S[NCH % 2]).then_inc(s_out, 16)
            for n in range(MOD_TILES + 9, len(WTILES)):
                load_tile(n)
            sp.wait_ge(outs_ready, 1)
            sp.dma_start(new_conv_p[0, 0], outrow[0:3, 0, :]).then_inc(out_sem, 16)
            sp.dma_start(new_conv_s[0, :, 2, :], outrow[3:11, 0, :]).then_inc(out_sem, 16)
            sp.wait_ge(outs_ready, 2)
            sp.dma_start(new_rg_p[0], outrow[0:1, 1, :]).then_inc(out_sem, 16)
            sp.dma_start(new_rg_s[0], outrow[1:9, 1, :]).then_inc(out_sem, 16)
            for i in range(TILES):
                sp.wait_ge(hf_ready, i + 1)
                sp.dma_start(hf_dram[i * P:i * P + rows(i), :], hf[i % 2][0:rows(i), :]).then_inc(hf_out[i % 2], 16)
            sp.wait_ge(blocks_ready, 1)
            sp.wait_ge(started, 1)
            n = sp.value_load(blk_i[0:1, NBLK:NBLK + 1], min_val=0, max_val=NBLK)
            sp.wait_ge(out_sem, 16 * 4)
            with sp.Fori(0, NBLK // 2) as i:
                for j in range(2):
                    with sp.If(n > i * 2 + j):
                        e = sp.value_load(blk_i[0:1, bass.ds(i * 2 + j, 1)], min_val=0, max_val=NE - 1)
                        sp.wait_ge(gu_done[j], i + 1)
                        for s, w in ((0, "we_gate"), (1, "we_up")):
                            sp.dma_start(ring[3 * j + s], t[w][0, bass.ds(e, 1)].rearrange("o (p k) n -> p (o k) n", p=P))\
                              .then_inc(we_in[3 * j + s], 16)
                        sp.wait_ge(dn_done[j], i + 1)
                        if j == 1:
                            sp.wait_ge(addr_ready, 1)
                        sp.dma_start(ring[3 * j + 2].rearrange("p k n -> p (k n)"),
                                     t["we_down"][0, bass.ds(e, 1)].rearrange("o (p k) n -> p (o k n)", p=P))\
                          .then_inc(we_in[3 * j + 2], 16)
            sp.wait_ge(scattered, 1)
            for i in range(TILES):
                r = rows(i)
                sp.dma_start(yp[i][0:r], pair_dram[2 * P * i:2 * P * i + 2 * r, :].rearrange("(p k) d -> p k d", k=2))\
                  .then_inc(yp_in[i], 16)
            for v, name in enumerate(("ln2_g", "ln2_b")):
                sp.dma_start(ln2[:, v, :], t[name][0:1, :].to_broadcast([P, D])).then_inc(ln2_in, 16)
            for i in range(TILES):
                sp.wait_ge(y_out_ready, i + 1)
                r = rows(i)
                dst = y_prompt[0][i * P:i * P + r, :] if i < 4 else y_sample.rearrange("b o d -> (b o) d")
                sp.dma_start(dst, ft[i][0:r, :]).then_inc(out_sem, 16)
            sp.wait_ge(out_sem, 16 * (4 + TILES))
            sp.wait_ge(s_out, 16)
            for j in range(2):
                sp.wait_ge(st_out[j], 16 * (NS // 2))

        @block.gpsimd
        def _(pool):
            steps = [0]

            def link(ins):
                steps[0] += 1
                ins.then_inc(pool_step, 1)
                pool.wait_ge(pool_step, steps[0])

            link(pool.memset(packrows[0:ROWS, :], 0.0))
            pool.sem_inc(rows_clear, 1)
            link(pool.memset(ident[:], 0.0))
            link(pool.memset(ones[:], 1.0))
            link(pool.memset(maskT[:], 1.0))
            link(pool.affine_select(out=ident[:], in_=ident[:], compare_op=ALU.not_equal, fill=1.0, base=0,
                               pattern=[[-1, P]], channel_multiplier=1))
            link(pool.affine_select(out=upper[:], in_=ones[:], compare_op=ALU.is_ge, fill=0.0, base=-1,
                               pattern=[[1, P]], channel_multiplier=-1))
            link(pool.affine_select(out=sel8[0:9, :], in_=ones[0:9, :], compare_op=ALU.is_ge, fill=0.0, base=-8,
                               pattern=[[0, P]], channel_multiplier=1))
            for q in range(2):
                m = maskT[64 * q:64 * q + 64, :]
                link(pool.affine_select(out=m, in_=m, compare_op=ALU.is_ge, fill=0.0, base=0,
                                   pattern=[[1, CH]], channel_multiplier=-1))
            pool.sem_inc(consts, 1)
            pool.wait_ge(w_used, MOD_TILES)
            link(pool.memset(bd[0], 0.0))
            link(pool.memset(bd[1], 0.0))
            for g, name in enumerate(("rg_wa", "rg_wx")):
                w = t[name][0].rearrange("(c two) i j -> two i c j", two=2)
                for q in range(2):
                    pool.dma_start(bd[g][64 * q:64 * q + 64, :, 64 * q:64 * q + 64], w[q]).then_inc(bd_in, 16)
            pool.dma_start(wa2[0:RANK, :], t["gla_wa2"][0]).then_inc(bd_in, 16)
            link(pool.memset(scan_mask[:], 1.0))
            link(pool.memset(scan_mask[:, 0:T:CH], 0.0))
            link(pool.memset(scan_mask[:, T:NT], 0.0))
            pool.sem_inc(consts, 1)

            pool.wait_ge(o_done, NCH)
            pool.iota(oobt[0:CAP, :], pattern=[[0, TW * 2]], base=OOB, channel_multiplier=0).then_inc(oob_ready, 1)
            pool.wait_ge(oob_ready, 1)
            pool.dma_start(table_dram.rearrange("(p b) c -> p (b c)", p=CAP), oobt[0:CAP, :]).then_inc(table_clear, 16)
            pool.wait_ge(yb_ready, KD)
            ii = iota_i.bitcast(I32)
            link(pool.iota(ii[:, 0:NG], pattern=[[1, NG]], base=-99, channel_multiplier=0))
            link(pool.tensor_copy(j4[:], ii[:, 0:NG]))
            link(pool.iota(ii[:, 0:NE], pattern=[[1, NE]], base=-99, channel_multiplier=0))
            link(pool.tensor_copy(j32[:], ii[:, 0:NE]))
            link(pool.iota(ii[:, 0:SPLITS], pattern=[[CAP, SPLITS]], base=0, channel_multiplier=0))
            link(pool.tensor_copy(m64[:], ii[:, 0:SPLITS]))
            link(pool.iota(ii[:, 0:NBLK], pattern=[[1, NBLK]], base=0, channel_multiplier=0))
            link(pool.tensor_copy(blk_f[:], ii[:, 0:NBLK]))
            for k in range(2):
                link(pool.iota(payload[:, :, k, 0], pattern=[[P, TILES]], base=0, channel_multiplier=1))
                link(pool.iota(payload[:, :, k, 1], pattern=[[2 * P, TILES]], base=k, channel_multiplier=2))
            link(pool.memset(LG[:, 4, :], 0.0))
            pool.sem_inc(iotas, 1)
            for s in STARTS_AT_ONE:
                pool.sem_inc(s, 1)
            pool.sem_inc(started, 1)
            pool.wait_ge(addr_ready, 1)
            pool.wait_ge(table_clear, 16)
            for i in range(TILES):
                for k in range(2):
                    pool.indirect_dma_start(
                        table_dram, bass.IndirectOffsetOnAxis(ap=addr_i[0:rows(i), i, k:k + 1], axis=0),
                        payload[0:rows(i), i, k, :], None).then_inc(table_filled, 16)
            for j in range(2):
                link(pool.memset(xg[j][0:CAP, :], 0.0))
            pool.wait_ge(table_filled, 16 * 2 * TILES)
            tv = table_dram.rearrange("(p b) c -> p b c", p=CAP)
            for j in range(2):
                h = TW // 2
                pool.dma_start(idx[0:CAP, j * h:j * h + h, :], tv[:, j * h:j * h + h, :]).then_inc(moved[j], 16)
            pool.wait_ge(moved[0], 16)
            pool.wait_ge(moved[1], 16)
            for j in range(2):
                pool.wait_ge(hf_out[j], 16 * (3 - j))

            def gather(j):
                pool.sem_inc(pool_turns, 1)
                pool.indirect_dma_start(xg[j][0:CAP, :], None, hf_dram,
                                        bass.IndirectOffsetOnAxis(ap=gidx[j][0:CAP, 0:1], axis=0),
                                        bounds_check=NT - 1, oob_is_err=False).then_inc(xg_in[j], 16)

            for j in range(2):
                pool.tensor_copy(gidx[j][0:CAP, :], idx[0:CAP, j, 0:1]).then_inc(idx_copied, 1)
                pool.wait_ge(idx_copied, j + 1)
                gather(j)
            pool.wait_ge(blocks_ready, 1)
            n = pool.value_load(blk_i[0:1, NBLK:NBLK + 1], min_val=0, max_val=NBLK)
            with pool.Fori(0, NBLK // 2) as i:
                for j in range(2):
                    with pool.If(n > i * 2 + j):
                        pool.wait_ge(xt_done[j], i + 2)
                        pool.tensor_copy(gidx[j][0:CAP, :], idx[0:CAP, bass.ds(i * 2 + (j + 2), 1), 0:1]
                                         .rearrange("p o c -> p (o c)")).then_inc(idx_copied, 1)
                        pool.wait_ge(idx_copied, i * 4 + (2 * j + 3))
                        gather(j)
                        pool.wait_ge(moved[j], i * 16 + 16)
                        pool.tensor_copy(sidx[j][0:CAP, :], idx[0:CAP, bass.ds(i * 2 + j, 1), 1:2]
                                         .rearrange("p o c -> p (o c)")).then_inc(idx_copied, 1)
                        pool.wait_ge(idx_copied, i * 4 + (2 * j + 4))
                        pool.wait_ge(y_ready[j], i * 2 + 3)
                        pool.sem_inc(pool_turns, 1)
                        pool.indirect_dma_start(
                            pair_dram, bass.IndirectOffsetOnAxis(ap=sidx[j][0:CAP, 0:1], axis=0),
                            yb[j][0:CAP, :], None, bounds_check=PAIRS - 1, oob_is_err=False).then_inc(moved[j], 16)
            with pool.Fori(0, NBLK // 2) as i:
                for j in range(2):
                    with pool.If(n > i * 2 + j):
                        pool.wait_ge(moved[j], i * 16 + 32)
                        pool.sem_inc(pool_turns, 1)
            pool.sem_inc(scattered, 1)

        @block.scalar
        def _(sc):
            steps = [0]

            def link(ins):
                steps[0] += 1
                ins.then_inc(act_step, 1)
                sc.wait_ge(act_step, steps[0])

            b_in = t["b_in"]
            sc.wait_ge(rows_clear, 1)
            packs = [(R_C, 8, t["c_sample"]), (R_C + 8, 1, t["c_prompt"]),
                     (R_CONVST, 24, t["state_conv"][0].rearrange("b w d -> (b w) d")),
                     (R_H0, 8, t["state_rglru"][0]), (R_CONVW, CONV, t["conv_w"][0]), (R_CONVB, 1, t["conv_b"]),
                     (R_BA, 1, t["rg_ba"]), (R_BX, 1, t["rg_bx"]), (R_LAM, 1, t["rg_lambda"]),
                     (R_BIN, 5, b_in[:, 0:5120].rearrange("o (r d) -> (o r) d", d=D)),
                     (R_BIN + 5, 2, b_in[:, 5136:7184].rearrange("o (r d) -> (o r) d", d=D))]
            for r, m, src in packs:
                sc.dma_start(packrows[r:r + m, :], src).then_inc(pack_in, 16)
            for c0, m, src in ((0, 512, t["gla_ba"]), (512, 256, t["gla_norm_g"]), (768, RANK, b_in[:, 5120:5136])):
                sc.dma_start(packrows[R_MISC:R_MISC + 1, c0:c0 + m], src).then_inc(pack_in, 16)
            sc.dma_start(mod_sb[0:9, :], t["b_mod"][0:1, :].to_broadcast([9, 6 * D])).then_inc(bmod_in, 16)
            sc.dma_start(alpha_w[:], t["w_in"][0][:, 5120:5136].rearrange("(k p) n -> p k n", p=P)).then_inc(small_in, 16)
            sc.dma_start(route_w[:, :, 0:NG], t["w_grp"][0].rearrange("(k p) n -> p k n", p=P)).then_inc(small_in, 16)
            sc.dma_start(route_w[:, :, NG:NG + NE], t["w_exp"][0].rearrange("(k p) n -> p k n", p=P)).then_inc(small_in, 16)
            sc.dma_start(route_b[:, 0:NG], t["b_grp"][0:1, :].to_broadcast([P, NG])).then_inc(small_in, 16)
            sc.dma_start(route_b[:, NG:NG + NE], t["b_exp"][0:1, :].to_broadcast([P, NE])).then_inc(small_in, 16)
            sc.dma_start(new_conv_s[0, :, 0:2, :], t["state_conv"][0][:, 1:3, :]).then_inc(s_out, 16)

            await_job(sc, ("pack", 0))
            link(sc.activation(fp[:], slot_banks(("pack", 0))[:, 0, :].rearrange("p (k r) -> p k r", r=64)[:, :, 0:ROWS],
                               ACT.Copy))
            sc.sem_inc(slot_free[0], 1)
            sc.activation(cs[:], fp[:, :, R_C:R_C + 9], ACT.Silu).then_inc(cs_ready, 1)
            for i in range(TILES + 1):
                if i < TILES:
                    sc.wait_ge(rstd_q, i + 1)
                    sc.activation(mv[0:rows(i), 2:3], mv[0:rows(i), 1:2], ACT.Sqrt).then_inc(rstd_a, 1)
                if i >= 1:
                    k = i - 1
                    await_job(sc, ("xt", k))
                    v = slot_banks(("xt", k)).rearrange("p h (k n) -> p (h k) n", k=4)[:, :, 0:rows(k)]
                    ins = sc.activation(hT[:, :, k * P:k * P + rows(k)], v, ACT.Copy)
                    ins.then_inc(freed(("xt", k)), 1)
            sc.wait_ge(lam_q, 1)
            link(sc.activation(lam[:, 2, :], lam[:, 1, :], ACT.Exp))
            sc.activation(lam[:, 3, :], lam[:, 2, :], ACT.Ln, bias=1.0).then_inc(lam_a, 1)
            sc.wait_ge(modT_ready, 1)
            sc.wait_ge(slot_free[INDEX[("xt", 4)] % 3], INDEX[("xt", 4)] // 3 + 1)
            for k in range(KD):
                sc.activation(hT[:, k, 0:T], hT[:, k, 0:T], ACT.Identity, bias=modT[:, k, 8:9],
                              scale=modT[:, 8 + k, 8:9]).then_inc(hT_act, 1)

            def evacuate(job, out, func, bias, ready, half_view=True):
                await_job(sc, job)
                src = two_halves(job)
                sc.activation(halves(out), src, func, bias=bias).then_inc(freed(job), 1)
                return ready

            def sqrt_step(c):
                sc.wait_ge(th_ready, c + 1)
                sc.activation(rg["sq"][c % 2], rg["th"][c % 2], ACT.Sqrt).then_inc(sqrt_ready, 1)

            for g in range(2):
                for c in range(4 * g, 4 * g + 4):
                    await_job(sc, ("rx", c))
                    link(sc.activation(halves(A[:, c, :]), two_halves(("rx", c)), ACT.Identity,
                                       bias=fp[:, c, R_BIN:R_BIN + 1]))
                    sc.sem_inc(freed(("rx", c)), 1)
                    sc.sem_inc(rx_ready, 1)
                    if c == 4:
                        sqrt_step(3)
                for c in range(4 * g, 4 * g + 4):
                    await_job(sc, ("ry", c))
                    link(sc.activation(halves(O[:, c, :]), two_halves(("ry", c)), ACT.Gelu_apprx_tanh,
                                       bias=fp[:, c, R_BIN + 1:R_BIN + 2]))
                    sc.sem_inc(freed(("ry", c)), 1)
                    sc.sem_inc(ry_ready, 1)
                    if c > 4 * g:
                        sqrt_step(c - 1)
                    if c == 0:
                        sc.wait_ge(lam_ready, 1)
                    if c >= 2:
                        sc.wait_ge(ya_ready, c - 1)
                    for name, job, row in (("r", "ra", R_BA), ("i", "ri", R_BX)):
                        await_job(sc, (job, c))
                        link(sc.activation(halves(rg[name][c % 2]), two_halves((job, c)), ACT.Sigmoid,
                                           bias=fp[:, c, row:row + 1]))
                        sc.sem_inc(freed((job, c)), 1)
                    sc.activation(rg["a"][c % 2], rg["r"][c % 2], ACT.Exp, scale=lam[:, 5, c:c + 1]).then_inc(gates_ready, 1)
                    sc.activation(rg["th"][c % 2], rg["r"][c % 2], ACT.Tanh, scale=lam[:, 4, c:c + 1]).then_inc(gates_ready, 1)
            sqrt_step(7)

            for c in range(8):
                await_job(sc, ("qk", c))
                sc.activation(halves(Q[:, c, :]), two_halves(("qk", c)), ACT.Identity,
                              bias=fp[:, c, R_BIN + 2:R_BIN + 3]).then_inc(freed(("qk", c)), 1)
            await_job(sc, ("al", 0))
            link(sc.activation(halves(al[0:RANK, :]), two_halves(("al", 0))[0:RANK], ACT.Identity,
                               bias=fp[0:RANK, 6, R_MISC:R_MISC + 1]))
            sc.sem_inc(freed(("al", 0)), 1)
            sc.sem_inc(al_ready, 1)
            sc.wait_ge(ya_ready, KD)
            for c in range(HEADS):
                await_job(sc, ("la", c))
                sc.activation(halves(L[:, c, :]), two_halves(("la", c)), ACT.Identity,
                              bias=fp[:, c, R_MISC:R_MISC + 1]).then_inc(freed(("la", c)), 1)
            sc.wait_ge(nabs_ready, 1)
            link(sc.activation(EX[:], EX[:], ACT.Exp))
            sc.activation(EX[:], EX[:], ACT.Ln, bias=1.0).then_inc(log_ready, 1)
            sc.wait_ge(bcum_ready, 1)
            sc.activation(L[:], EX[:], ACT.Exp, scale=1.0 / TAU).then_inc(e1_ready, 1)
            sc.activation(K2[:], EX[:], ACT.Exp, scale=-1.0 / TAU).then_inc(e1_ready, 1)
            sc.wait_ge(dexp_q, 1)
            sc.activation(EX[:, :, 0:T], EX[:, :, 0:T], ACT.Exp, scale=1.0 / TAU).then_inc(e2_ready, 1)

            sc.wait_ge(gla_in_ready, 1)
            for c in range(8):
                await_job(sc, ("v", c))
                if c >= 2:
                    await_job(sc, ("vt", c - 2))
                link(sc.activation(halves(vf[c % 2]), two_halves(("v", c)), ACT.Identity,
                                   bias=fp[:, c, R_BIN + 3:R_BIN + 4]))
                sc.sem_inc(freed(("v", c)), 1)
                sc.sem_inc(vf_ready, 1)
            for i in range(4):
                await_job(sc, ("kt", i))
                ins = sc.activation(kout_tok[:, i, :], slot_banks(("kt", i))[:, 0, :], ACT.Copy)
                ins.then_inc(freed(("kt", i)), 1)
            sc.sem_inc(kt_ready, 1)
            for n in range(NCH):
                await_job(sc, ("os", n))
                sc.activation(O[:, :, T + n:T + n + 1], slot_banks(("os", n))[:, 0, 0:8].unsqueeze(2), ACT.Copy)\
                  .then_inc(freed(("os", n)), 1)
                sc.wait_ge(o_done, n + 1)
                sc.activation(O[:, :, n * CH:(n + 1) * CH], ps[:, 7, :].rearrange("p (a b) -> p a b", b=CH), ACT.Copy)\
                  .then_inc(o_copied, 1)
            def square(h):
                if h >= 2:
                    await_job(sc, ("ss", h - 2))
                sc.activation(sq[h % 2], O[:, 2 * h:2 * h + 2, :], ACT.Square).then_inc(sq_ready, 1)

            def root(h):
                sc.wait_ge(var_ready, h + 1)
                sc.activation(rms[h % 2], rms[h % 2], ACT.Sqrt).then_inc(rms_ready, 1)

            def gate(c):
                await_job(sc, ("gg", c))
                if c >= 2:
                    sc.wait_ge(yb_ready, c - 1)
                link(sc.activation(halves(gt[c % 2]), two_halves(("gg", c)), ACT.Silu,
                                   bias=fp[:, c, R_BIN + 4:R_BIN + 5]))
                sc.sem_inc(freed(("gg", c)), 1)
                sc.sem_inc(gt_ready, 1)

            sc.wait_ge(o_copied, NCH)
            sc.wait_ge(freed(("os", 7)), INDEX[("os", 7)] // 3 + 1)
            for j in range(2):
                sc.wait_ge(st_out[j], 16 * (NS // 2))
            square(0)
            square(1)
            root(0)
            gate(0)
            square(2)
            root(1)
            gate(1)
            square(3)
            root(2)
            gate(2)
            root(3)
            for c in range(3, 8):
                gate(c)
            sc.wait_ge(yb_ready, KD)
            sc.wait_ge(s_out, 32)
            for job, dst, row in (("ga", Z, 5), ("gb", Q, 6)):
                for c in range(KD):
                    await_job(sc, (job, c))
                    link(sc.activation(halves(dst[:, c, :]), two_halves((job, c)), ACT.Sigmoid,
                                       bias=fp[:, c, R_BIN + row:R_BIN + row + 1]))
                    sc.sem_inc(freed((job, c)), 1)
                    sc.sem_inc(sig_ready, 1)
            for k, (job, m) in enumerate((("rlT", 11), ("hlT", 9))):
                await_job(sc, (job, 0))
                if k == 0:
                    sc.wait_ge(table_clear, 16)
                link(sc.activation(outrow[0:m, k, :].rearrange("p (h n) -> p h n", h=2), slot_banks((job, 0))[0:m], ACT.Copy))
                sc.sem_inc(freed((job, 0)), 1)
                sc.sem_inc(outs_ready, 1)
            sc.wait_ge(z_ready, KD)
            for v, name in enumerate(("ln1_g", "ln1_b")):
                sc.dma_start(lnp[:, v, :], t[name][0:1, :].to_broadcast([P, D])).then_inc(lnp_in, 16)
            for i in range(TILES):
                for k in range(2):
                    sc.wait_ge(rstd_q, TILES + 2 * i + k + 1)
                    sc.activation(mv[0:rows(i), 2:3], mv[0:rows(i), 1:2], ACT.Sqrt).then_inc(rstd_a, 1)
                await_job(sc, ("ht", i))
                if i >= 2:
                    await_job(sc, ("lg", i - 2))
                v = slot_banks(("ht", i)).rearrange("p h (k n) -> p (h k) n", k=4)[:, :, 0:rows(i)]
                link(sc.activation(hfT[i % 2][:, :, 0:rows(i)], v, ACT.Copy))
                sc.sem_inc(freed(("ht", i)), 1)
                sc.sem_inc(hfT_ready, 1)
            sc.wait_ge(ge_q, 1)
            sc.activation(g_e[:], g_e[:], ACT.Exp).then_inc(ge_a, 1)
            sc.wait_ge(ge_q, 2)
            sc.activation(g_m[:, 6, :], g_m[:, 5, :], ACT.Exp).then_inc(ge_a, 1)

            sc.wait_ge(blocks_ready, 1)
            sc.wait_ge(started, 1)
            sc.wait_ge(xt_done[0], 2)
            sc.activation(xT[0], ps[:, 0, :].rearrange("p (k n) -> p k n", k=KD), ACT.Copy).then_inc(xT_ready[0], 1)
            n = sc.value_load(blk_i[0:1, NBLK:NBLK + 1], min_val=0, max_val=NBLK)
            with sc.Fori(0, NBLK // 2) as i:
                for j in range(2):
                    with sc.If(n > i * 2 + j):
                        sc.wait_ge(gu_done[j], i + 2)
                        sc.wait_ge(act_ready[j], i + 1)
                        sc.activation(sg[j][CAP:2 * CAP, :], ps[0:CAP, 2 + j, :], ACT.Silu).then_inc(sg_ready[j], 1)
                        sc.wait_ge(xt_done[1 - j], i + (2 + j))
                        sc.wait_ge(gu_done[1 - j], i + (1 + j))
                        sc.activation(xT[1 - j], ps[:, 1 - j, :].rearrange("p (k n) -> p k n", k=KD), ACT.Copy)\
                          .then_inc(xT_ready[1 - j], 1)
                        sc.wait_ge(tr_done[j], i + 2)
                        sc.wait_ge(dn_done[j], i + 1)
                        sc.activation(acT[j], ps[:, 6 + j, 0:4 * CAP].rearrange("p (k n) -> p k n", k=4), ACT.Copy)\
                          .then_inc(acT_ready[j], 1)
                        sc.wait_ge(dn_done[j], i + 2)
                        sc.wait_ge(moved[j], i * 16 + 16)
                        sc.activation(yb[j][0:CAP, 512:1024], ps[CAP:2 * CAP, 4 + j, :], ACT.Copy).then_inc(y_ready[j], 1)
            for i in range(TILES):
                r = rows(i)
                sc.wait_ge(yp_in[i], 16)
                sc.activation(yp[i][0:r, 0, :], yp[i][0:r, 0, :], ACT.Copy, scale=wpair[0:r, i, 0:1]).then_inc(yw_ready, 1)
            for i in range(TILES):
                r = rows(i)
                sc.wait_ge(fin_q, i + 1)
                sc.activation(mv[0:r, 2:3], mv[0:r, 1:2], ACT.Sqrt).then_inc(fin_a, 1)

        @block.vector
        def _(v):
            steps = [0]

            def link(ins):
                steps[0] += 1
                ins.then_inc(dve_step, 1)
                v.wait_ge(dve_step, steps[0])

            roots = [0]

            def layer_stats(x, r, ask, answer):
                link(v.bn_stats(stats[0:r, 0, :], x[:, 0:512]))
                link(v.bn_stats(stats[0:r, 1, :], x[:, 512:1024]))
                link(v.bn_aggr(mv[0:r, 0:2], stats[0:r].rearrange("p a b -> p (a b)")))
                v.tensor_scalar_add(mv[0:r, 1:2], mv[0:r, 1:2], LN_EPS).then_inc(ask, 1)
                roots[0] += 1
                v.wait_ge(answer, roots[0])
                link(v.reciprocal(mv[0:r, 3:4], mv[0:r, 2:3]))

            def normalise(out, x, r):
                return v.tensor_scalar(out, x, mv[0:r, 0:1], mv[0:r, 3:4], ALU.subtract, ALU.mult)

            v.wait_ge(x_in, 32)
            for i in range(TILES):
                r = rows(i)
                layer_stats(x_tok[0:r, i, :], r, rstd_q, rstd_a)
                if i >= 2:
                    await_job(v, ("xt", i - 2))
                link(normalise(xn[i % 2][0:r, :], x_tok[0:r, i, :], r))
                v.sem_inc(xn_ready, 1)
            v.wait_ge(cs_ready, 1)
            lm = fp[:, :, R_LAM]
            link(v.tensor_scalar(lam[:, 0, :], lm, -1.0, 0.0, ALU.mult, ALU.max))
            v.scalar_tensor_tensor(lam[:, 1, :], lm, -1.0, lm, ALU.mult, ALU.min).then_inc(lam_q, 1)
            v.wait_ge(lam_a, 1)
            link(v.tensor_tensor(lam[:, 3, :], lam[:, 3, :], lam[:, 0, :], ALU.add))
            link(v.tensor_scalar_mul(lam[:, 4, :], lam[:, 3, :], 8.0))
            v.tensor_scalar_mul(lam[:, 5, :], lam[:, 3, :], -8.0).then_inc(lam_ready, 1)

            def add_mod(m):
                await_job(v, ("mod", m))
                cols = mod_sb[0:9, m * 512:(m + 1) * 512]
                link(v.tensor_tensor(cols, cols, slot_banks(("mod", m))[0:9, 0, :], ALU.add))
                v.sem_inc(freed(("mod", m)), 1)

            v.wait_ge(bmod_in, 16)
            for m in range(6):
                add_mod(m)
            await_job(v, ("modT", 0))
            mt = slot_banks(("modT", 0))[:, 0, 0:144].rearrange("p (a b) -> p a b", b=9)
            link(v.tensor_copy(modT[:, 0:8, :], mt[:, 0:8, :]))
            link(v.tensor_scalar_add(modT[:, 8:16, :], mt[:, 8:16, :], 1.0))
            v.sem_inc(freed(("modT", 0)), 1)
            v.sem_inc(modT_ready, 1)
            v.wait_ge(slot_free[INDEX[("xt", 4)] % 3], INDEX[("xt", 4)] // 3 + 1)
            hs = hT[:, :, T:NT]
            link(v.tensor_tensor(hs, hs, modT[:, 8:16, 0:8], ALU.mult))
            v.tensor_tensor(hs, hs, modT[:, 0:8, 0:8], ALU.add).then_inc(hT_dve, 1)
            for m in range(6, 12):
                add_mod(m)

            def conv(c):
                v.wait_ge(rx_ready, c + 1)
                if c >= 2:
                    await_job(v, ("ri", c - 2))
                if c == 0:
                    await_job(v, ("mod", 11))
                xc = rg["xc"][c % 2]
                w = [fp[:, c, R_CONVW + k:R_CONVW + k + 1] for k in range(CONV)]
                link(v.tensor_copy(rl[:, c, :], A[:, c, 509:520]))
                link(v.tensor_scalar(xc[:], A[:, c, :], w[3], fp[:, c, R_CONVB:R_CONVB + 1], ALU.mult, ALU.add))
                for k in range(1, CONV):
                    link(v.scalar_tensor_tensor(xc[:, k:T], A[:, c, 0:T - k], w[3 - k], xc[:, k:T], ALU.mult, ALU.add))
                for k in range(3):
                    s = fp[:, c, R_CONVST + k:R_CONVST + 24:3]
                    link(v.scalar_tensor_tensor(xc[:, T:NT], s, w[k], xc[:, T:NT], ALU.mult, ALU.add))
                v.sem_inc(xc_ready, 1)

            def recur(c):
                j = c % 2
                a, th, u, h = rg["a"][j], rg["th"][j], rg["i"][j], rg["r"][j]
                v.wait_ge(gates_ready, 2 * c + 2)
                link(v.tensor_tensor(u[:], u[:], rg["xc"][j][:], ALU.mult))
                link(v.tensor_tensor(rg["sq"][j][:], a[:], a[:], ALU.mult))
                link(v.scalar_tensor_tensor(th[:], rg["sq"][j][:], 1.0, th[:], ALU.add, ALU.mult))
                v.sem_inc(th_ready, 1)
                v.wait_ge(sqrt_ready, c + 1)
                link(v.tensor_tensor(u[:], u[:], rg["sq"][j][:], ALU.mult))
                link(v.tensor_tensor(tmp8[:, 0, :], a[:, T:NT], fp[:, c, R_H0:R_H0 + 8], ALU.mult))
                link(v.tensor_tensor_scan(h[:, 0:T], a[:, 0:T], u[:, 0:T], 0.0, ALU.mult, ALU.add))
                link(v.tensor_tensor(h[:, T:NT], u[:, T:NT], tmp8[:, 0, :], ALU.add))
                link(v.tensor_copy(hl[:, c, :], h[:, T - 1:NT]))
                v.wait_ge(ry_ready, c + 1)
                link(v.tensor_tensor(A[:, c, :], h[:], O[:, c, :], ALU.mult))
                v.sem_inc(ya_ready, 1)

            for c in range(KD):
                conv(c)
                if c:
                    recur(c - 1)
            recur(KD - 1)

            v.wait_ge(freed(("la", 3)), INDEX[("la", 3)] // 3 + 1)
            v.wait_ge(freed(("la", 2)), INDEX[("la", 2)] // 3 + 1)
            v.wait_ge(freed(("la", 1)), INDEX[("la", 1)] // 3 + 1)
            link(v.scalar_tensor_tensor(EX[:], L[:], -1.0, L[:], ALU.mult, ALU.min))
            v.sem_inc(nabs_ready, 1)
            v.wait_ge(log_ready, 1)
            link(v.scalar_tensor_tensor(L[:], L[:], 0.0, EX[:], ALU.min, ALU.subtract))
            v.wait_ge(consts, 2)
            for h in range(HEADS):
                link(v.tensor_tensor_scan(EX[:, h, :], scan_mask[:], L[:, h, :], 0.0, ALU.mult, ALU.add))
            v.sem_inc(bcum_ready, 1)
            v.tensor_copy(bt[:], EX[:, :, CH - 1:T:CH])
            v.wait_ge(e1_ready, 2)
            link(v.tensor_copy(ela[:], L[:, :, T:NT]))
            link(v.tensor_copy(dec[:], L[:, :, CH - 1:T:CH]))
            for h in range(HEADS):
                e = EX[:, h, 0:T].rearrange("p (n c) -> p n c", c=CH)
                link(v.tensor_tensor(e, bt[:, h, :].unsqueeze(2).to_broadcast([P, NCH, CH]), e, ALU.subtract))
            v.sem_inc(dexp_q, 1)
            link(v.tensor_scalar_mul(qs[:], Q[:, 0:HEADS, T:NT], DKH ** -0.5))
            link(v.scalar_tensor_tensor(Q[:, 0:HEADS, 0:T], Q[:, 0:HEADS, 0:T], DKH ** -0.5, L[:, :, 0:T],
                                        ALU.mult, ALU.mult))
            v.wait_ge(e2_ready, 1)
            link(v.tensor_tensor(EX[:, :, 0:T], EX[:, :, 0:T], Q[:, HEADS:8, 0:T], ALU.mult))
            link(v.tensor_tensor(Q[:, HEADS:8, 0:T], Q[:, HEADS:8, 0:T], K2[:, :, 0:T], ALU.mult))
            v.sem_inc(gla_in_ready, 1)
            for c in range(8):
                await_job(v, ("vt", c))
                b = slot_banks(("vt", c))
                link(v.tensor_copy(v_tok[:, :, c * P:(c + 1) * P], b[:, 0, :].rearrange("p (i n) -> p i n", i=4)))
                link(v.tensor_copy(v_samp[0:NS, c * P:(c + 1) * P], b[0:NS, 1, 0:P]))
                v.sem_inc(freed(("vt", c)), 1)
                v.sem_inc(vt_ready, 1)
            for n in range(NCH):
                q = 64 * (n % 2)
                v.wait_ge(at_done, n + 1)
                if n >= 2:
                    v.wait_ge(o_done, n - 1)
                if n == 0:
                    v.wait_ge(kt_ready, 1)
                link(v.tensor_tensor(attm[n % 2][q:q + 64], ps[q:q + 64, 6, 0:256].rearrange("p (h i) -> p h i", h=HEADS),
                                     maskT[q:q + 64, :].unsqueeze(1).to_broadcast([64, HEADS, CH]), ALU.mult))
                v.sem_inc(attm_ready, 1)
                await_job(v, ("ds", n))
                if n >= 1:
                    v.wait_ge(o_done, n)
                ds = slot_banks(("ds", n)).rearrange("p b (h w) -> p (b h) w", w=DVH)
                new = S[(n + 1) % 2]
                for h in range(HEADS):
                    if n == 0:
                        link(v.tensor_copy(new[:, h, :], ds[:, h, :]))
                    else:
                        link(v.scalar_tensor_tensor(new[:, h, :], S[n % 2][:, h, :], dec[:, h, n:n + 1], ds[:, h, :],
                                                    ALU.mult, ALU.add))
                v.sem_inc(freed(("ds", n)), 1)
                v.sem_inc(s_ready, 1)
                v.wait_ge(st_in[n % 2], 16 * (n // 2 + 1))
                for h in range(HEADS):
                    link(v.tensor_scalar_mul(st[n % 2][:, h, :], st[n % 2][:, h, :], ela[:, h, n:n + 1]))
                await_job(v, ("vb", n))
                vb = slot_banks(("vb", n)).rearrange("p b (h w) -> p (b h) w", w=DVH)
                for h in range(HEADS):
                    link(v.scalar_tensor_tensor(st[n % 2][:, h, :], vb[:, h, :], Q[:, HEADS + h, T + n:T + n + 1],
                                                st[n % 2][:, h, :], ALU.mult, ALU.add))
                v.sem_inc(freed(("vb", n)), 1)
                v.sem_inc(st_ready, 1)

            def variance(h):
                await_job(v, ("ss", h))
                link(v.tensor_scalar(halves(rms[h % 2]), two_halves(("ss", h)), 1.0 / DVH, RMS_EPS, ALU.mult, ALU.add))
                v.sem_inc(freed(("ss", h)), 1)
                v.sem_inc(var_ready, 1)

            def rescale(h):
                v.wait_ge(rms_ready, h + 1)
                link(v.reciprocal(rms[h % 2][:], rms[h % 2][:]))
                for d in range(2):
                    link(v.scalar_tensor_tensor(O[:, 2 * h + d, :], O[:, 2 * h + d, :], fp[:, 4 + d, R_MISC:R_MISC + 1],
                                                rms[h % 2][:], ALU.mult, ALU.mult))

            def gate(c):
                v.wait_ge(gt_ready, c + 1)
                link(v.tensor_tensor(O[:, c, :], O[:, c, :], gt[c % 2][:], ALU.mult))
                v.sem_inc(yb_ready, 1)

            variance(0)
            variance(1)
            rescale(0)
            gate(0)
            variance(2)
            rescale(1)
            gate(1)
            variance(3)
            rescale(2)
            gate(2)
            rescale(3)
            for c in range(3, 8):
                gate(c)
            for c in range(KD):
                v.wait_ge(sig_ready, c + 1)
                await_job(v, ("pa", c))
                link(v.tensor_tensor(halves(Z[:, c, :]), halves(Z[:, c, :]), two_halves(("pa", c)), ALU.mult))
                v.sem_inc(freed(("pa", c)), 1)
            for c in range(KD):
                v.wait_ge(sig_ready, KD + c + 1)
                await_job(v, ("pb", c))
                link(v.tensor_tensor(halves(Q[:, c, :]), halves(Q[:, c, :]), two_halves(("pb", c)), ALU.mult))
                v.sem_inc(freed(("pb", c)), 1)
                link(v.tensor_tensor(Z[:, c, :], Z[:, c, :], Q[:, c, :], ALU.add))
                v.sem_inc(z_ready, 1)
            for k in range(4):
                await_job(v, ("bc", k))
                out = bc[:, k, :].rearrange("p (h n) -> p h n", h=2)
                link(v.tensor_scalar_add(out, slot_banks(("bc", k)), 1.0 if k == 2 else 0.0))
                v.sem_inc(freed(("bc", k)), 1)
            link(v.tensor_scalar_add(mod_sb[0:NS, 4 * D:5 * D], mod_sb[0:NS, 4 * D:5 * D], 1.0))

            def modvec(k, i):
                return bc[:, k, :] if i < 4 else mod_sb[0:NS, (2 + k) * D:(3 + k) * D]

            def add_route_bias(i):
                r = rows(i)
                await_job(v, ("lg", i))
                if i == 4:
                    v.wait_ge(iotas, 1)
                link(v.tensor_tensor(LG[0:r, i, :], slot_banks(("lg", i))[0:r, 0, 0:NG + NE], route_b[0:r, :], ALU.add))
                v.sem_inc(freed(("lg", i)), 1)

            v.wait_ge(lnp_in, 32)
            for i in range(TILES):
                r = rows(i)
                await_job(v, ("wo", i))
                u = lt[0][0:r, :]
                uh = u.rearrange("p (h n) -> p h n", h=2)
                x = x_tok[0:r, i, :]
                link(v.tensor_tensor(uh, slot_banks(("wo", i))[0:r], modvec(0, i).rearrange("p (h n) -> p h n", h=2), ALU.mult))
                v.sem_inc(freed(("wo", i)), 1)
                link(v.scalar_tensor_tensor(u, x, ALPHA, u, ALU.mult, ALU.add))
                layer_stats(u, r, rstd_q, rstd_a)
                link(normalise(u, u, r))
                link(v.tensor_tensor(u, u, lnp[0:r, 0, :], ALU.mult))
                link(v.tensor_tensor(x, u, lnp[0:r, 1, :], ALU.add))
                layer_stats(x, r, rstd_q, rstd_a)
                if i >= 2:
                    v.wait_ge(hf_out[i % 2], 16 * (i // 2))
                    await_job(v, ("ht", i - 2))
                h = hf[i % 2][0:r, :]
                link(normalise(h, x, r))
                link(v.tensor_tensor(h, h, modvec(2, i), ALU.mult))
                link(v.tensor_tensor(h, h, modvec(1, i), ALU.add))
                v.sem_inc(hf_ready, 1)
                if i >= 1:
                    add_route_bias(i - 1)
            add_route_bias(4)

            v.wait_ge(iotas, 1)
            GL = LG[:, :, 0:NG]
            EL = LG[:, :, NG:NG + NE].rearrange("p t (g e) -> p t g e", g=NG)
            bro = lambda a, n: a.unsqueeze(2).to_broadcast([P, TILES, n])
            j4b = j4.unsqueeze(1).to_broadcast([P, TILES, NG])
            j32b = j32.unsqueeze(1).to_broadcast([P, TILES, NE])

            def first_of(eq, jb, low, oh, n):
                link(v.tensor_tensor(eq, eq, jb, ALU.mult))
                link(v.tensor_reduce(low, eq, AX, ALU.min))
                link(v.tensor_tensor(oh, jb, bro(low, n), ALU.is_equal))

            link(v.tensor_reduce(g_m[:, 0, :], GL, AX, ALU.max))
            link(v.tensor_tensor(g_e[:], GL, bro(g_m[:, 0, :], NG), ALU.subtract))
            v.sem_inc(ge_q, 1)
            link(v.tensor_tensor(g_eq[:], GL, bro(g_m[:, 0, :], NG), ALU.is_equal))
            link(v.tensor_tensor(g_eq[:], g_eq[:], j4b, ALU.mult))
            link(v.tensor_reduce(g_m[:, 1, :], g_eq[:], AX, ALU.min))
            link(v.tensor_tensor(g_eq[:], j4b, bro(g_m[:, 1, :], NG), ALU.is_equal))
            v.wait_ge(ge_a, 1)
            link(v.tensor_reduce(g_m[:, 2, :], g_e[:], AX, ALU.add))
            link(v.reciprocal(g_m[:, 2, :], g_m[:, 2, :]))
            mlg = ml.rearrange("p t (g e) -> p t g e", g=NG)
            for i in range(TILES):
                gb = g_eq[:, i, :].unsqueeze(2).to_broadcast([P, NG, EPG])
                link(v.tensor_tensor(mlg[:, i], EL[:, i], gb, ALU.mult))
                link(v.tensor_scalar(e_eq[:, i, :].rearrange("p (g e) -> p g e", g=NG), gb, -1.0, BIG, ALU.add, ALU.mult))
            link(v.tensor_tensor(ml[:], ml[:], e_eq[:], ALU.add))
            for k in range(2):
                link(v.tensor_reduce(g_m[:, 3 + k, :], ml[:], AX, ALU.max))
                link(v.tensor_tensor(e_eq[:], ml[:], bro(g_m[:, 3 + k, :], NE), ALU.is_equal))
                first_of(e_eq[:], j32b, g_m[:, 7, :], OH[:, :, k, :], NE)
                if k == 0:
                    link(v.scalar_tensor_tensor(ml[:], OH[:, :, 0, :], -3.0 * BIG, ml[:], ALU.mult, ALU.add))
            link(v.tensor_tensor(g_m[:, 5, :], g_m[:, 4, :], g_m[:, 3, :], ALU.subtract))
            v.sem_inc(ge_q, 1)
            link(v.tensor_tensor(M[:], OH[:, :, 0, :], OH[:, :, 1, :], ALU.add))
            v.sem_inc(m_ready, 1)
            v.wait_ge(ge_a, 2)
            link(v.tensor_scalar_add(g_m[:, 8, :], g_m[:, 6, :], 1.0))
            link(v.reciprocal(g_m[:, 8, :], g_m[:, 8, :]))
            link(v.tensor_tensor(wpair[:, :, 0], g_m[:, 8, :], g_m[:, 2, :], ALU.mult))
            link(v.tensor_tensor(wpair[:, :, 1], wpair[:, :, 0], g_m[:, 6, :], ALU.mult))
            await_job(v, ("rk", 0))
            rk = slot_banks(("rk", 0))[:, 0, 0:(TILES + 1) * NE].rearrange("p (t e) -> p t e", e=NE)
            link(v.tensor_copy(rank[:], rk[:, 0:TILES, :]))
            cb = rk[:, TILES, :].unsqueeze(2).to_broadcast([P, NE, SPLITS])
            link(v.tensor_tensor(many[:], cb, m64.unsqueeze(1).to_broadcast([P, NE, SPLITS]), ALU.is_gt))
            link(v.tensor_reduce(cnt[:, 0, :], many[:], AX, ALU.add))
            link(v.tensor_tensor_scan(cnt[:, 1, :], ones[:, 0:NE], cnt[:, 0, :], 0.0, ALU.mult, ALU.add))
            link(v.tensor_tensor(cnt[:, 2, :], cnt[:, 1, :], cnt[:, 0, :], ALU.subtract))
            big = area(B, NBLK, NE)
            link(v.tensor_tensor(big[0:1], cnt[0:1, 1, :].unsqueeze(1).to_broadcast([1, NBLK, NE]),
                                 blk_f[0:1, :].unsqueeze(2).to_broadcast([1, NBLK, NE]), ALU.is_le))
            link(v.tensor_reduce(blk_f[0:1, :], big[0:1], AX, ALU.add))
            link(v.tensor_scalar_min(blk_f[0:1, :], blk_f[0:1, :], float(NE - 1)))
            link(v.tensor_copy(blk_i[0:1, 0:NBLK], blk_f[0:1, :]))
            link(v.tensor_copy(blk_i[0:1, NBLK:NBLK + 1], cnt[0:1, 1, NE - 1:NE]))
            v.sem_inc(blocks_ready, 1)
            for k in range(2):
                link(v.tensor_tensor(prod[:, :, k, :], OH[:, :, k, :], rank[:], ALU.mult))
            link(v.tensor_reduce(r1[:], prod[:], AX, ALU.add))
            for k in range(2):
                link(v.tensor_tensor(prod[:, :, k, :], OH[:, :, k, :],
                                     cnt[:, 2, :].unsqueeze(1).to_broadcast([P, TILES, NE]), ALU.mult))
            link(v.tensor_reduce(b1[:], prod[:], AX, ALU.add))
            r1f = r1.rearrange("p t k -> p (t k)")
            link(v.tensor_tensor(ge[:], r1f.unsqueeze(2).to_broadcast([P, 2 * TILES, SPLITS - 1]),
                                 m64[:, 1:SPLITS].unsqueeze(1).to_broadcast([P, 2 * TILES, SPLITS - 1]), ALU.is_ge))
            link(v.tensor_reduce(q1.rearrange("p t k -> p (t k)"), ge[:], AX, ALU.add))
            link(v.scalar_tensor_tensor(addr_f[:], r1[:], float(TW), b1[:], ALU.mult, ALU.add))
            link(v.scalar_tensor_tensor(addr_f[:], q1[:], float(1 - CAP * TW), addr_f[:], ALU.mult, ALU.add))
            link(v.tensor_copy(addr_i[:], addr_f[:]))
            v.sem_inc(addr_ready, 1)

            n = v.value_load(blk_i[0:1, NBLK:NBLK + 1], min_val=0, max_val=NBLK)
            with v.Fori(0, NBLK // 2) as i:
                for j in range(2):
                    with v.If(n > i * 2 + j):
                        v.wait_ge(sg_ready[j], i + 1)
                        v.wait_ge(tr_done[j], i + 1)
                        v.tensor_tensor(act[j][0:CAP, :], sg[j][CAP:2 * CAP, :], ps[CAP:2 * CAP, 2 + j, :], ALU.mult)\
                         .then_inc(act_ready[j], 1)
                        v.wait_ge(dn_done[j], i + 2)
                        v.wait_ge(moved[j], i * 16 + 16)
                        v.tensor_copy(yb[j][0:CAP, 0:512], ps[0:CAP, 4 + j, :]).then_inc(y_ready[j], 1)

            v.wait_ge(ln2_in, 32)
            roots[0] = 0
            for i in range(TILES):
                r = rows(i)
                x = x_tok[0:r, i, :]
                v.wait_ge(yw_ready, i + 1)
                y0 = yp[i][0:r, 0, :]
                link(v.scalar_tensor_tensor(y0, yp[i][0:r, 1, :], wpair[0:r, i, 1:2], y0, ALU.mult, ALU.add))
                link(v.tensor_tensor(y0, y0, modvec(3, i), ALU.mult))
                link(v.scalar_tensor_tensor(y0, x, ALPHA, y0, ALU.mult, ALU.add))
                layer_stats(y0, r, fin_q, fin_a)
                link(normalise(y0, y0, r))
                link(v.tensor_tensor(y0, y0, ln2[0:r, 0, :], ALU.mult))
                link(v.tensor_tensor(ft[i][0:r, :], y0, ln2[0:r, 1, :], ALU.add))
                v.sem_inc(y_out_ready, 1)

        @block.tensor
        def _(pe):
            def start(job):
                n = INDEX[job]
                if n >= 3:
                    pe.wait_ge(slot_free[n % 3], n // 3)
                return slot_banks(job)

            def done(ins):
                ins.then_inc(job_done, 1)

            tiles = [0]

            def weight_tile():
                s, _, turn = RING[tiles[0]]
                tiles[0] += 1
                pe.wait_ge(w_in_slot[s], 16 * turn)
                return ring[s]

            def tile_used():
                pe.sem_inc(w_used, 1)

            def project(job, w, col, m, src, k_blocks=KD):
                out = start(job)
                for h in range(2):
                    for k in range(k_blocks):
                        ins = pe.matmul(out[0:m, h, 0:HALF], w[:, k, col:col + m],
                                        src[:, k, h * HALF:(h + 1) * HALF], start=(k == 0), stop=(k == k_blocks - 1))
                done(ins)

            pe.wait_ge(pack_in, 16 * 14)
            pe.wait_ge(consts, 1)
            out = start(("pack", 0))
            for k in range(KD):
                ins = pe.transpose(out[:, 0, k * 64:k * 64 + ROWS], packrows[0:ROWS, k * P:(k + 1) * P], ident[0:ROWS, 0:ROWS])
            done(ins)
            for i in range(TILES):
                out = start(("xt", i))
                pe.wait_ge(xn_ready, i + 1)
                r = rows(i)
                for k in range(KD):
                    ins = pe.transpose(out[:, k // 4, (k % 4) * P:(k % 4) * P + r], xn[i % 2][0:r, k * P:(k + 1) * P],
                                       ident[0:r, 0:r])
                done(ins)
            pe.wait_ge(cs_ready, 1)
            for m in range(12):
                if m == 6:
                    out = start(("modT", 0))
                    for c in range(16):
                        ins = pe.transpose(out[:, 0, c * 9:c * 9 + 9], mod_sb[0:9, c * P:(c + 1) * P], ident[0:9, 0:9])
                    done(ins)
                w = weight_tile()
                out = start(("mod", m))
                for k in range(KD):
                    ins = pe.matmul(out[0:9, 0, :], cs[:, k, :], w[:, k, :], start=(k == 0), stop=(k == KD - 1))
                done(ins)
                pe.wait_ge(job_done, INDEX[("mod", m)] + 1)
                tile_used()
            pe.wait_ge(hT_act, KD)
            pe.wait_ge(hT_dve, 1)

            def last_of_tile(job):
                pe.wait_ge(job_done, INDEX[job] + 1)
                tile_used()

            for g in range(2):
                w = weight_tile()
                for c in range(4 * g, 4 * g + 4):
                    project(("rx", c), w, (c % 4) * P, P, hT)
                last_of_tile(("rx", 4 * g + 3))
                w = weight_tile()
                for c in range(4 * g, 4 * g + 4):
                    project(("ry", c), w, (c % 4) * P, P, hT)
                    if c == 4 * g + 3:
                        last_of_tile(("ry", c))
                    if c == 0:
                        pe.wait_ge(bd_in, 16 * 5)
                    pe.wait_ge(xc_ready, c + 1)
                    for job, gate in (("ra", bd[0]), ("ri", bd[1])):
                        out = start((job, c))
                        for h in range(2):
                            ins = pe.matmul(out[:, h, 0:HALF], gate[:, c, :], rg["xc"][c % 2][:, h * HALF:(h + 1) * HALF],
                                            start=True, stop=True)
                        done(ins)
            for g in range(2):
                w = weight_tile()
                for c in range(4 * g, 4 * g + 4):
                    project(("qk", c), w, (c % 4) * P, P, hT)
                last_of_tile(("qk", 4 * g + 3))
            pe.wait_ge(small_in, 16 * 5)
            project(("al", 0), alpha_w, 0, RANK, hT)
            pe.wait_ge(al_ready, 1)
            for c in range(HEADS):
                out = start(("la", c))
                for h in range(2):
                    ins = pe.matmul(out[:, h, 0:HALF], wa2[0:RANK, c * P:(c + 1) * P], al[0:RANK, h * HALF:(h + 1) * HALF],
                                    start=True, stop=True)
                done(ins)

            def v_transpose(c):
                pe.wait_ge(vf_ready, c + 1)
                out = start(("vt", c))
                for i in range(4):
                    pe.transpose(out[:, 0, i * P:(i + 1) * P], vf[c % 2][:, i * P:(i + 1) * P], ident[:])
                done(pe.transpose(out[0:NS, 1, 0:P], vf[c % 2][:, T:NT], ident[:]))

            for c in range(8):
                if c % 4 == 0:
                    w = weight_tile()
                project(("v", c), w, (c % 4) * P, P, hT)
                if c % 4 == 3:
                    last_of_tile(("v", c))
                if c:
                    v_transpose(c - 1)
            v_transpose(7)
            pe.wait_ge(gla_in_ready, 1)
            for i in range(4):
                out = start(("kt", i))
                for h in range(HEADS):
                    ins = pe.transpose(out[:, 0, h * P:(h + 1) * P], EX[:, h, i * P:(i + 1) * P], ident[:])
                done(ins)
            pe.wait_ge(vt_ready, 8)
            pe.wait_ge(kt_ready, 1)
            for n in range(NCH):
                q, tile = 64 * (n % 2), n // 2
                cols = slice(n * CH, (n + 1) * CH)
                if n >= 1:
                    pe.wait_ge(attm_ready, n)
                for h in range(HEADS):
                    ins = pe.matmul(ps[q:q + 64, 6, h * CH:(h + 1) * CH], Q[:, HEADS + h, cols], Q[:, h, cols],
                                    start=True, stop=True)
                ins.then_inc(at_done, 1)
                out = start(("ds", n))
                for h in range(HEADS):
                    ins = pe.matmul(out[:, h // 2, (h % 2) * DVH:(h % 2 + 1) * DVH],
                                    kout_tok[q:q + 64, tile, h * P:(h + 1) * P],
                                    v_tok[q:q + 64, tile, h * DVH:(h + 1) * DVH], start=True, stop=True)
                done(ins)
                out = start(("vb", n))
                for h in range(2):
                    ins = pe.matmul(out[:, h, :], ident[0:NS, n:n + 1].to_broadcast([NS, P]), v_samp[0:NS, h * 512:(h + 1) * 512],
                                    start=True, stop=True)
                done(ins)
                pe.wait_ge(attm_ready, n + 1)
                if n >= 1:
                    pe.wait_ge(s_ready, n)
                    pe.wait_ge(o_copied, n)
                for hd in range(8):
                    h, d = hd // 2, hd % 2
                    o = ps[:, 7, hd * CH:(hd + 1) * CH]
                    ins = pe.matmul(o, v_tok[q:q + 64, tile, hd * P:(hd + 1) * P], attm[n % 2][q:q + 64, h, :],
                                    start=True, stop=(n == 0))
                    if n:
                        ins = pe.matmul(o, S[n % 2][:, h, d * P:(d + 1) * P], Q[:, h, cols], start=False, stop=True)
                ins.then_inc(o_done, 1)
                pe.wait_ge(st_ready, n + 1)
                out = start(("os", n))
                for hd in range(8):
                    ins = pe.matmul(out[:, 0, hd:hd + 1], st[n % 2][:, hd // 2, (hd % 2) * P:(hd % 2 + 1) * P],
                                    qs[:, hd // 2, n:n + 1], start=True, stop=True)
                done(ins)

            def squares(h):
                pe.wait_ge(sq_ready, h + 1)
                out = start(("ss", h))
                for half in range(2):
                    for d in range(2):
                        ins = pe.matmul(out[:, half, 0:HALF], ones[:], sq[h % 2][:, d, half * HALF:(half + 1) * HALF],
                                        start=(d == 0), stop=(d == 1))
                done(ins)

            squares(0)
            squares(1)
            for c in range(8):
                if c % 4 == 0:
                    w = weight_tile()
                project(("gg", c), w, (c % 4) * P, P, hT)
                if c % 4 == 3:
                    last_of_tile(("gg", c))
                if c < 2:
                    squares(c + 2)
            for a, b, src, ready in (("ga", "pa", A, ya_ready), ("gb", "pb", O, yb_ready)):
                for g in range(2):
                    w = weight_tile()
                    for c in range(4 * g, 4 * g + 4):
                        project((a, c), w, (c % 4) * P, P, hT)
                    last_of_tile((a, 4 * g + 3))
                    w = weight_tile()
                    pe.wait_ge(ready, KD)
                    for c in range(4 * g, 4 * g + 4):
                        project((b, c), w, (c % 4) * P, P, src)
                    last_of_tile((b, 4 * g + 3))
            for k in range(4):
                out = start(("bc", k))
                for h in range(2):
                    c0 = (2 + k) * D + h * 512
                    ins = pe.matmul(out[:, h, :], sel8[0:9, :], mod_sb[0:9, c0:c0 + 512], start=True, stop=True)
                done(ins)
            for job, src, m in (("rlT", rl, 11), ("hlT", hl, 9)):
                out = start((job, 0))
                for k in range(KD):
                    ins = pe.transpose(out[0:m, k // 4, (k % 4) * P:(k % 4 + 1) * P], src[:, k, :], ident[:])
                done(ins)

            def route(i):
                r = rows(i)
                pe.wait_ge(hf_ready, i + 1)
                out = start(("ht", i))
                for k in range(KD):
                    ins = pe.transpose(out[:, k // 4, (k % 4) * P:(k % 4) * P + r], hf[i % 2][0:r, k * P:(k + 1) * P],
                                       ident[0:r, 0:r])
                done(ins)
                pe.wait_ge(hfT_ready, i + 1)
                out = start(("lg", i))
                for k in range(KD):
                    ins = pe.matmul(out[0:r, 0, 0:NG + NE], hfT[i % 2][:, k, 0:r], route_w[:, k, :],
                                    start=(k == 0), stop=(k == KD - 1))
                done(ins)

            pe.wait_ge(z_ready, KD)
            wo = [weight_tile(), weight_tile()]
            for i in range(TILES):
                r = rows(i)
                out = start(("wo", i))
                for h in range(2):
                    for k in range(KD):
                        ins = pe.matmul(out[0:r, h, :], Z[:, k, i * P:i * P + r], wo[h][:, k, :],
                                        start=(k == 0), stop=(k == KD - 1))
                done(ins)
                if i >= 1:
                    route(i - 1)
            route(4)
            pe.wait_ge(m_ready, 1)
            out = start(("rk", 0))
            for i in range(TILES + 1):
                o = out[:, 0, i * NE:(i + 1) * NE]
                for k in range(min(i, TILES)):
                    r = rows(k)
                    pe.matmul(o, ones[0:r, :], M[0:r, k, :], start=(k == 0), stop=(i == TILES and k == TILES - 1))
                if i < TILES:
                    r = rows(i)
                    pe.matmul(o, upper[0:r, :], M[0:r, i, :], start=(i == 0), stop=True)
            done(pe.matmul(out[:, 0, 480:512], ones[:], M[:, 0, :], start=True, stop=True))

            def transpose_rows(j):
                pe.sem_inc(pe_turns, 1)
                for k in range(KD):
                    ins = pe.transpose(ps[:, j, k * CAP:(k + 1) * CAP],
                                       xg[j][0:CAP, :].rearrange("s (p k) -> s k p", k=KD)[:, k, :], ident[0:CAP, 0:CAP])
                ins.then_inc(xt_done[j], 1)

            pe.wait_ge(started, 1)
            pe.wait_ge(blocks_ready, 1)
            pe.wait_ge(xg_in[0], 16)
            transpose_rows(0)
            n = pe.value_load(blk_i[0:1, NBLK:NBLK + 1], min_val=0, max_val=NBLK)
            with pe.Fori(0, NBLK // 2) as i:
                for j in range(2):
                    with pe.If(n > i * 2 + j):
                        pe.wait_ge(xT_ready[j], i + 2)
                        pe.wait_ge(act_ready[j], i + 1)
                        pe.wait_ge(we_in[3 * j], i * 16 + 16)
                        pe.wait_ge(we_in[3 * j + 1], i * 16 + 16)
                        for k in range(KD):
                            for q in range(2):
                                ins = pe.matmul(ps[CAP * q:CAP * q + CAP, 2 + j, :], xT[j][:, k, :], ring[3 * j + q][:, k, :],
                                                start=(k == 0), stop=(k == KD - 1))
                        ins.then_inc(gu_done[j], 1)
                        pe.wait_ge(xg_in[1 - j], i * 16 + 16 * (1 + j))
                        pe.wait_ge(xT_ready[1 - j], i + (1 + j))
                        transpose_rows(1 - j)
                        pe.wait_ge(act_ready[j], i + 2)
                        pe.wait_ge(acT_ready[j], i + 1)
                        pe.sem_inc(pe_turns, 1)
                        for k in range(4):
                            ins = pe.transpose(ps[:, 6 + j, k * CAP:(k + 1) * CAP],
                                               act[j][0:CAP, :].rearrange("s (p k) -> s k p", k=4)[:, k, :],
                                               ident[0:CAP, 0:CAP])
                        ins.then_inc(tr_done[j], 1)
                        pe.wait_ge(acT_ready[j], i + 2)
                        pe.wait_ge(y_ready[j], i * 2 + 1)
                        pe.wait_ge(we_in[3 * j + 2], i * 16 + 16)
                        wd = ring[3 * j + 2].rearrange("p k n -> p (k n)").rearrange("p (k n) -> p k n", k=4)
                        for k in range(4):
                            for q in range(2):
                                ins = pe.matmul(ps[CAP * q:CAP * q + CAP, 4 + j, :], acT[j][:, k, :],
                                                wd[:, k, q * 512:(q + 1) * 512], start=(k == 0), stop=(k == 3))
                        ins.then_inc(dn_done[j], 1)


_INS = ["x_prompt", "x_sample", "state_conv", "state_rglru", "state_gla", "c_prompt", "c_sample", "w_mod", "b_mod",
        "w_in", "b_in", "conv_w", "conv_b", "rg_wa", "rg_ba", "rg_wx", "rg_bx", "rg_lambda", "gla_wa2", "gla_ba",
        "gla_norm_g", "p_a", "p_b", "w_o", "ln1_g", "ln1_b", "w_grp", "b_grp", "w_exp", "b_exp", "we_gate", "we_up",
        "we_down", "ln2_g", "ln2_b"]
_OUTS = [(1, T, D), (NS, 1, D), (1, 1, CONV - 1, D), (1, 1, D), (1, 1, HEADS, DKH, DVH), (1, NS, CONV - 1, D),
         (1, NS, D), (1, NS, HEADS, DKH, DVH)]


def kernel(**inputs):
    import numpy as np
    import concourse.bacc as bacc
    from concourse.bass_utils import run_bass_kernel_spmd as run

    nc = bacc.Bacc("TRN2", target_bir_lowering=False, num_devices=1)
    arrays, t = {}, {}
    for name in _INS:
        a = np.ascontiguousarray(inputs[name])
        arrays[f"in_{name}"] = a
        t[name] = nc.dram_tensor(f"in_{name}", a.shape, mybir.dt.from_np(a.dtype), kind="ExternalInput").ap()
    outs = [nc.dram_tensor(f"out_{i}", s, F32, kind="ExternalOutput").ap() for i, s in enumerate(_OUTS)]
    build(nc, t, outs)
    r = run(nc, [arrays], core_ids=[0])
    return tuple(r.results[0][f"out_{i}"] for i in range(len(_OUTS)))
```

```python
from contextlib import ExitStack

import concourse.bass as bass
from concourse import mybir

F32 = mybir.dt.float32
I32 = mybir.dt.int32
ACT = mybir.ActivationFunctionType
ALU = mybir.AluOpType
AX = mybir.AxisListType.X

P = 128
D = 1024
KD = D // P
T = 512
NS = 8
NT = T + NS
HALF = NT // 2
TILES = 5
ORDER = (4, 0, 1, 2, 3)
CONV = 4
HEADS = 4
DKH = 128
DVH = 256
CH = 64
NCH = T // CH
RANK = 16
TAU = 16.0
NG = 4
EPG = 8
NE = NG * EPG
DE = 512
CAP = 64
PAIRS = 2 * NT
NBLK = 48
TW = NBLK + 2
SPLITS = 9
OOB = 1 << 20
ALPHA = 2.0 ** 0.25
LN_EPS = 1e-5
RMS_EPS = 1e-6
BIG = 1e30
WT = KD * 512

R_C = 0
R_CONVST = 9
R_H0 = 33
R_CONVW = 41
R_CONVB = 45
R_BA = 46
R_BX = 47
R_LAM = 48
R_BIN = 49
R_MISC = 56
ROWS = 57


EARLY_MOD = 4
LATE_MOD = {("rx", 1): 4, ("rx", 3): 5, ("ry", 1): 6, ("ry", 3): 7, ("rx", 5): 8, ("rx", 7): 9, ("ry", 5): 10, ("ry", 7): 11}


def plan_jobs():
    jobs = [("pack", 0), ("xt", 0), ("xt", 1)]
    for m in range(3):
        jobs += [("mod", m), ("xt", m + 2)]
    jobs += [("mod", 3), ("modT", 0)]
    for g in range(2):
        for c in range(4 * g, 4 * g + 4):
            jobs.append(("rx", c))
            if c % 2:
                jobs.append(("mod", LATE_MOD[("rx", c)]))
        for c in range(4 * g, 4 * g + 4):
            jobs += [("ry", c), ("ra", c), ("ri", c)]
            if c % 2:
                jobs.append(("mod", LATE_MOD[("ry", c)]))
    jobs += [("qk", c) for c in range(8)] + [("al", 0)] + [("la", c) for c in range(HEADS)]
    for c in range(8):
        jobs.append(("v", c))
        if c:
            jobs.append(("vt", c - 1))
    jobs.append(("vt", 7))
    jobs += [("kt", i) for i in range(4)]
    for n in range(NCH):
        jobs += [("ds", n), ("vb", n), ("os", n)]
    jobs += [("ss", 0), ("ss", 1), ("gg", 0), ("ss", 2), ("gg", 1), ("ss", 3)]
    jobs += [("gg", c) for c in range(2, 8)]
    for a, b in (("ga", "pa"), ("gb", "pb")):
        for g in range(2):
            jobs += [(a, c) for c in range(4 * g, 4 * g + 4)] + [(b, c) for c in range(4 * g, 4 * g + 4)]
    jobs += [("bc", v) for v in range(4)] + [("rlT", 0), ("hlT", 0)]
    for p in range(TILES):
        jobs.append(("wo", ORDER[p]))
        if p >= 1:
            jobs += [("ht", ORDER[p - 1]), ("lg", ORDER[p - 1])]
    jobs += [("ht", ORDER[4]), ("lg", ORDER[4]), ("rk", 0)]
    return jobs


JOBS = plan_jobs()
INDEX = {job: n for n, job in enumerate(JOBS)}
WTILES = ([("w_mod", m * 512) for m in range(EARLY_MOD)]
          + [("w_in", c) for c in (0, 1024, 512, 1536, 2048, 2560, 3072, 3584, 4096, 4608)]
          + [("w_in", 5136), ("p_a", 0), ("w_in", 5136 + 512), ("p_a", 512)]
          + [("w_in", 6160), ("p_b", 0), ("w_in", 6160 + 512), ("p_b", 512)]
          + [("w_o", 0), ("w_o", 512)])
MOD_TILES = EARLY_MOD


def ring_slot(t):
    return t % 3 if t < MOD_TILES else t % 2


def ring_plan():
    last, turns, plan = {}, {}, []
    for t in range(len(WTILES)):
        s = ring_slot(t)
        turns[s] = turns.get(s, 0) + 1
        plan.append((s, last.get(s), turns[s]))
        last[s] = t
    return plan


RING = ring_plan()


def build(nc, t, outs):
    (y_prompt, y_sample, new_conv_p, new_rg_p, new_gla_p, new_conv_s, new_rg_s, new_gla_s) = outs
    hf_dram = nc.dram_tensor("hf_scratch", (NT, D), F32, kind="Internal").ap()
    table_dram = nc.dram_tensor("table_scratch", (CAP * TW, 2), I32, kind="Internal").ap()
    pair_dram = nc.dram_tensor("pair_scratch", (PAIRS, D), F32, kind="Internal").ap()

    with ExitStack() as ctx:
        sem_names = {}

        def sem(name):
            sem_names[name] = ctx.enter_context(nc.semaphore(name))
            return sem_names[name]

        MEM = 53100
        mem = ctx.enter_context(nc.sbuf_tensor("mem", [P, MEM], F32))
        ps = ctx.enter_context(nc.psum_tensor("ps", [P, 8, 512], F32))

        def area(at, *shape):
            n = 1
            for s in shape:
                n *= s
            v = mem[:, at:at + n]
            if len(shape) == 2:
                v = v.rearrange("p (a b) -> p a b", b=shape[1])
            if len(shape) == 3:
                v = v.rearrange("p (a b c) -> p a b c", b=shape[1], c=shape[2])
            return v

        ring = [area(s * WT, KD, 512) for s in range(6)]
        B = 3 * WT
        hT = area(B, KD, NT)
        O = area(B + 4160, KD, NT)
        TB = B + 8320
        xn = [area(TB + 1024 * j, D) for j in range(2)]
        packrows = area(TB + 2048, D)
        v_tok = area(2 * WT, 4, D)
        bd = [area(2 * WT + 1024 * j, KD, P) for j in range(2)]
        x_tok = area(6 * WT, TILES, D)
        mod_sb = area(6 * WT + 5120, 6 * D)
        A0 = 6 * WT + 5120 + 6144
        A = area(A0, KD, NT)
        Q = area(A0 + 4160, KD, NT)
        mod_w = area(A0 + 4160, KD, 512)
        Z0 = A0 + 8320
        Z = area(Z0, KD, NT)
        L = area(Z0, HEADS, NT)
        K2 = area(Z0 + 2080, HEADS, NT)
        EX = area(TB, HEADS, NT)
        rg = {n: [area(Z0 + (2 * i + j) * NT, NT) for j in range(2)]
              for i, n in enumerate(("xc", "r", "i", "a"))}
        rg["th"] = [area(TB + j * NT, NT) for j in range(2)]
        rg["sq"] = [area(TB + (2 + j) * NT, NT) for j in range(2)]
        vf = [area(Z0 + j * NT, NT) for j in range(2)]
        S = [area(Z0, HEADS, DVH), area(Z0 + 1040, HEADS, DVH)]
        kout_tok = area(Z0 + 2080, 4, 512)
        st = [area(TB + 1024 * j, HEADS, DVH) for j in range(2)]
        attm = [area(TB + 2048 + 256 * j, HEADS, CH) for j in range(2)]
        sq = [area(TB + 1040 * j, 2, NT) for j in range(2)]
        rms = [area(Z0 + 2080 + NT * j, NT) for j in range(2)]
        gt = [area(Z0 + 3120 + NT * j, NT) for j in range(2)]
        bc = area(A0, 4, D)
        lnp = area(A0 + 4160, 2, D)
        hf = [area(A0 + 4160 + 2048 + 1024 * j, D) for j in range(2)]
        lt = area(B + WT + 2048, D)
        hfT = [area(B + WT + 1024 * j, KD, P) for j in range(2)]
        xT = [area(Z0 + 512 * j, KD, CAP) for j in range(2)]
        sg = [area(Z0 + 1024 + 512 * j, DE) for j in range(2)]
        act = [area(Z0 + 2048 + 512 * j, DE) for j in range(2)]
        acT = [area(Z0 + 3072 + 256 * j, 4, CAP) for j in range(2)]
        xg = [area(A0 + 4160 + 1024 * j, D) for j in range(2)]
        yb = [area(A0 + 4160 + 2048 + 1024 * j, D) for j in range(2)]
        ln2 = area(0, 2, D)
        yp = [area(WT + 2048 * i, 2, D) for i in range(TILES)]
        ft = [area(4 * WT + 1024 * j, D) for j in range(TILES)]
        small = [Z0 + 4160]

        def keep(*shape):
            n = 1
            for s in shape:
                n *= s
            v = area(small[0], *shape)
            small[0] += n
            assert small[0] <= MEM, small[0]
            return v

        ident = keep(P)
        ones = keep(P)
        upper = keep(P)
        maskT = keep(CH)
        sel8 = keep(P)
        fp = keep(KD, ROWS)
        cs = keep(KD, 9)
        modT = keep(16, 9)
        alpha_w = keep(KD, RANK)
        route_w = keep(KD, NG + NE)
        route_b = keep(NG + NE)
        lam = keep(6, 8)
        rl = keep(KD, 11)
        hl = keep(KD, 9)
        tmp8 = keep(4, 8)
        qs = keep(HEADS, NS)
        ela = keep(HEADS, NS)
        dec = keep(HEADS, NCH)
        bt = keep(HEADS, NCH)
        stats = keep(2, 6)
        mv = keep(4)
        wpair = keep(TILES, 2)
        fmv = keep(TILES, 4)
        wa2 = area(2 * WT + 2048, 512)
        al = area(2 * WT + 2560, NT)
        scan_mask = area(2 * WT + 3080, NT)
        v_samp = area(2 * WT, D)
        v_samp = keep(D)
        rt = [TB]

        def rtmp(*shape):
            n = 1
            for s in shape:
                n *= s
            v = area(rt[0], *shape)
            rt[0] += n
            assert rt[0] <= TB + 3968
            return v

        LG = rtmp(TILES, NG + NE)
        j4 = rtmp(NG)
        j32 = rtmp(NE)
        m64 = rtmp(SPLITS)
        g_eq = rtmp(TILES, NG)
        g_e = rtmp(TILES, NG)
        g_m = rtmp(12, TILES)
        ml = rtmp(TILES, NE)
        e_eq = rtmp(TILES, NE)
        OH = rtmp(TILES, 2, NE)
        M = rtmp(TILES, NE)
        rank = rtmp(TILES, NE)
        before = rtmp(TILES + 1, NE)
        cnt = rtmp(5, NE)
        pl_f = rtmp(2 * NBLK)
        pl_i = rtmp(2 * NBLK).bitcast(I32)
        many = rtmp(NE, SPLITS)
        prod = rtmp(TILES, 2, NE)
        r1 = rtmp(TILES, 2)
        b1 = rtmp(TILES, 2)
        q1 = rtmp(TILES, 2)
        ge = rtmp(TILES * 2, SPLITS - 1)
        blk_f = rtmp(NBLK)
        iota_i = rtmp(64)
        addr_f = rtmp(TILES, 2)
        addr_i = keep(TILES, 2).bitcast(I32)
        payload = keep(TILES, 2, 2).bitcast(I32)
        plan = area(Z0 + 3720, 3 * NBLK + 2 * NE + 4).bitcast(I32)
        BLK_SLOT, BLK_IN0, BLK_IN1 = 0, NBLK, 2 * NBLK
        LD_EXPERT, LD_AFTER = 3 * NBLK, 3 * NBLK + NE
        N_BLK, N_LD, N_EVEN, N_ODD = (3 * NBLK + 2 * NE + k for k in range(4))
        idx = area(Z0 + 3584, TW, 2).bitcast(I32)
        gidx = [area(Z0 + 3700 + j, 1).bitcast(I32) for j in range(2)]
        sidx = [area(Z0 + 3702 + j, 1).bitcast(I32) for j in range(2)]
        oobt = area(2 * WT, TW * 2).bitcast(I32)
        outrow = area(2 * WT + 1024, 2, D)

        job_done = sem("job_done")
        slot_free = [sem(f"slot_free{s}") for s in range(3)]
        w_in_slot = [sem(f"w_in_slot{s}") for s in range(3)]
        w_used = sem("w_used")
        rows_clear = sem("rows_clear")
        pack_in = sem("pack_in")
        x_in = sem("x_in")
        bmod_in = sem("bmod_in")
        mod_w_in = sem("mod_w_in")
        mod_ready = sem("mod_ready")
        small_in = sem("small_in")
        bd_clear = sem("bd_clear")
        bd_in = sem("bd_in")
        consts = sem("consts")
        pool_step = sem("pool_step")
        act_step = sem("act_step")
        dve_step = sem("dve_step")
        xn_ready = sem("xn_ready")
        rstd_q = sem("rstd_q")
        rstd_a = sem("rstd_a")
        cs_ready = sem("cs_ready")
        x_tr = sem("x_tr")
        modT_ready = sem("modT_ready")
        hT_act = sem("hT_act")
        hT_dve = sem("hT_dve")
        lam_q = sem("lam_q")
        lam_a = sem("lam_a")
        lam_ready = sem("lam_ready")
        rx_ready = sem("rx_ready")
        ry_ready = sem("ry_ready")
        xc_ready = sem("xc_ready")
        gates_ready = sem("gates_ready")
        th_ready = sem("th_ready")
        sqrt_ready = sem("sqrt_ready")
        ya_ready = sem("ya_ready")
        qk_ready = sem("qk_ready")
        al_ready = sem("al_ready")
        lax_ready = sem("lax_ready")
        nabs_ready = sem("nabs_ready")
        log_ready = sem("log_ready")
        bcum_ready = sem("bcum_ready")
        e1_ready = sem("e1_ready")
        dexp_q = sem("dexp_q")
        e2_ready = sem("e2_ready")
        gla_in_ready = sem("gla_in_ready")
        vf_ready = sem("vf_ready")
        vt_ready = sem("vt_ready")
        kt_ready = sem("kt_ready")
        at_done = sem("at_done")
        attm_ready = sem("attm_ready")
        o_done = sem("o_done")
        o_copied = sem("o_copied")
        s_ready = sem("s_ready")
        st_in = [sem(f"st_in{j}") for j in range(2)]
        st_ready = sem("st_ready")
        st_out = [sem(f"st_out{j}") for j in range(2)]
        os_copied = sem("os_copied")
        sq_ready = sem("sq_ready")
        var_ready = sem("var_ready")
        rms_ready = sem("rms_ready")
        gt_ready = sem("gt_ready")
        yb_ready = sem("yb_ready")
        sig_ready = sem("sig_ready")
        z_ready = sem("z_ready")
        s_out = sem("s_out")
        outs_ready = sem("outs_ready")
        lnp_in = sem("lnp_in")
        hf_ready = sem("hf_ready")
        hf_out = [sem(f"hf_out{j}") for j in range(2)]
        hfT_ready = sem("hfT_ready")
        ge_q = sem("ge_q")
        ge_a = sem("ge_a")
        m_ready = sem("m_ready")
        iotas = sem("iotas")
        addr_ready = sem("addr_ready")
        table_clear = sem("table_clear")
        oob_ready = sem("oob_ready")
        table_filled = sem("table_filled")
        loads_ready = sem("loads_ready")
        blocks_ready = sem("blocks_ready")
        pair = lambda name: [sem(f"{name}{j}") for j in range(2)]
        we_in = [sem(f"we_in{s}") for s in range(6)]
        xg_clear = sem("xg_clear")
        gidx_copied = sem("gidx_copied")
        sidx_copied = sem("sidx_copied")
        xg_in = pair("xg_in")
        moved = pair("moved")
        xt_done = pair("xt_done")
        xT_ready = pair("xT_ready")
        gu_done = sem("gu_done")
        sg_ready = pair("sg_ready")
        act_ready = pair("act_ready")
        tr_done = pair("tr_done")
        acT_ready = pair("acT_ready")
        dn_done = sem("dn_done")
        y_ready = pair("y_ready")
        started = sem("started")
        scattered = sem("scattered")
        pe_turns = sem("pe_turns")
        pool_turns = sem("pool_turns")
        sp_turns = sem("sp_turns")
        ln2_in = sem("ln2_in")
        yp_in = [sem(f"yp_in{i}") for i in range(TILES)]
        yw_ready = sem("yw_ready")
        fin_q = sem("fin_q")
        fin_a = sem("fin_a")
        norm_ready = sem("norm_ready")
        y_out_ready = sem("y_out_ready")
        out_sem = sem("out_sem")
        STARTS_AT_ONE = [s for l in (xt_done, xT_ready, act_ready, tr_done, acT_ready, y_ready)
                         for s in l]

        def rows(i):
            return P if i < 4 else NS

        def slot_banks(job):
            s = 2 * (INDEX[job] % 3)
            return ps[:, s:s + 2, :]

        def two_halves(job):
            return slot_banks(job)[:, :, 0:HALF]

        def halves(v):
            return v.rearrange("p (h n) -> p h n", h=2)

        def await_job(eng, job):
            eng.wait_ge(job_done, INDEX[job] + 1)

        def freed(job):
            return slot_free[INDEX[job] % 3]

        block = ctx.enter_context(nc.Block())

        @block.sync
        def _(sp):
            sp.dma_start(x_tok[0:NS, 4, :], t["x_sample"].rearrange("b o d -> (b o) d")).then_inc(x_in, 16)
            sp.dma_start(x_tok[:, 0:4, :], t["x_prompt"][0].rearrange("(i p) d -> p i d", p=P)).then_inc(x_in, 16)

            def load_tile(n):
                name, col = WTILES[n]
                s, before, _ = RING[n]
                if before is not None:
                    sp.wait_ge(w_used, before + 1)
                sp.dma_start(ring[s], t[name][0][:, col:col + 512].rearrange("(k p) n -> p k n", p=P))\
                  .then_inc(w_in_slot[s], 16)

            def load_late_mod(m):
                if m > EARLY_MOD:
                    sp.wait_ge(job_done, INDEX[("mod", m - 1)] + 1)
                sp.dma_start(mod_w[:], t["w_mod"][0][:, m * 512:(m + 1) * 512].rearrange("(k p) n -> p k n", p=P))\
                  .then_inc(mod_w_in, 16)

            for n in range(MOD_TILES + 2):
                load_tile(n)
            load_late_mod(EARLY_MOD)
            for n in range(3):
                load_late_mod(EARLY_MOD + 1 + 2 * n)
                load_tile(MOD_TILES + 2 + n)
                load_late_mod(EARLY_MOD + 2 + 2 * n)
            load_late_mod(11)
            for n in range(MOD_TILES + 5, MOD_TILES + 8):
                load_tile(n)

            def load_state(b):
                if b >= 2:
                    sp.wait_ge(st_out[b % 2], 16 * (b // 2))
                    sp.wait_ge(job_done, INDEX[("os", b - 2)] + 1)
                else:
                    sp.wait_ge(job_done, INDEX[("kt", 3)] + 1)
                    sp.wait_ge(kt_ready, 1)
                sp.dma_start(st[b % 2], t["state_gla"][0, b].rearrange("h k v -> k h v")).then_inc(st_in[b % 2], 16)

            load_tile(MOD_TILES + 8)
            load_state(0)
            load_state(1)
            for b in range(NS):
                sp.wait_ge(st_ready, b + 1)
                sp.dma_start(new_gla_s[0, b].rearrange("h k v -> k h v"), st[b % 2]).then_inc(st_out[b % 2], 16)
                if b + 2 < NS:
                    load_state(b + 2)
            sp.wait_ge(s_ready, NCH)
            sp.dma_start(new_gla_p[0, 0].rearrange("h k v -> k h v"), S[NCH % 2]).then_inc(s_out, 16)
            for n in range(MOD_TILES + 9, len(WTILES)):
                load_tile(n)
            sp.wait_ge(outs_ready, 1)
            sp.dma_start(new_conv_p[0, 0], outrow[0:3, 0, :]).then_inc(out_sem, 16)
            sp.dma_start(new_conv_s[0, :, 2, :], outrow[3:11, 0, :]).then_inc(out_sem, 16)
            sp.wait_ge(outs_ready, 2)
            sp.dma_start(new_rg_p[0], outrow[0:1, 1, :]).then_inc(out_sem, 16)
            sp.dma_start(new_rg_s[0], outrow[1:9, 1, :]).then_inc(out_sem, 16)
            for m in range(3):
                sp.sem_inc(we_in[3 + m], 16)

            def load_expert(slot, m, e):
                w = t[("we_gate", "we_up", "we_down")[m]][0, bass.ds(e, 1) if not isinstance(e, int) else slice(e, e + 1)]
                to = ring[3 * slot + m]
                if m < 2:
                    sp.dma_start(to, w.rearrange("o (p k) n -> p (o k) n", p=P)).then_inc(we_in[3 * slot + m], 16)
                else:
                    sp.dma_start(to.rearrange("p k n -> p (k n)"), w.rearrange("o (p k) n -> p (o k n)", p=P))\
                      .then_inc(we_in[3 * slot + m], 16)

            def store_hf(p):
                i = ORDER[p]
                sp.wait_ge(hf_ready, p + 1)
                sp.dma_start(hf_dram[i * P:i * P + rows(i), :], hf[p % 2][0:rows(i), :]).then_inc(hf_out[p % 2], 16)

            sp.wait_ge(out_sem, 16 * 4)
            load_expert(0, 2, 0)
            for p in range(4):
                store_hf(p)
            sp.wait_ge(job_done, INDEX[("wo", ORDER[4])] + 1)
            load_expert(0, 0, 0)
            load_expert(0, 1, 0)
            load_expert(1, 0, 1)
            store_hf(4)
            sp.wait_ge(job_done, INDEX[("lg", ORDER[4])] + 1)
            load_expert(1, 1, 1)
            sp.wait_ge(blocks_ready, 1)
            load_expert(1, 2, 1)
            sp.wait_ge(loads_ready, 1)
            sp.wait_ge(started, 1)
            n = sp.value_load(plan[0:1, N_LD:N_LD + 1], min_val=0, max_val=NE)
            with sp.Fori(1, NE // 2) as i:
                for j in range(2):
                    with sp.If(n > i * 2 + j):
                        e = sp.value_load(plan[0:1, bass.ds(i * 2 + (j + LD_EXPERT), 1)], min_val=0, max_val=NE - 1)
                        after = sp.value_load(plan[0:1, bass.ds(i * 2 + (j + LD_AFTER), 1)], min_val=0, max_val=NBLK)
                        for m in range(3):
                            if m != 1:
                                sp.wait_ge(gu_done if m == 0 else dn_done, after + 2)
                                sp.sem_inc(sp_turns, 1)
                            sp.wait_ge(we_in[3 * j + m], i * 16 + 16 * j)
                            load_expert(j, m, e)
            sp.wait_ge(scattered, 1)
            for i in range(TILES):
                r = rows(i)
                sp.dma_start(yp[i][0:r], pair_dram[2 * P * i:2 * P * i + 2 * r, :].rearrange("(p k) d -> p k d", k=2))\
                  .then_inc(yp_in[i], 16)
            for v, name in enumerate(("ln2_g", "ln2_b")):
                sp.dma_start(ln2[:, v, :], t[name][0:1, :].to_broadcast([P, D])).then_inc(ln2_in, 16)
            for i in range(TILES):
                sp.wait_ge(y_out_ready, i + 1)
                r = rows(i)
                dst = y_prompt[0][i * P:i * P + r, :] if i < 4 else y_sample.rearrange("b o d -> (b o) d")
                sp.dma_start(dst, ft[i][0:r, :]).then_inc(out_sem, 16)
            sp.wait_ge(out_sem, 16 * (4 + TILES))
            sp.wait_ge(s_out, 16)
            for j in range(2):
                sp.wait_ge(st_out[j], 16 * (NS // 2))

        @block.gpsimd
        def _(pool):
            steps = [0]

            def link(ins):
                steps[0] += 1
                ins.then_inc(pool_step, 1)
                pool.wait_ge(pool_step, steps[0])

            link(pool.memset(packrows[0:ROWS, :], 0.0))
            pool.sem_inc(rows_clear, 1)
            link(pool.memset(ident[:], 0.0))
            link(pool.memset(ones[:], 1.0))
            link(pool.memset(maskT[:], 1.0))
            link(pool.affine_select(out=ident[:], in_=ident[:], compare_op=ALU.not_equal, fill=1.0, base=0,
                               pattern=[[-1, P]], channel_multiplier=1))
            link(pool.affine_select(out=upper[:], in_=ones[:], compare_op=ALU.is_ge, fill=0.0, base=-1,
                               pattern=[[1, P]], channel_multiplier=-1))
            link(pool.affine_select(out=sel8[0:9, :], in_=ones[0:9, :], compare_op=ALU.is_ge, fill=0.0, base=-8,
                               pattern=[[0, P]], channel_multiplier=1))
            for q in range(2):
                m = maskT[64 * q:64 * q + 64, :]
                link(pool.affine_select(out=m, in_=m, compare_op=ALU.is_ge, fill=0.0, base=0,
                                   pattern=[[1, CH]], channel_multiplier=-1))
            pool.sem_inc(consts, 1)
            pool.wait_ge(w_used, MOD_TILES)
            link(pool.memset(bd[0], 0.0))
            link(pool.memset(bd[1], 0.0))
            for g, name in enumerate(("rg_wa", "rg_wx")):
                w = t[name][0].rearrange("(c two) i j -> two i c j", two=2)
                for q in range(2):
                    pool.dma_start(bd[g][64 * q:64 * q + 64, :, 64 * q:64 * q + 64], w[q]).then_inc(bd_in, 16)
            pool.dma_start(wa2[0:RANK, :], t["gla_wa2"][0]).then_inc(bd_in, 16)
            link(pool.memset(scan_mask[:], 1.0))
            link(pool.memset(scan_mask[:, 0:T:CH], 0.0))
            link(pool.memset(scan_mask[:, T:NT], 0.0))
            pool.sem_inc(consts, 1)

            pool.wait_ge(o_done, NCH)
            pool.iota(oobt[0:CAP, :], pattern=[[0, TW * 2]], base=OOB, channel_multiplier=0).then_inc(oob_ready, 1)
            pool.wait_ge(oob_ready, 1)
            pool.dma_start(table_dram.rearrange("(p b) c -> p (b c)", p=CAP), oobt[0:CAP, :]).then_inc(table_clear, 16)
            pool.wait_ge(yb_ready, KD)
            ii = iota_i.bitcast(I32)
            link(pool.iota(ii[:, 0:NG], pattern=[[1, NG]], base=-99, channel_multiplier=0))
            link(pool.tensor_copy(j4[:], ii[:, 0:NG]))
            link(pool.iota(ii[:, 0:NE], pattern=[[1, NE]], base=-99, channel_multiplier=0))
            link(pool.tensor_copy(j32[:], ii[:, 0:NE]))
            link(pool.iota(ii[:, 0:SPLITS], pattern=[[CAP, SPLITS]], base=0, channel_multiplier=0))
            link(pool.tensor_copy(m64[:], ii[:, 0:SPLITS]))
            link(pool.iota(ii[:, 0:NBLK], pattern=[[1, NBLK]], base=0, channel_multiplier=0))
            link(pool.tensor_copy(blk_f[:], ii[:, 0:NBLK]))
            for k in range(2):
                link(pool.iota(payload[:, :, k, 0], pattern=[[P, TILES]], base=0, channel_multiplier=1))
                link(pool.iota(payload[:, :, k, 1], pattern=[[2 * P, TILES]], base=k, channel_multiplier=2))
            link(pool.memset(LG[:, 4, :], 0.0))
            link(pool.memset(before[:, 0, :], 0.0))
            pool.sem_inc(iotas, 1)
            for s in STARTS_AT_ONE:
                pool.sem_inc(s, 1)
            pool.sem_inc(gu_done, 2)
            pool.sem_inc(dn_done, 2)
            pool.sem_inc(started, 1)
            pool.wait_ge(addr_ready, 1)
            pool.wait_ge(table_clear, 16)
            for i in range(TILES):
                for k in range(2):
                    pool.indirect_dma_start(
                        table_dram, bass.IndirectOffsetOnAxis(ap=addr_i[0:rows(i), i, k:k + 1], axis=0),
                        payload[0:rows(i), i, k, :], None).then_inc(table_filled, 16)
            for j in range(2):
                link(pool.memset(xg[j][0:CAP, :], 0.0))
            pool.wait_ge(table_filled, 16 * 2 * TILES)
            tv = table_dram.rearrange("(p b) c -> p b c", p=CAP)
            for j in range(2):
                h = TW // 2
                pool.dma_start(idx[0:CAP, j * h:j * h + h, :], tv[:, j * h:j * h + h, :]).then_inc(moved[j], 16)
            pool.wait_ge(moved[0], 16)
            pool.wait_ge(moved[1], 16)
            for j in range(2):
                pool.wait_ge(hf_out[j], 16 * (3 - j))

            def gather(j):
                pool.sem_inc(pool_turns, 1)
                pool.indirect_dma_start(xg[j][0:CAP, :], None, hf_dram,
                                        bass.IndirectOffsetOnAxis(ap=gidx[j][0:CAP, 0:1], axis=0),
                                        bounds_check=NT - 1, oob_is_err=False).then_inc(xg_in[j], 16)

            for j in range(2):
                pool.tensor_copy(gidx[j][0:CAP, :], idx[0:CAP, j, 0:1]).then_inc(gidx_copied, 1)
                pool.wait_ge(gidx_copied, j + 1)
                gather(j)
            pool.wait_ge(blocks_ready, 1)
            n = pool.value_load(plan[0:1, N_BLK:N_BLK + 1], min_val=0, max_val=NBLK)

            def column(b, c):
                return idx[0:CAP, bass.ds(b, 1), c:c + 1].rearrange("p o c -> p (o c)")

            def scatter(i, j):
                pool.wait_ge(moved[j], i * 16 + 16)
                pool.tensor_copy(sidx[j][0:CAP, :], column(i * 2 + j, 1)).then_inc(sidx_copied, 1)
                pool.wait_ge(sidx_copied, i * 2 + (j + 1))
                pool.wait_ge(y_ready[j], i * 2 + 3)
                pool.sem_inc(pool_turns, 1)
                pool.indirect_dma_start(
                    pair_dram, bass.IndirectOffsetOnAxis(ap=sidx[j][0:CAP, 0:1], axis=0),
                    yb[j][0:CAP, :], None, bounds_check=PAIRS - 1, oob_is_err=False).then_inc(moved[j], 16)

            def two_blocks(i):
                for j in range(2):
                    with pool.If(n > i * 2 + j):
                        pool.wait_ge(xt_done[j], i + 2)
                        pool.tensor_copy(gidx[j][0:CAP, :], column(i * 2 + (j + 2), 0)).then_inc(gidx_copied, 1)
                        pool.wait_ge(gidx_copied, i * 2 + (j + 3))
                        gather(j)
                    if j == 1:
                        with pool.If(n > i * 2):
                            scatter(i, 0)
                    elif not isinstance(i, int):
                        with pool.If(n > i * 2 - 1):
                            scatter(i - 1, 1)

            two_blocks(0)
            with pool.Fori(1, NBLK // 2) as i:
                two_blocks(i)
            for j, at in ((0, N_EVEN), (1, N_ODD)):
                m = pool.value_load(plan[0:1, at:at + 1], min_val=0, max_val=NBLK // 2)
                pool.wait_ge(moved[j], m * 16 + 16)
                pool.sem_inc(pool_turns, 1)
            pool.sem_inc(scattered, 1)
            pool.wait_ge(ln2_in, 32)
            for i in range(TILES):
                r = rows(i)
                pool.wait_ge(norm_ready, i + 1)
                link(pool.tensor_tensor(yp[i][0:r, 1, :], yp[i][0:r, 1, :], ln2[0:r, 0, :], ALU.mult))
                pool.tensor_tensor(ft[i][0:r, :], yp[i][0:r, 1, :], ln2[0:r, 1, :], ALU.add).then_inc(y_out_ready, 1)

        @block.scalar
        def _(sc):
            steps = [0]

            def link(ins):
                steps[0] += 1
                ins.then_inc(act_step, 1)
                sc.wait_ge(act_step, steps[0])

            b_in = t["b_in"]
            sc.wait_ge(rows_clear, 1)
            packs = [(R_C, 8, t["c_sample"]), (R_C + 8, 1, t["c_prompt"]),
                     (R_CONVST, 24, t["state_conv"][0].rearrange("b w d -> (b w) d")),
                     (R_H0, 8, t["state_rglru"][0]), (R_CONVW, CONV, t["conv_w"][0]), (R_CONVB, 1, t["conv_b"]),
                     (R_BA, 1, t["rg_ba"]), (R_BX, 1, t["rg_bx"]), (R_LAM, 1, t["rg_lambda"]),
                     (R_BIN, 5, b_in[:, 0:5120].rearrange("o (r d) -> (o r) d", d=D)),
                     (R_BIN + 5, 2, b_in[:, 5136:7184].rearrange("o (r d) -> (o r) d", d=D))]
            for r, m, src in packs:
                sc.dma_start(packrows[r:r + m, :], src).then_inc(pack_in, 16)
            for c0, m, src in ((0, 512, t["gla_ba"]), (512, 256, t["gla_norm_g"]), (768, RANK, b_in[:, 5120:5136])):
                sc.dma_start(packrows[R_MISC:R_MISC + 1, c0:c0 + m], src).then_inc(pack_in, 16)
            sc.dma_start(mod_sb[0:1, :], t["b_mod"][0:1, :]).then_inc(bmod_in, 16)
            sc.dma_start(alpha_w[:], t["w_in"][0][:, 5120:5136].rearrange("(k p) n -> p k n", p=P)).then_inc(small_in, 16)
            sc.dma_start(route_w[:, :, 0:NG], t["w_grp"][0].rearrange("(k p) n -> p k n", p=P)).then_inc(small_in, 16)
            sc.dma_start(route_w[:, :, NG:NG + NE], t["w_exp"][0].rearrange("(k p) n -> p k n", p=P)).then_inc(small_in, 16)
            sc.dma_start(route_b[:, 0:NG], t["b_grp"][0:1, :].to_broadcast([P, NG])).then_inc(small_in, 16)
            sc.dma_start(route_b[:, NG:NG + NE], t["b_exp"][0:1, :].to_broadcast([P, NE])).then_inc(small_in, 16)
            sc.dma_start(new_conv_s[0, :, 0:2, :], t["state_conv"][0][:, 1:3, :]).then_inc(s_out, 16)

            await_job(sc, ("pack", 0))
            link(sc.activation(fp[:], slot_banks(("pack", 0))[:, 0, :].rearrange("p (k r) -> p k r", r=64)[:, :, 0:ROWS],
                               ACT.Copy))
            sc.sem_inc(slot_free[0], 1)
            sc.activation(cs[:], fp[:, :, R_C:R_C + 9], ACT.Silu).then_inc(cs_ready, 1)

            def copy_mod(m):
                await_job(sc, ("mod", m))
                for g in range(4):
                    ins = sc.activation(mod_sb[0:9, m * 512 + g * P:m * 512 + (g + 1) * P],
                                        slot_banks(("mod", m))[32 * g:32 * g + 9, 0, 0:P], ACT.Copy)
                    if g < 3:
                        ins.then_inc(mod_ready, 1)
                    else:
                        link(ins)
                sc.sem_inc(mod_ready, 1)
                sc.sem_inc(freed(("mod", m)), 1)

            for i in range(TILES + 1):
                if i < TILES:
                    sc.wait_ge(rstd_q, i + 1)
                    sc.activation(mv[0:rows(i), 2:3], mv[0:rows(i), 1:2], ACT.Sqrt).then_inc(rstd_a, 1)
                if i >= 1:
                    k = i - 1
                    await_job(sc, ("xt", k))
                    v = slot_banks(("xt", k)).rearrange("p h (k n) -> p (h k) n", k=4)[:, :, 0:rows(k)]
                    ins = sc.activation(hT[:, :, k * P:k * P + rows(k)], v, ACT.Copy)
                    ins.then_inc(freed(("xt", k)), 1)
                    if k >= 1:
                        copy_mod(k - 1)
            sc.wait_ge(modT_ready, 1)
            sc.wait_ge(slot_free[INDEX[("xt", 4)] % 3], INDEX[("xt", 4)] // 3 + 1)
            for k in range(0, KD, 2):
                sc.activation(hT[:, k, 0:T], hT[:, k, 0:T], ACT.Identity, bias=modT[:, k, 8:9],
                              scale=modT[:, 8 + k, 8:9]).then_inc(hT_act, 1)
            sc.wait_ge(lam_q, 1)
            link(sc.activation(lam[:, 2, :], lam[:, 1, :], ACT.Exp))
            sc.activation(lam[:, 3, :], lam[:, 2, :], ACT.Ln, bias=1.0).then_inc(lam_a, 1)

            def evacuate(job, out, func, bias, ready, half_view=True):
                await_job(sc, job)
                src = two_halves(job)
                sc.activation(halves(out), src, func, bias=bias).then_inc(freed(job), 1)
                return ready

            def sqrt_step(c):
                sc.wait_ge(th_ready, c + 1)
                sc.activation(rg["sq"][c % 2], rg["th"][c % 2], ACT.Sqrt).then_inc(sqrt_ready, 1)

            for g in range(2):
                for c in range(4 * g, 4 * g + 4):
                    await_job(sc, ("rx", c))
                    link(sc.activation(halves(A[:, c, :]), two_halves(("rx", c)), ACT.Identity,
                                       bias=fp[:, c, R_BIN:R_BIN + 1]))
                    sc.sem_inc(freed(("rx", c)), 1)
                    sc.sem_inc(rx_ready, 1)
                    if c == 4:
                        sqrt_step(3)
                    if ("rx", c) in LATE_MOD:
                        copy_mod(LATE_MOD[("rx", c)])
                for c in range(4 * g, 4 * g + 4):
                    await_job(sc, ("ry", c))
                    link(sc.activation(halves(O[:, c, :]), two_halves(("ry", c)), ACT.Gelu_apprx_tanh,
                                       bias=fp[:, c, R_BIN + 1:R_BIN + 2]))
                    sc.sem_inc(freed(("ry", c)), 1)
                    sc.sem_inc(ry_ready, 1)
                    if c > 4 * g:
                        sqrt_step(c - 1)
                    if c == 0:
                        sc.wait_ge(lam_ready, 1)
                    if c >= 2:
                        sc.wait_ge(ya_ready, c - 1)
                    for name, job, row in (("r", "ra", R_BA), ("i", "ri", R_BX)):
                        await_job(sc, (job, c))
                        link(sc.activation(halves(rg[name][c % 2]), two_halves((job, c)), ACT.Sigmoid,
                                           bias=fp[:, c, row:row + 1]))
                        sc.sem_inc(freed((job, c)), 1)
                    sc.activation(rg["a"][c % 2], rg["r"][c % 2], ACT.Exp, scale=lam[:, 5, c:c + 1]).then_inc(gates_ready, 1)
                    sc.activation(rg["th"][c % 2], rg["r"][c % 2], ACT.Tanh, scale=lam[:, 4, c:c + 1]).then_inc(gates_ready, 1)
                    if ("ry", c) in LATE_MOD:
                        copy_mod(LATE_MOD[("ry", c)])
            sqrt_step(7)

            for c in range(8):
                await_job(sc, ("qk", c))
                sc.activation(halves(Q[:, c, :]), two_halves(("qk", c)), ACT.Identity,
                              bias=fp[:, c, R_BIN + 2:R_BIN + 3]).then_inc(freed(("qk", c)), 1)
            await_job(sc, ("al", 0))
            link(sc.activation(halves(al[0:RANK, :]), two_halves(("al", 0))[0:RANK], ACT.Identity,
                               bias=fp[0:RANK, 6, R_MISC:R_MISC + 1]))
            sc.sem_inc(freed(("al", 0)), 1)
            sc.sem_inc(al_ready, 1)
            sc.wait_ge(ya_ready, KD)
            for c in range(HEADS):
                await_job(sc, ("la", c))
                sc.activation(halves(L[:, c, :]), two_halves(("la", c)), ACT.Identity,
                              bias=fp[:, c, R_MISC:R_MISC + 1]).then_inc(freed(("la", c)), 1)
            sc.wait_ge(nabs_ready, 1)
            link(sc.activation(EX[:], EX[:], ACT.Exp))
            sc.activation(EX[:], EX[:], ACT.Ln, bias=1.0).then_inc(log_ready, 1)
            sc.wait_ge(bcum_ready, 1)
            sc.activation(L[:], EX[:], ACT.Exp, scale=1.0 / TAU).then_inc(e1_ready, 1)
            sc.activation(K2[:], EX[:], ACT.Exp, scale=-1.0 / TAU).then_inc(e1_ready, 1)
            sc.wait_ge(dexp_q, 1)
            sc.activation(EX[:, :, 0:T], EX[:, :, 0:T], ACT.Exp, scale=1.0 / TAU).then_inc(e2_ready, 1)

            sc.wait_ge(gla_in_ready, 1)
            for c in range(8):
                await_job(sc, ("v", c))
                if c >= 2:
                    await_job(sc, ("vt", c - 2))
                link(sc.activation(halves(vf[c % 2]), two_halves(("v", c)), ACT.Identity,
                                   bias=fp[:, c, R_BIN + 3:R_BIN + 4]))
                sc.sem_inc(freed(("v", c)), 1)
                sc.sem_inc(vf_ready, 1)
            for i in range(4):
                await_job(sc, ("kt", i))
                ins = sc.activation(kout_tok[:, i, :], slot_banks(("kt", i))[:, 0, :], ACT.Copy)
                ins.then_inc(freed(("kt", i)), 1)
            sc.sem_inc(kt_ready, 1)
            for n in range(NCH):
                await_job(sc, ("os", n))
                sc.activation(O[:, :, T + n:T + n + 1], slot_banks(("os", n))[:, 0, 0:8].unsqueeze(2), ACT.Copy)\
                  .then_inc(freed(("os", n)), 1)
                sc.wait_ge(o_done, n + 1)
                sc.activation(O[:, :, n * CH:(n + 1) * CH], ps[:, 7, :].rearrange("p (a b) -> p a b", b=CH), ACT.Copy)\
                  .then_inc(o_copied, 1)
            def square(h):
                if h >= 2:
                    await_job(sc, ("ss", h - 2))
                sc.activation(sq[h % 2], O[:, 2 * h:2 * h + 2, :], ACT.Square).then_inc(sq_ready, 1)

            def root(h):
                sc.wait_ge(var_ready, h + 1)
                sc.activation(rms[h % 2], rms[h % 2], ACT.Sqrt).then_inc(rms_ready, 1)

            def gate(c):
                await_job(sc, ("gg", c))
                if c >= 2:
                    sc.wait_ge(yb_ready, c - 1)
                link(sc.activation(halves(gt[c % 2]), two_halves(("gg", c)), ACT.Silu,
                                   bias=fp[:, c, R_BIN + 4:R_BIN + 5]))
                sc.sem_inc(freed(("gg", c)), 1)
                sc.sem_inc(gt_ready, 1)

            sc.wait_ge(o_copied, NCH)
            sc.wait_ge(freed(("os", 7)), INDEX[("os", 7)] // 3 + 1)
            for j in range(2):
                sc.wait_ge(st_out[j], 16 * (NS // 2))
            square(0)
            square(1)
            root(0)
            gate(0)
            square(2)
            root(1)
            gate(1)
            square(3)
            root(2)
            gate(2)
            root(3)
            for c in range(3, 8):
                gate(c)
            sc.wait_ge(yb_ready, KD)
            sc.wait_ge(s_out, 32)
            for job, dst, row in (("ga", Z, 5), ("gb", Q, 6)):
                for c in range(KD):
                    await_job(sc, (job, c))
                    link(sc.activation(halves(dst[:, c, :]), two_halves((job, c)), ACT.Sigmoid,
                                       bias=fp[:, c, R_BIN + row:R_BIN + row + 1]))
                    sc.sem_inc(freed((job, c)), 1)
                    sc.sem_inc(sig_ready, 1)
            for k, (job, m) in enumerate((("rlT", 11), ("hlT", 9))):
                await_job(sc, (job, 0))
                if k == 0:
                    sc.wait_ge(table_clear, 16)
                link(sc.activation(outrow[0:m, k, :].rearrange("p (h n) -> p h n", h=2), slot_banks((job, 0))[0:m], ACT.Copy))
                sc.sem_inc(freed((job, 0)), 1)
                sc.sem_inc(outs_ready, 1)
            sc.wait_ge(z_ready, KD)
            for v, name in enumerate(("ln1_g", "ln1_b")):
                sc.dma_start(lnp[:, v, :], t[name][0:1, :].to_broadcast([P, D])).then_inc(lnp_in, 16)
            for p, i in enumerate(ORDER):
                for k in range(2):
                    sc.wait_ge(rstd_q, TILES + 2 * p + k + 1)
                    sc.activation(mv[0:rows(i), 2:3], mv[0:rows(i), 1:2], ACT.Sqrt).then_inc(rstd_a, 1)
                await_job(sc, ("ht", i))
                if p >= 2:
                    await_job(sc, ("lg", ORDER[p - 2]))
                v = slot_banks(("ht", i)).rearrange("p h (k n) -> p (h k) n", k=4)[:, :, 0:rows(i)]
                link(sc.activation(hfT[p % 2][:, :, 0:rows(i)], v, ACT.Copy))
                sc.sem_inc(freed(("ht", i)), 1)
                sc.sem_inc(hfT_ready, 1)
            sc.wait_ge(ge_q, 1)
            sc.activation(g_e[:], g_e[:], ACT.Exp).then_inc(ge_a, 1)
            sc.wait_ge(ge_q, 2)
            sc.activation(g_m[:, 6, :], g_m[:, 5, :], ACT.Exp).then_inc(ge_a, 1)

            sc.wait_ge(blocks_ready, 1)
            sc.wait_ge(started, 1)
            sc.wait_ge(xt_done[0], 2)
            sc.activation(xT[0], ps[:, 0, :].rearrange("p (k n) -> p k n", k=KD), ACT.Copy).then_inc(xT_ready[0], 1)
            n = sc.value_load(plan[0:1, N_BLK:N_BLK + 1], min_val=0, max_val=NBLK)
            with sc.Fori(0, NBLK // 2) as i:
                for j in range(2):
                    with sc.If(n > i * 2 + j):
                        sc.wait_ge(gu_done, i * 2 + (j + 3))
                        sc.wait_ge(act_ready[j], i + 1)
                        sc.activation(sg[j][CAP:2 * CAP, :], ps[0:CAP, 2 + j, :], ACT.Silu).then_inc(sg_ready[j], 1)
                        sc.wait_ge(xt_done[1 - j], i + (2 + j))
                        sc.wait_ge(gu_done, i * 2 + (j + 2))
                        sc.activation(xT[1 - j], ps[:, 1 - j, :].rearrange("p (k n) -> p k n", k=KD), ACT.Copy)\
                          .then_inc(xT_ready[1 - j], 1)
                        sc.wait_ge(tr_done[j], i + 2)
                        sc.wait_ge(dn_done, i * 2 + (j + 1))
                        sc.activation(acT[j], ps[:, 6 + j, 0:4 * CAP].rearrange("p (k n) -> p k n", k=4), ACT.Copy)\
                          .then_inc(acT_ready[j], 1)
            def weigh(i):
                r = rows(i)
                sc.wait_ge(yp_in[i], 16)
                sc.activation(yp[i][0:r, 0, :], yp[i][0:r, 0, :], ACT.Copy, scale=wpair[0:r, i, 0:1]).then_inc(yw_ready, 1)

            weigh(0)
            for i in range(TILES):
                r = rows(i)
                if i + 1 < TILES:
                    weigh(i + 1)
                sc.wait_ge(fin_q, 2 * i + 1)
                sc.activation(fmv[0:r, i, 2:3], fmv[0:r, i, 1:2], ACT.Sqrt).then_inc(fin_a, 1)
                sc.wait_ge(fin_q, 2 * i + 2)
                sc.activation(yp[i][0:r, 1, :], yp[i][0:r, 0, :], ACT.Identity, bias=fmv[0:r, i, 2:3],
                              scale=fmv[0:r, i, 3:4]).then_inc(norm_ready, 1)

        @block.vector
        def _(v):
            steps = [0]

            def link(ins):
                steps[0] += 1
                ins.then_inc(dve_step, 1)
                v.wait_ge(dve_step, steps[0])

            roots = [0]

            def layer_stats(x, r, ask, answer):
                link(v.bn_stats(stats[0:r, 0, :], x[:, 0:512]))
                link(v.bn_stats(stats[0:r, 1, :], x[:, 512:1024]))
                link(v.bn_aggr(mv[0:r, 0:2], stats[0:r].rearrange("p a b -> p (a b)")))
                v.tensor_scalar_add(mv[0:r, 1:2], mv[0:r, 1:2], LN_EPS).then_inc(ask, 1)
                roots[0] += 1
                v.wait_ge(answer, roots[0])
                link(v.reciprocal(mv[0:r, 3:4], mv[0:r, 2:3]))

            def normalise(out, x, r):
                return v.tensor_scalar(out, x, mv[0:r, 0:1], mv[0:r, 3:4], ALU.subtract, ALU.mult)

            v.wait_ge(x_in, 32)
            for i in range(TILES):
                r = rows(i)
                layer_stats(x_tok[0:r, i, :], r, rstd_q, rstd_a)
                if i >= 2:
                    await_job(v, ("xt", i - 2))
                link(normalise(xn[i % 2][0:r, :], x_tok[0:r, i, :], r))
                v.sem_inc(xn_ready, 1)
            await_job(v, ("modT", 0))
            mt = slot_banks(("modT", 0))[:, 0, 0:144].rearrange("p (a b) -> p a b", b=9)
            link(v.tensor_copy(modT[:, 0:8, :], mt[:, 0:8, :]))
            link(v.tensor_scalar_add(modT[:, 8:16, :], mt[:, 8:16, :], 1.0))
            v.sem_inc(freed(("modT", 0)), 1)
            v.sem_inc(modT_ready, 1)
            v.wait_ge(slot_free[INDEX[("xt", 4)] % 3], INDEX[("xt", 4)] // 3 + 1)
            hs = hT[:, :, T:NT]
            link(v.tensor_tensor(hs, hs, modT[:, 8:16, 0:8], ALU.mult))
            v.tensor_tensor(hs, hs, modT[:, 0:8, 0:8], ALU.add).then_inc(hT_dve, 1)
            for k in range(1, KD, 2):
                v.tensor_scalar(hT[:, k, 0:T], hT[:, k, 0:T], modT[:, 8 + k, 8:9], modT[:, k, 8:9], ALU.mult, ALU.add)\
                 .then_inc(hT_dve, 1)
            lm = fp[:, :, R_LAM]
            link(v.tensor_scalar(lam[:, 0, :], lm, -1.0, 0.0, ALU.mult, ALU.max))
            v.scalar_tensor_tensor(lam[:, 1, :], lm, -1.0, lm, ALU.mult, ALU.min).then_inc(lam_q, 1)
            v.wait_ge(lam_a, 1)
            link(v.tensor_tensor(lam[:, 3, :], lam[:, 3, :], lam[:, 0, :], ALU.add))
            link(v.tensor_scalar_mul(lam[:, 4, :], lam[:, 3, :], 8.0))
            v.tensor_scalar_mul(lam[:, 5, :], lam[:, 3, :], -8.0).then_inc(lam_ready, 1)

            def conv(c):
                v.wait_ge(rx_ready, c + 1)
                if c >= 2:
                    await_job(v, ("ri", c - 2))
                xc = rg["xc"][c % 2]
                w = [fp[:, c, R_CONVW + k:R_CONVW + k + 1] for k in range(CONV)]
                link(v.tensor_copy(rl[:, c, :], A[:, c, 509:520]))
                link(v.tensor_scalar(xc[:], A[:, c, :], w[3], fp[:, c, R_CONVB:R_CONVB + 1], ALU.mult, ALU.add))
                for k in range(1, CONV):
                    link(v.scalar_tensor_tensor(xc[:, k:T], A[:, c, 0:T - k], w[3 - k], xc[:, k:T], ALU.mult, ALU.add))
                for k in range(3):
                    s = fp[:, c, R_CONVST + k:R_CONVST + 24:3]
                    link(v.scalar_tensor_tensor(xc[:, T:NT], s, w[k], xc[:, T:NT], ALU.mult, ALU.add))
                v.sem_inc(xc_ready, 1)

            def recur(c):
                j = c % 2
                a, th, u, h = rg["a"][j], rg["th"][j], rg["i"][j], rg["r"][j]
                v.wait_ge(gates_ready, 2 * c + 2)
                link(v.tensor_tensor(u[:], u[:], rg["xc"][j][:], ALU.mult))
                link(v.tensor_tensor(rg["sq"][j][:], a[:], a[:], ALU.mult))
                link(v.scalar_tensor_tensor(th[:], rg["sq"][j][:], 1.0, th[:], ALU.add, ALU.mult))
                v.sem_inc(th_ready, 1)
                v.wait_ge(sqrt_ready, c + 1)
                link(v.tensor_tensor(u[:], u[:], rg["sq"][j][:], ALU.mult))
                link(v.tensor_tensor(tmp8[:, 0, :], a[:, T:NT], fp[:, c, R_H0:R_H0 + 8], ALU.mult))
                link(v.tensor_tensor_scan(h[:, 0:T], a[:, 0:T], u[:, 0:T], 0.0, ALU.mult, ALU.add))
                link(v.tensor_tensor(h[:, T:NT], u[:, T:NT], tmp8[:, 0, :], ALU.add))
                link(v.tensor_copy(hl[:, c, :], h[:, T - 1:NT]))
                v.wait_ge(ry_ready, c + 1)
                link(v.tensor_tensor(A[:, c, :], h[:], O[:, c, :], ALU.mult))
                v.sem_inc(ya_ready, 1)

            for c in range(KD):
                conv(c)
                if c:
                    recur(c - 1)
            recur(KD - 1)

            v.wait_ge(freed(("la", 3)), INDEX[("la", 3)] // 3 + 1)
            v.wait_ge(freed(("la", 2)), INDEX[("la", 2)] // 3 + 1)
            v.wait_ge(freed(("la", 1)), INDEX[("la", 1)] // 3 + 1)
            link(v.scalar_tensor_tensor(EX[:], L[:], -1.0, L[:], ALU.mult, ALU.min))
            v.sem_inc(nabs_ready, 1)
            v.wait_ge(log_ready, 1)
            link(v.scalar_tensor_tensor(L[:], L[:], 0.0, EX[:], ALU.min, ALU.subtract))
            v.wait_ge(consts, 2)
            for h in range(HEADS):
                link(v.tensor_tensor_scan(EX[:, h, :], scan_mask[:], L[:, h, :], 0.0, ALU.mult, ALU.add))
            v.sem_inc(bcum_ready, 1)
            v.tensor_copy(bt[:], EX[:, :, CH - 1:T:CH])
            v.wait_ge(e1_ready, 2)
            link(v.tensor_copy(ela[:], L[:, :, T:NT]))
            link(v.tensor_copy(dec[:], L[:, :, CH - 1:T:CH]))
            for h in range(HEADS):
                e = EX[:, h, 0:T].rearrange("p (n c) -> p n c", c=CH)
                link(v.tensor_tensor(e, bt[:, h, :].unsqueeze(2).to_broadcast([P, NCH, CH]), e, ALU.subtract))
            v.sem_inc(dexp_q, 1)
            link(v.tensor_scalar_mul(qs[:], Q[:, 0:HEADS, T:NT], DKH ** -0.5))
            link(v.scalar_tensor_tensor(Q[:, 0:HEADS, 0:T], Q[:, 0:HEADS, 0:T], DKH ** -0.5, L[:, :, 0:T],
                                        ALU.mult, ALU.mult))
            v.wait_ge(e2_ready, 1)
            link(v.tensor_tensor(EX[:, :, 0:T], EX[:, :, 0:T], Q[:, HEADS:8, 0:T], ALU.mult))
            link(v.tensor_tensor(Q[:, HEADS:8, 0:T], Q[:, HEADS:8, 0:T], K2[:, :, 0:T], ALU.mult))
            v.sem_inc(gla_in_ready, 1)
            for c in range(8):
                await_job(v, ("vt", c))
                b = slot_banks(("vt", c))
                link(v.tensor_copy(v_tok[:, :, c * P:(c + 1) * P], b[:, 0, :].rearrange("p (i n) -> p i n", i=4)))
                link(v.tensor_copy(v_samp[0:NS, c * P:(c + 1) * P], b[0:NS, 1, 0:P]))
                v.sem_inc(freed(("vt", c)), 1)
                v.sem_inc(vt_ready, 1)
            for n in range(NCH):
                q = 64 * (n % 2)
                v.wait_ge(at_done, n + 1)
                if n >= 2:
                    v.wait_ge(o_done, n - 1)
                if n == 0:
                    v.wait_ge(kt_ready, 1)
                link(v.tensor_tensor(attm[n % 2][q:q + 64], ps[q:q + 64, 6, 0:256].rearrange("p (h i) -> p h i", h=HEADS),
                                     maskT[q:q + 64, :].unsqueeze(1).to_broadcast([64, HEADS, CH]), ALU.mult))
                v.sem_inc(attm_ready, 1)
                await_job(v, ("ds", n))
                if n >= 1:
                    v.wait_ge(o_done, n)
                ds = slot_banks(("ds", n)).rearrange("p b (h w) -> p (b h) w", w=DVH)
                new = S[(n + 1) % 2]
                for h in range(HEADS):
                    if n == 0:
                        link(v.tensor_copy(new[:, h, :], ds[:, h, :]))
                    else:
                        link(v.scalar_tensor_tensor(new[:, h, :], S[n % 2][:, h, :], dec[:, h, n:n + 1], ds[:, h, :],
                                                    ALU.mult, ALU.add))
                v.sem_inc(freed(("ds", n)), 1)
                v.sem_inc(s_ready, 1)
                v.wait_ge(st_in[n % 2], 16 * (n // 2 + 1))
                for h in range(HEADS):
                    link(v.tensor_scalar_mul(st[n % 2][:, h, :], st[n % 2][:, h, :], ela[:, h, n:n + 1]))
                await_job(v, ("vb", n))
                vb = slot_banks(("vb", n)).rearrange("p b (h w) -> p (b h) w", w=DVH)
                for h in range(HEADS):
                    link(v.scalar_tensor_tensor(st[n % 2][:, h, :], vb[:, h, :], Q[:, HEADS + h, T + n:T + n + 1],
                                                st[n % 2][:, h, :], ALU.mult, ALU.add))
                v.sem_inc(freed(("vb", n)), 1)
                v.sem_inc(st_ready, 1)

            def variance(h):
                await_job(v, ("ss", h))
                link(v.tensor_scalar(halves(rms[h % 2]), two_halves(("ss", h)), 1.0 / DVH, RMS_EPS, ALU.mult, ALU.add))
                v.sem_inc(freed(("ss", h)), 1)
                v.sem_inc(var_ready, 1)

            def rescale(h):
                v.wait_ge(rms_ready, h + 1)
                link(v.reciprocal(rms[h % 2][:], rms[h % 2][:]))
                for d in range(2):
                    link(v.scalar_tensor_tensor(O[:, 2 * h + d, :], O[:, 2 * h + d, :], fp[:, 4 + d, R_MISC:R_MISC + 1],
                                                rms[h % 2][:], ALU.mult, ALU.mult))

            def gate(c):
                v.wait_ge(gt_ready, c + 1)
                link(v.tensor_tensor(O[:, c, :], O[:, c, :], gt[c % 2][:], ALU.mult))
                v.sem_inc(yb_ready, 1)

            variance(0)
            variance(1)
            rescale(0)
            gate(0)
            variance(2)
            rescale(1)
            gate(1)
            variance(3)
            rescale(2)
            gate(2)
            rescale(3)
            for c in range(3, 8):
                gate(c)
            for c in range(KD):
                v.wait_ge(sig_ready, c + 1)
                await_job(v, ("pa", c))
                link(v.tensor_tensor(halves(Z[:, c, :]), halves(Z[:, c, :]), two_halves(("pa", c)), ALU.mult))
                v.sem_inc(freed(("pa", c)), 1)
            for c in range(KD):
                v.wait_ge(sig_ready, KD + c + 1)
                await_job(v, ("pb", c))
                link(v.tensor_tensor(halves(Q[:, c, :]), halves(Q[:, c, :]), two_halves(("pb", c)), ALU.mult))
                v.sem_inc(freed(("pb", c)), 1)
                link(v.tensor_tensor(Z[:, c, :], Z[:, c, :], Q[:, c, :], ALU.add))
                v.sem_inc(z_ready, 1)
            for k in range(4):
                await_job(v, ("bc", k))
                out = bc[:, k, :].rearrange("p (h n) -> p h n", h=2)
                link(v.tensor_scalar_add(out, slot_banks(("bc", k)), 1.0 if k == 2 else 0.0))
                v.sem_inc(freed(("bc", k)), 1)
            link(v.tensor_scalar_add(mod_sb[0:NS, 4 * D:5 * D], mod_sb[0:NS, 4 * D:5 * D], 1.0))

            def modvec(k, i):
                return bc[:, k, :] if i < 4 else mod_sb[0:NS, (2 + k) * D:(3 + k) * D]

            def add_route_bias(i):
                r = rows(i)
                await_job(v, ("lg", i))
                if i == 4:
                    v.wait_ge(iotas, 1)
                link(v.tensor_tensor(LG[0:r, i, :], slot_banks(("lg", i))[0:r, 0, 0:NG + NE], route_b[0:r, :], ALU.add))
                v.sem_inc(freed(("lg", i)), 1)

            v.wait_ge(lnp_in, 32)
            for p, i in enumerate(ORDER):
                r = rows(i)
                await_job(v, ("wo", i))
                u = lt[0:r, :]
                uh = u.rearrange("p (h n) -> p h n", h=2)
                x = x_tok[0:r, i, :]
                link(v.tensor_tensor(uh, slot_banks(("wo", i))[0:r], modvec(0, i).rearrange("p (h n) -> p h n", h=2), ALU.mult))
                v.sem_inc(freed(("wo", i)), 1)
                link(v.scalar_tensor_tensor(u, x, ALPHA, u, ALU.mult, ALU.add))
                layer_stats(u, r, rstd_q, rstd_a)
                link(normalise(u, u, r))
                link(v.tensor_tensor(u, u, lnp[0:r, 0, :], ALU.mult))
                link(v.tensor_tensor(x, u, lnp[0:r, 1, :], ALU.add))
                layer_stats(x, r, rstd_q, rstd_a)
                if p >= 2:
                    v.wait_ge(hf_out[p % 2], 16 * (p // 2))
                    await_job(v, ("ht", ORDER[p - 2]))
                h = hf[p % 2][0:r, :]
                link(normalise(h, x, r))
                link(v.tensor_tensor(h, h, modvec(2, i), ALU.mult))
                link(v.tensor_tensor(h, h, modvec(1, i), ALU.add))
                v.sem_inc(hf_ready, 1)
                if p >= 1:
                    add_route_bias(ORDER[p - 1])
            add_route_bias(ORDER[4])

            v.wait_ge(iotas, 1)
            GL = LG[:, :, 0:NG]
            EL = LG[:, :, NG:NG + NE].rearrange("p t (g e) -> p t g e", g=NG)
            bro = lambda a, n: a.unsqueeze(2).to_broadcast([P, TILES, n])
            j4b = j4.unsqueeze(1).to_broadcast([P, TILES, NG])
            j32b = j32.unsqueeze(1).to_broadcast([P, TILES, NE])

            def first_of(eq, jb, low, oh, n):
                link(v.tensor_tensor(eq, eq, jb, ALU.mult))
                link(v.tensor_reduce(low, eq, AX, ALU.min))
                link(v.tensor_tensor(oh, jb, bro(low, n), ALU.is_equal))

            link(v.tensor_reduce(g_m[:, 0, :], GL, AX, ALU.max))
            link(v.tensor_tensor(g_e[:], GL, bro(g_m[:, 0, :], NG), ALU.subtract))
            v.sem_inc(ge_q, 1)
            link(v.tensor_tensor(g_eq[:], GL, bro(g_m[:, 0, :], NG), ALU.is_equal))
            link(v.tensor_tensor(g_eq[:], g_eq[:], j4b, ALU.mult))
            link(v.tensor_reduce(g_m[:, 1, :], g_eq[:], AX, ALU.min))
            link(v.tensor_tensor(g_eq[:], j4b, bro(g_m[:, 1, :], NG), ALU.is_equal))
            v.wait_ge(ge_a, 1)
            link(v.tensor_reduce(g_m[:, 2, :], g_e[:], AX, ALU.add))
            link(v.reciprocal(g_m[:, 2, :], g_m[:, 2, :]))
            mlg = ml.rearrange("p t (g e) -> p t g e", g=NG)
            for i in range(TILES):
                gb = g_eq[:, i, :].unsqueeze(2).to_broadcast([P, NG, EPG])
                link(v.tensor_tensor(mlg[:, i], EL[:, i], gb, ALU.mult))
                link(v.tensor_scalar(e_eq[:, i, :].rearrange("p (g e) -> p g e", g=NG), gb, -1.0, BIG, ALU.add, ALU.mult))
            link(v.tensor_tensor(ml[:], ml[:], e_eq[:], ALU.add))
            for k in range(2):
                link(v.tensor_reduce(g_m[:, 3 + k, :], ml[:], AX, ALU.max))
                link(v.tensor_tensor(e_eq[:], ml[:], bro(g_m[:, 3 + k, :], NE), ALU.is_equal))
                first_of(e_eq[:], j32b, g_m[:, 7, :], OH[:, :, k, :], NE)
                if k == 0:
                    link(v.scalar_tensor_tensor(ml[:], OH[:, :, 0, :], -3.0 * BIG, ml[:], ALU.mult, ALU.add))
            link(v.tensor_tensor(g_m[:, 5, :], g_m[:, 4, :], g_m[:, 3, :], ALU.subtract))
            v.sem_inc(ge_q, 1)
            link(v.tensor_tensor(M[:], OH[:, :, 0, :], OH[:, :, 1, :], ALU.add))
            v.sem_inc(m_ready, 1)
            v.wait_ge(ge_a, 2)
            link(v.tensor_scalar_add(g_m[:, 8, :], g_m[:, 6, :], 1.0))
            link(v.reciprocal(g_m[:, 8, :], g_m[:, 8, :]))
            link(v.tensor_tensor(wpair[:, :, 0], g_m[:, 8, :], g_m[:, 2, :], ALU.mult))
            link(v.tensor_tensor(wpair[:, :, 1], wpair[:, :, 0], g_m[:, 6, :], ALU.mult))
            await_job(v, ("rk", 0))
            rk = slot_banks(("rk", 0))[:, :, 0:TILES * NE].rearrange("p h (t e) -> p h t e", e=NE)
            for i in range(TILES):
                link(v.tensor_tensor(before[:, i + 1, :], before[:, i, :], rk[:, 1, i, :], ALU.add))
            link(v.tensor_tensor(rank[:], rk[:, 0], before[:, 0:TILES, :], ALU.add))
            cb = before[:, TILES, :].unsqueeze(2).to_broadcast([P, NE, SPLITS])
            link(v.tensor_tensor(many[:], cb, m64.unsqueeze(1).to_broadcast([P, NE, SPLITS]), ALU.is_gt))
            link(v.tensor_reduce(cnt[:, 0, :], many[:], AX, ALU.add))
            link(v.tensor_tensor_scan(cnt[:, 1, :], ones[:, 0:NE], cnt[:, 0, :], 0.0, ALU.mult, ALU.add))
            link(v.tensor_tensor(cnt[:, 2, :], cnt[:, 1, :], cnt[:, 0, :], ALU.subtract))
            link(v.tensor_scalar_min(cnt[:, 3, :], cnt[:, 0, :], 1.0))
            link(v.tensor_scalar(cnt[:, 3, 0:2], cnt[:, 0, 0:2], 0.0, 1.0, ALU.mult, ALU.add))
            link(v.tensor_tensor_scan(cnt[:, 4, :], ones[:, 0:NE], cnt[:, 3, :], 0.0, ALU.mult, ALU.add))
            big = area(Z0 + 1024, NBLK, NE)

            def counted(limits, values, weights, n, out):
                b = big[0:1, 0:n, :]
                link(v.tensor_tensor(b, values.unsqueeze(1).to_broadcast([1, n, NE]),
                                     limits.unsqueeze(2).to_broadcast([1, n, NE]), ALU.is_le))
                if weights is not None:
                    link(v.tensor_tensor(b, b, weights.unsqueeze(1).to_broadcast([1, n, NE]), ALU.mult))
                link(v.tensor_reduce(out, b, AX, ALU.add))

            counted(blk_f[0:1, 0:NE], cnt[0:1, 4, :], None, NE, pl_f[0:1, 0:NE])
            link(v.tensor_scalar_min(plan[0:1, LD_EXPERT:LD_EXPERT + NE], pl_f[0:1, 0:NE], float(NE - 1)))
            link(v.tensor_scalar_add(pl_f[0:1, NE:2 * NE], blk_f[0:1, 0:NE], -1.0))
            counted(pl_f[0:1, NE:2 * NE], cnt[0:1, 4, :], cnt[0:1, 0, :], NE, pl_f[0:1, 0:NE])
            link(v.tensor_copy(plan[0:1, LD_AFTER:LD_AFTER + NE], pl_f[0:1, 0:NE]))
            link(v.tensor_copy(plan[0:1, N_BLK:N_BLK + 1], cnt[0:1, 1, NE - 1:NE]))
            link(v.tensor_copy(plan[0:1, N_LD:N_LD + 1], cnt[0:1, 4, NE - 1:NE]))
            v.sem_inc(loads_ready, 1)
            for k in range(2):
                link(v.tensor_tensor(prod[:, :, k, :], OH[:, :, k, :], rank[:], ALU.mult))
            link(v.tensor_reduce(r1[:], prod[:], AX, ALU.add))
            for k in range(2):
                link(v.tensor_tensor(prod[:, :, k, :], OH[:, :, k, :],
                                     cnt[:, 2, :].unsqueeze(1).to_broadcast([P, TILES, NE]), ALU.mult))
            link(v.tensor_reduce(b1[:], prod[:], AX, ALU.add))
            r1f = r1.rearrange("p t k -> p (t k)")
            link(v.tensor_tensor(ge[:], r1f.unsqueeze(2).to_broadcast([P, 2 * TILES, SPLITS - 1]),
                                 m64[:, 1:SPLITS].unsqueeze(1).to_broadcast([P, 2 * TILES, SPLITS - 1]), ALU.is_ge))
            link(v.tensor_reduce(q1.rearrange("p t k -> p (t k)"), ge[:], AX, ALU.add))
            link(v.scalar_tensor_tensor(addr_f[:], r1[:], float(TW), b1[:], ALU.mult, ALU.add))
            link(v.scalar_tensor_tensor(addr_f[:], q1[:], float(1 - CAP * TW), addr_f[:], ALU.mult, ALU.add))
            link(v.tensor_copy(addr_i[:], addr_f[:]))
            v.sem_inc(addr_ready, 1)

            counted(blk_f[0:1, :], cnt[0:1, 1, :], cnt[0:1, 3, :], NBLK, pl_f[0:1, 0:NBLK])
            link(v.tensor_copy(pl_i[0:1, 0:NBLK], pl_f[0:1, 0:NBLK]))
            one = lambda c, x, y, o1, o2: link(v.tensor_scalar(plan[0:1, c:c + NBLK], pl_i[0:1, 0:NBLK], x, y, o1, o2))
            link(v.tensor_single_scalar(pl_i[0:1, NBLK:2 * NBLK], pl_i[0:1, 0:NBLK], 1, ALU.bitwise_and))
            link(v.tensor_scalar_mul(plan[0:1, BLK_SLOT:BLK_SLOT + NBLK], pl_i[0:1, NBLK:2 * NBLK], 3 * WT))
            for at, plus in ((BLK_IN0, 2), (BLK_IN1, 3)):
                link(v.tensor_scalar_add(pl_i[0:1, NBLK:2 * NBLK], pl_i[0:1, 0:NBLK], plus))
                link(v.tensor_single_scalar(plan[0:1, at:at + NBLK], pl_i[0:1, NBLK:2 * NBLK], 1, ALU.logical_shift_right))
            for at, plus in ((N_EVEN, 1), (N_ODD, 0)):
                link(v.tensor_scalar_add(pl_i[0:1, 0:1], plan[0:1, N_BLK:N_BLK + 1], plus))
                link(v.tensor_single_scalar(plan[0:1, at:at + 1], pl_i[0:1, 0:1], 1, ALU.logical_shift_right))
            v.sem_inc(blocks_ready, 1)

            n = v.value_load(plan[0:1, N_BLK:N_BLK + 1], min_val=0, max_val=NBLK)

            def take_result(i, j):
                v.wait_ge(dn_done, i * 2 + (j + 3))
                v.wait_ge(moved[j], i * 16 + 16)
                for q in range(2):
                    v.tensor_copy(yb[j][0:CAP, q * 512:(q + 1) * 512], ps[CAP * q:CAP * q + CAP, 4 + j, :])\
                     .then_inc(y_ready[j], 1)

            def two_blocks(i):
                for j in range(2):
                    with v.If(n > i * 2 + j):
                        v.wait_ge(sg_ready[j], i + 1)
                        v.wait_ge(tr_done[j], i + 1)
                        v.tensor_tensor(act[j][0:CAP, :], sg[j][CAP:2 * CAP, :], ps[CAP:2 * CAP, 2 + j, :], ALU.mult)\
                         .then_inc(act_ready[j], 1)
                    if j == 1:
                        with v.If(n > i * 2):
                            take_result(i, 0)
                    elif not isinstance(i, int):
                        with v.If(n > i * 2 - 1):
                            take_result(i - 1, 1)

            two_blocks(0)
            with v.Fori(1, NBLK // 2) as i:
                two_blocks(i)

            for i in range(TILES):
                r = rows(i)
                x = x_tok[0:r, i, :]
                v.wait_ge(yw_ready, i + 1)
                y0 = yp[i][0:r, 0, :]
                link(v.scalar_tensor_tensor(y0, yp[i][0:r, 1, :], wpair[0:r, i, 1:2], y0, ALU.mult, ALU.add))
                link(v.tensor_tensor(y0, y0, modvec(3, i), ALU.mult))
                link(v.scalar_tensor_tensor(y0, x, ALPHA, y0, ALU.mult, ALU.add))
                link(v.bn_stats(stats[0:r, 0, :], y0[:, 0:512]))
                link(v.bn_stats(stats[0:r, 1, :], y0[:, 512:1024]))
                link(v.bn_aggr(fmv[0:r, i, 0:2], stats[0:r].rearrange("p a b -> p (a b)")))
                link(v.tensor_scalar_add(fmv[0:r, i, 1:2], fmv[0:r, i, 1:2], LN_EPS))
                v.sem_inc(fin_q, 1)
                v.wait_ge(fin_a, i + 1)
                link(v.reciprocal(fmv[0:r, i, 3:4], fmv[0:r, i, 2:3]))
                link(v.scalar_tensor_tensor(fmv[0:r, i, 2:3], fmv[0:r, i, 0:1], -1.0, fmv[0:r, i, 3:4], ALU.mult, ALU.mult))
                v.sem_inc(fin_q, 1)

        @block.tensor
        def _(pe):
            def start(job):
                n = INDEX[job]
                if n >= 3:
                    pe.wait_ge(slot_free[n % 3], n // 3)
                return slot_banks(job)

            def done(ins):
                ins.then_inc(job_done, 1)

            tiles = [0]

            def weight_tile():
                s, _, turn = RING[tiles[0]]
                tiles[0] += 1
                pe.wait_ge(w_in_slot[s], 16 * turn)
                return ring[s]

            def tile_used():
                pe.sem_inc(w_used, 1)

            def project(job, w, col, m, src, k_blocks=KD):
                out = start(job)
                for h in range(2):
                    for k in range(k_blocks):
                        ins = pe.matmul(out[0:m, h, 0:HALF], w[:, k, col:col + m],
                                        src[:, k, h * HALF:(h + 1) * HALF], start=(k == 0), stop=(k == k_blocks - 1))
                done(ins)

            pe.wait_ge(pack_in, 16 * 14)
            pe.wait_ge(consts, 1)
            out = start(("pack", 0))
            for k in range(KD):
                ins = pe.transpose(out[:, 0, k * 64:k * 64 + ROWS], packrows[0:ROWS, k * P:(k + 1) * P], ident[0:ROWS, 0:ROWS])
            done(ins)

            def transpose_x(i):
                out = start(("xt", i))
                pe.wait_ge(xn_ready, i + 1)
                r = rows(i)
                for k in range(KD):
                    ins = pe.transpose(out[:, k // 4, (k % 4) * P:(k % 4) * P + r], xn[i % 2][0:r, k * P:(k + 1) * P],
                                       ident[0:r, 0:r])
                done(ins)

            def modulation(m, w):
                out = start(("mod", m))
                for k in range(KD + 1):
                    for g in range(4):
                        o = out[32 * g:32 * g + 9, 0, 0:P]
                        if k < KD:
                            pe.matmul(o, cs[:, k, :], w[:, k, g * P:(g + 1) * P], start=(k == 0), stop=False)
                        else:
                            ins = pe.matmul(o, ones[0:1, 0:9], mod_sb[0:1, m * 512 + g * P:m * 512 + (g + 1) * P],
                                            start=False, stop=True)
                done(ins)

            def late_modulation(job):
                if job in LATE_MOD:
                    m = LATE_MOD[job]
                    pe.wait_ge(mod_w_in, 16 * (m - EARLY_MOD + 1))
                    modulation(m, mod_w)

            transpose_x(0)
            transpose_x(1)
            pe.wait_ge(cs_ready, 1)
            pe.wait_ge(bmod_in, 16)
            for m in range(EARLY_MOD):
                modulation(m, weight_tile())
                pe.wait_ge(job_done, INDEX[("mod", m)] + 1)
                tile_used()
                if m < 3:
                    transpose_x(m + 2)
            pe.wait_ge(mod_ready, 4 * EARLY_MOD)
            out = start(("modT", 0))
            for c in range(16):
                ins = pe.transpose(out[:, 0, c * 9:c * 9 + 9], mod_sb[0:9, c * P:(c + 1) * P], ident[0:9, 0:9])
            done(ins)
            pe.wait_ge(hT_act, KD // 2)
            pe.wait_ge(hT_dve, 1 + KD // 2)

            def last_of_tile(job):
                pe.wait_ge(job_done, INDEX[job] + 1)
                tile_used()

            for g in range(2):
                w = weight_tile()
                for c in range(4 * g, 4 * g + 4):
                    project(("rx", c), w, (c % 4) * P, P, hT)
                    late_modulation(("rx", c))
                last_of_tile(("rx", 4 * g + 3))
                w = weight_tile()
                for c in range(4 * g, 4 * g + 4):
                    project(("ry", c), w, (c % 4) * P, P, hT)
                    if c == 4 * g + 3:
                        last_of_tile(("ry", c))
                    if c == 0:
                        pe.wait_ge(bd_in, 16 * 5)
                    pe.wait_ge(xc_ready, c + 1)
                    for job, gate in (("ra", bd[0]), ("ri", bd[1])):
                        out = start((job, c))
                        for h in range(2):
                            ins = pe.matmul(out[:, h, 0:HALF], gate[:, c, :], rg["xc"][c % 2][:, h * HALF:(h + 1) * HALF],
                                            start=True, stop=True)
                        done(ins)
                    late_modulation(("ry", c))
            for g in range(2):
                w = weight_tile()
                for c in range(4 * g, 4 * g + 4):
                    project(("qk", c), w, (c % 4) * P, P, hT)
                last_of_tile(("qk", 4 * g + 3))
            pe.wait_ge(small_in, 16 * 5)
            project(("al", 0), alpha_w, 0, RANK, hT)
            pe.wait_ge(al_ready, 1)
            for c in range(HEADS):
                out = start(("la", c))
                for h in range(2):
                    ins = pe.matmul(out[:, h, 0:HALF], wa2[0:RANK, c * P:(c + 1) * P], al[0:RANK, h * HALF:(h + 1) * HALF],
                                    start=True, stop=True)
                done(ins)

            def v_transpose(c):
                pe.wait_ge(vf_ready, c + 1)
                out = start(("vt", c))
                for i in range(4):
                    pe.transpose(out[:, 0, i * P:(i + 1) * P], vf[c % 2][:, i * P:(i + 1) * P], ident[:])
                done(pe.transpose(out[0:NS, 1, 0:P], vf[c % 2][:, T:NT], ident[:]))

            for c in range(8):
                if c % 4 == 0:
                    w = weight_tile()
                project(("v", c), w, (c % 4) * P, P, hT)
                if c % 4 == 3:
                    last_of_tile(("v", c))
                if c:
                    v_transpose(c - 1)
            v_transpose(7)
            pe.wait_ge(gla_in_ready, 1)
            for i in range(4):
                out = start(("kt", i))
                for h in range(HEADS):
                    ins = pe.transpose(out[:, 0, h * P:(h + 1) * P], EX[:, h, i * P:(i + 1) * P], ident[:])
                done(ins)
            pe.wait_ge(vt_ready, 8)
            pe.wait_ge(kt_ready, 1)
            for n in range(NCH):
                q, tile = 64 * (n % 2), n // 2
                cols = slice(n * CH, (n + 1) * CH)
                if n >= 1:
                    pe.wait_ge(attm_ready, n)
                for h in range(HEADS):
                    ins = pe.matmul(ps[q:q + 64, 6, h * CH:(h + 1) * CH], Q[:, HEADS + h, cols], Q[:, h, cols],
                                    start=True, stop=True)
                ins.then_inc(at_done, 1)
                out = start(("ds", n))
                for h in range(HEADS):
                    ins = pe.matmul(out[:, h // 2, (h % 2) * DVH:(h % 2 + 1) * DVH],
                                    kout_tok[q:q + 64, tile, h * P:(h + 1) * P],
                                    v_tok[q:q + 64, tile, h * DVH:(h + 1) * DVH], start=True, stop=True)
                done(ins)
                out = start(("vb", n))
                for h in range(2):
                    ins = pe.matmul(out[:, h, :], ident[0:NS, n:n + 1].to_broadcast([NS, P]), v_samp[0:NS, h * 512:(h + 1) * 512],
                                    start=True, stop=True)
                done(ins)
                pe.wait_ge(attm_ready, n + 1)
                if n >= 1:
                    pe.wait_ge(s_ready, n)
                    pe.wait_ge(o_copied, n)
                for hd in range(8):
                    h, d = hd // 2, hd % 2
                    o = ps[:, 7, hd * CH:(hd + 1) * CH]
                    ins = pe.matmul(o, v_tok[q:q + 64, tile, hd * P:(hd + 1) * P], attm[n % 2][q:q + 64, h, :],
                                    start=True, stop=(n == 0))
                    if n:
                        ins = pe.matmul(o, S[n % 2][:, h, d * P:(d + 1) * P], Q[:, h, cols], start=False, stop=True)
                ins.then_inc(o_done, 1)
                pe.wait_ge(st_ready, n + 1)
                out = start(("os", n))
                for hd in range(8):
                    ins = pe.matmul(out[:, 0, hd:hd + 1], st[n % 2][:, hd // 2, (hd % 2) * P:(hd % 2 + 1) * P],
                                    qs[:, hd // 2, n:n + 1], start=True, stop=True)
                done(ins)

            def squares(h):
                pe.wait_ge(sq_ready, h + 1)
                out = start(("ss", h))
                for half in range(2):
                    for d in range(2):
                        ins = pe.matmul(out[:, half, 0:HALF], ones[:], sq[h % 2][:, d, half * HALF:(half + 1) * HALF],
                                        start=(d == 0), stop=(d == 1))
                done(ins)

            squares(0)
            squares(1)
            for c in range(8):
                if c % 4 == 0:
                    w = weight_tile()
                project(("gg", c), w, (c % 4) * P, P, hT)
                if c % 4 == 3:
                    last_of_tile(("gg", c))
                if c < 2:
                    squares(c + 2)
            for a, b, src, ready in (("ga", "pa", A, ya_ready), ("gb", "pb", O, yb_ready)):
                for g in range(2):
                    w = weight_tile()
                    for c in range(4 * g, 4 * g + 4):
                        project((a, c), w, (c % 4) * P, P, hT)
                    last_of_tile((a, 4 * g + 3))
                    w = weight_tile()
                    pe.wait_ge(ready, KD)
                    for c in range(4 * g, 4 * g + 4):
                        project((b, c), w, (c % 4) * P, P, src)
                    last_of_tile((b, 4 * g + 3))
            pe.wait_ge(mod_ready, 4 * 12)
            for k in range(4):
                out = start(("bc", k))
                for h in range(2):
                    c0 = (2 + k) * D + h * 512
                    ins = pe.matmul(out[:, h, :], sel8[0:9, :], mod_sb[0:9, c0:c0 + 512], start=True, stop=True)
                done(ins)
            for job, src, m in (("rlT", rl, 11), ("hlT", hl, 9)):
                out = start((job, 0))
                for k in range(KD):
                    ins = pe.transpose(out[0:m, k // 4, (k % 4) * P:(k % 4 + 1) * P], src[:, k, :], ident[:])
                done(ins)

            def route(p):
                i = ORDER[p]
                r = rows(i)
                pe.wait_ge(hf_ready, p + 1)
                out = start(("ht", i))
                for k in range(KD):
                    ins = pe.transpose(out[:, k // 4, (k % 4) * P:(k % 4) * P + r], hf[p % 2][0:r, k * P:(k + 1) * P],
                                       ident[0:r, 0:r])
                done(ins)
                pe.wait_ge(hfT_ready, p + 1)
                out = start(("lg", i))
                for k in range(KD):
                    ins = pe.matmul(out[0:r, 0, 0:NG + NE], hfT[p % 2][:, k, 0:r], route_w[:, k, :],
                                    start=(k == 0), stop=(k == KD - 1))
                done(ins)

            pe.wait_ge(z_ready, KD)
            wo = [weight_tile(), weight_tile()]
            for p, i in enumerate(ORDER):
                r = rows(i)
                out = start(("wo", i))
                for h in range(2):
                    for k in range(KD):
                        ins = pe.matmul(out[0:r, h, :], Z[:, k, i * P:i * P + r], wo[h][:, k, :],
                                        start=(k == 0), stop=(k == KD - 1))
                done(ins)
                if p >= 1:
                    route(p - 1)
            route(4)
            pe.wait_ge(m_ready, 1)
            out = start(("rk", 0))
            for h, w in enumerate((upper, ones)):
                pe.matmul(out[:, h, 0:4 * NE], w[:], M[:, 0:4, :].rearrange("p t e -> p (t e)"), start=True, stop=True)
                ins = pe.matmul(out[:, h, 4 * NE:5 * NE], w[0:NS, :], M[0:NS, 4, :], start=True, stop=True)
            done(ins)

            def transpose_rows(j):
                pe.sem_inc(pe_turns, 1)
                for k in range(KD):
                    ins = pe.transpose(ps[:, j, k * CAP:(k + 1) * CAP],
                                       xg[j][0:CAP, :].rearrange("s (p k) -> s k p", k=KD)[:, k, :], ident[0:CAP, 0:CAP])
                ins.then_inc(xt_done[j], 1)

            def gate_up(j, slot):
                for k in range(KD):
                    for q in range(2):
                        ins = pe.matmul(ps[CAP * q:CAP * q + CAP, 2 + j, :], xT[j][:, k, :], ring[3 * slot + q][:, k, :],
                                        start=(k == 0), stop=(k == KD - 1))
                ins.then_inc(gu_done, 1)

            def down(j, slot):
                wd = ring[3 * slot + 2].rearrange("p k n -> p (k n)").rearrange("p (k n) -> p k n", k=4)
                for k in range(4):
                    for q in range(2):
                        ins = pe.matmul(ps[CAP * q:CAP * q + CAP, 4 + j, :], acT[j][:, k, :],
                                        wd[:, k, q * 512:(q + 1) * 512], start=(k == 0), stop=(k == 3))
                ins.then_inc(dn_done, 1)

            pe.wait_ge(started, 1)
            pe.wait_ge(blocks_ready, 1)
            pe.wait_ge(xg_in[0], 16)
            transpose_rows(0)
            n = pe.value_load(plan[0:1, N_BLK:N_BLK + 1], min_val=0, max_val=NBLK)

            def weights_of(b):
                return (pe.value_load(plan[0:1, bass.ds(b + BLK_SLOT, 1)], min_val=0, max_val=3 * WT),
                        pe.value_load(plan[0:1, bass.ds(b + BLK_IN0, 1)], min_val=1, max_val=NE),
                        pe.value_load(plan[0:1, bass.ds(b + BLK_IN1, 1)], min_val=1, max_val=NE))

            def finish(i, j):
                pe.wait_ge(acT_ready[j], i + 2)
                pe.wait_ge(y_ready[j], i * 2 + 1)
                lies, in0, in1 = weights_of(i * 2 + j)
                pe.wait_ge(we_in[2], in0 * 16)
                pe.wait_ge(we_in[5], in1 * 16)
                for slot in range(2):
                    with pe.If(lies < 1 if slot == 0 else lies > 0):
                        down(j, slot)

            def two_blocks(i):
                for j in range(2):
                    with pe.If(n > i * 2 + j):
                        pe.wait_ge(xT_ready[j], i + 2)
                        pe.wait_ge(act_ready[j], i + 1)
                        lies, in0, in1 = weights_of(i * 2 + j)
                        for m in range(2):
                            pe.wait_ge(we_in[m], in0 * 16)
                            pe.wait_ge(we_in[3 + m], in1 * 16)
                        for slot in range(2):
                            with pe.If(lies < 1 if slot == 0 else lies > 0):
                                gate_up(j, slot)
                        pe.wait_ge(xg_in[1 - j], i * 16 + 16 * (1 + j))
                        pe.wait_ge(xT_ready[1 - j], i + (1 + j))
                        transpose_rows(1 - j)
                    if j == 1:
                        with pe.If(n > i * 2):
                            finish(i, 0)
                    elif not isinstance(i, int):
                        with pe.If(n > i * 2 - 1):
                            finish(i - 1, 1)
                    with pe.If(n > i * 2 + j):
                        pe.wait_ge(act_ready[j], i + 2)
                        pe.wait_ge(acT_ready[j], i + 1)
                        pe.sem_inc(pe_turns, 1)
                        for k in range(4):
                            ins = pe.transpose(ps[:, 6 + j, k * CAP:(k + 1) * CAP],
                                               act[j][0:CAP, :].rearrange("s (p k) -> s k p", k=4)[:, k, :],
                                               ident[0:CAP, 0:CAP])
                        ins.then_inc(tr_done[j], 1)

            two_blocks(0)
            with pe.Fori(1, NBLK // 2) as i:
                two_blocks(i)


_INS = ["x_prompt", "x_sample", "state_conv", "state_rglru", "state_gla", "c_prompt", "c_sample", "w_mod", "b_mod",
        "w_in", "b_in", "conv_w", "conv_b", "rg_wa", "rg_ba", "rg_wx", "rg_bx", "rg_lambda", "gla_wa2", "gla_ba",
        "gla_norm_g", "p_a", "p_b", "w_o", "ln1_g", "ln1_b", "w_grp", "b_grp", "w_exp", "b_exp", "we_gate", "we_up",
        "we_down", "ln2_g", "ln2_b"]
_OUTS = [(1, T, D), (NS, 1, D), (1, 1, CONV - 1, D), (1, 1, D), (1, 1, HEADS, DKH, DVH), (1, NS, CONV - 1, D),
         (1, NS, D), (1, NS, HEADS, DKH, DVH)]


def kernel(**inputs):
    import numpy as np
    import concourse.bacc as bacc
    from concourse.bass_utils import run_bass_kernel_spmd as run

    nc = bacc.Bacc("TRN2", target_bir_lowering=False, num_devices=1)
    arrays, t = {}, {}
    for name in _INS:
        a = np.ascontiguousarray(inputs[name])
        arrays[f"in_{name}"] = a
        t[name] = nc.dram_tensor(f"in_{name}", a.shape, mybir.dt.from_np(a.dtype), kind="ExternalInput").ap()
    outs = [nc.dram_tensor(f"out_{i}", s, F32, kind="ExternalOutput").ap() for i, s in enumerate(_OUTS)]
    build(nc, t, outs)
    r = run(nc, [arrays], core_ids=[0])
    return tuple(r.results[0][f"out_{i}"] for i in range(len(_OUTS)))
```

```python
from contextlib import ExitStack

import concourse.bass as bass
from concourse import mybir

F32 = mybir.dt.float32
I32 = mybir.dt.int32
ACT = mybir.ActivationFunctionType
ALU = mybir.AluOpType
AX = mybir.AxisListType.X

P = 128
D = 1024
KD = D // P
T = 512
NS = 8
NT = T + NS
HALF = NT // 2
TILES = 5
ORDER = (4, 0, 1, 2, 3)
CONV = 4
HEADS = 4
DKH = 128
DVH = 256
CH = 64
NCH = T // CH
RANK = 16
TAU = 16.0
NG = 4
EPG = 8
NE = NG * EPG
DE = 512
CAP = 64
PAIRS = 2 * NT
NBLK = 48
TW = NBLK + 2
SPLITS = 9
OOB = 1 << 20
ALPHA = 2.0 ** 0.25
LN_EPS = 1e-5
RMS_EPS = 1e-6
BIG = 1e30
MAX = 3.4e38
WT = KD * 512

R_C = 0
R_CONVST = 9
R_H0 = 33
R_CONVW = 41
R_CONVB = 45
R_BA = 46
R_BX = 47
R_LAM = 48
R_BIN = 49
R_MISC = 56
ROWS = 57


EARLY_MOD = 4
LATE_MOD = {("rx", 1): 4, ("rx", 3): 5, ("ry", 1): 6, ("ry", 3): 7, ("rx", 5): 8, ("rx", 7): 9, ("ry", 5): 10, ("ry", 7): 11}


def plan_jobs():
    jobs = [("pack", 0), ("xt", 0), ("xt", 1)]
    for m in range(3):
        jobs += [("mod", m), ("xt", m + 2)]
    jobs += [("mod", 3), ("modT", 0)]
    for g in range(2):
        for c in range(4 * g, 4 * g + 4):
            jobs.append(("rx", c))
            if c % 2:
                jobs.append(("mod", LATE_MOD[("rx", c)]))
        for c in range(4 * g, 4 * g + 4):
            jobs += [("ry", c), ("ra", c), ("ri", c)]
            if c % 2:
                jobs.append(("mod", LATE_MOD[("ry", c)]))
    jobs += [("qk", c) for c in range(8)] + [("al", 0)] + [("la", c) for c in range(HEADS)]
    for c in range(8):
        jobs.append(("v", c))
        if c:
            jobs.append(("vt", c - 1))
    jobs.append(("vt", 7))
    jobs += [("kt", i) for i in range(4)]
    for n in range(NCH):
        jobs += [("ds", n), ("gg", n), ("os", n)]
    for c in range(4):
        jobs += [("ga", c), ("ss", c)]
    jobs += [("pa", c) for c in range(4)]
    for a, b, g in (("ga", "pa", 1), ("gb", "pb", 0), ("gb", "pb", 1)):
        jobs += [(a, c) for c in range(4 * g, 4 * g + 4)] + [(b, c) for c in range(4 * g, 4 * g + 4)]
    jobs += [("rlT", 0), ("hlT", 0)]
    for p in range(TILES):
        jobs.append(("wo", ORDER[p]))
        if p >= 1:
            jobs += [("ht", ORDER[p - 1]), ("lg", ORDER[p - 1])]
    jobs += [("ht", ORDER[4]), ("lg", ORDER[4]), ("rk", 0), ("table", 0), ("plan", 0)]
    return jobs


JOBS = plan_jobs()
INDEX = {job: n for n, job in enumerate(JOBS)}
WTILES = ([("w_mod", m * 512) for m in range(EARLY_MOD)]
          + [("w_in", c) for c in (0, 1024, 512, 1536, 2048, 2560, 3072, 3584, 4096, 4608)]
          + [("w_in", 5136), ("p_a", 0), ("w_in", 5136 + 512), ("p_a", 512)]
          + [("w_in", 6160), ("p_b", 0), ("w_in", 6160 + 512), ("p_b", 512)]
          + [("w_o", 0), ("w_o", 512)])
MOD_TILES = EARLY_MOD


def ring_slot(t):
    if t == len(WTILES) - 1:
        return 2
    return t % 3 if t < MOD_TILES else (t + 1) % 2


def ring_plan():
    last, turns, plan = {}, {}, []
    for t in range(len(WTILES)):
        s = ring_slot(t)
        turns[s] = turns.get(s, 0) + 1
        plan.append((s, last.get(s), turns[s]))
        last[s] = t
    return plan


RING = ring_plan()


def build(nc, t, outs):
    (y_prompt, y_sample, new_conv_p, new_rg_p, new_gla_p, new_conv_s, new_rg_s, new_gla_s) = outs
    hf_dram = nc.dram_tensor("hf_scratch", (NT, D), F32, kind="Internal").ap()
    mod_dram = nc.dram_tensor("mod_scratch", (9, 6 * D), F32, kind="Internal").ap()
    vs_dram = nc.dram_tensor("v_scratch", (NS, D), F32, kind="Internal").ap()
    pair_dram = nc.dram_tensor("pair_scratch", (PAIRS, D), F32, kind="Internal").ap()

    with ExitStack() as ctx:
        def sem(name):
            return ctx.enter_context(nc.semaphore(name))

        MEM = 53100
        mem = ctx.enter_context(nc.sbuf_tensor("mem", [P, MEM], F32))
        ps = ctx.enter_context(nc.psum_tensor("ps", [P, 8, 512], F32))

        def area(at, *shape):
            n = 1
            for s in shape:
                n *= s
            v = mem[:, at:at + n]
            if len(shape) == 2:
                v = v.rearrange("p (a b) -> p a b", b=shape[1])
            if len(shape) == 3:
                v = v.rearrange("p (a b c) -> p a b c", b=shape[1], c=shape[2])
            return v

        ring = [area(s * WT, KD, 512) for s in range(6)]
        B = 3 * WT
        hT = area(B, KD, NT)
        O = area(B + 4160, KD, NT)
        TB = B + 8320
        xn = [area(TB + 1024 * j, D) for j in range(2)]
        packrows = area(TB + 2048, D)
        v_tok = area(2 * WT, 4, D)
        bd = [area(2 * WT + 1024 * j, KD, P) for j in range(2)]
        x_tok = area(6 * WT, TILES, D)
        mod_sb = area(6 * WT + 5120, 6 * D)
        G = area(6 * WT + 5120, KD, NT)
        A0 = 6 * WT + 5120 + 6144
        A = area(A0, KD, NT)
        Q = area(A0 + 4160, KD, NT)
        mod_w = area(A0 + 4160, KD, 512)
        Z0 = A0 + 8320
        Z = area(Z0, KD, NT)
        L = area(Z0, HEADS, NT)
        K2 = area(Z0 + 2080, HEADS, NT)
        EX = area(TB, HEADS, NT)
        rg = {n: [area(Z0 + (2 * i + j) * NT, NT) for j in range(2)]
              for i, n in enumerate(("xc", "r", "i", "a"))}
        rg["th"] = [area(TB + j * NT, NT) for j in range(2)]
        rg["sq"] = [area(TB + (2 + j) * NT, NT) for j in range(2)]
        vf = [area(B + 4160 + j * NT, NT) for j in range(2)]
        S = [area(Z0, HEADS, DVH), area(Z0 + 1040, HEADS, DVH)]
        kout_tok = area(Z0 + 2080, 4, 512)
        st = [area(TB + 1024 * j, HEADS, DVH) for j in range(2)]
        vb = area(TB + 2560, HEADS, DVH)
        attm = [area(TB + 2048 + 256 * j, HEADS, CH) for j in range(2)]
        sq = [area(TB + 1040 * j, 2, NT) for j in range(2)]
        rms = [area(TB + 2080 + NT * j, NT) for j in range(2)]
        bc = area(A0, 4, D)
        lnp = area(A0 + 4160, 2, D)
        hf = [area(A0 + 4160 + 2048 + 1024 * j, D) for j in range(2)]
        lt = area(B + WT + 2048, D)
        hfT = [area(B + WT + 1024 * j, KD, P) for j in range(2)]
        xT = [area(Z0 + 512 * j, KD, CAP) for j in range(2)]
        sg = [area(Z0 + 1024 + 512 * j, DE) for j in range(2)]
        act = [area(Z0 + 2048 + 512 * j, DE) for j in range(2)]
        acT = [area(Z0 + 3072 + 256 * j, 4, CAP) for j in range(2)]
        xg = [area(A0 + 4160 + 1024 * j, D) for j in range(2)]
        yb = [area(A0 + 4160 + 2048 + 1024 * j, D) for j in range(2)]
        ln2 = area(A0, 2, D)
        yp = [area(WT + 2048 * i, 2, D) for i in range(TILES)]
        ft = [area(4 * WT + 1024 * j, D) for j in range(TILES)]
        small = [Z0 + 4160]

        def keep(*shape):
            n = 1
            for s in shape:
                n *= s
            v = area(small[0], *shape)
            small[0] += n
            assert small[0] <= MEM, small[0]
            return v

        ident = keep(P)
        ones = keep(P)
        upper = keep(P)
        maskT = keep(CH)
        sel8 = keep(P)
        fp = keep(KD, ROWS)
        cs = keep(KD, 9)
        modT = keep(16, 9)
        alpha_w = keep(KD, RANK)
        route_w = keep(KD, NG + NE)
        route_b = keep(NG + NE)
        lam = keep(6, 8)
        rl = keep(KD, 11)
        hl = keep(KD, 9)
        tmp8 = keep(4, 8)
        qs = keep(HEADS, NS)
        ela = keep(HEADS, NS)
        dec = keep(HEADS, NCH)
        bt = keep(HEADS, NCH)
        stats = keep(2, 6)
        mv = keep(4)
        wpair = keep(TILES, 2)
        fmv = keep(TILES, 4)
        wa2 = area(2 * WT + 2048, 512)
        al = area(2 * WT + 2560, NT)
        scan_mask = area(2 * WT + 3080, NT)
        v_samp = area(2 * WT, D)
        v_samp = keep(D)
        rt = [TB]

        def rtmp(*shape):
            n = 1
            for s in shape:
                n *= s
            v = area(rt[0], *shape)
            rt[0] += n
            assert rt[0] <= TB + 3968
            return v

        LG = rtmp(TILES, NG + NE)
        j4 = rtmp(NG)
        j32 = rtmp(NE)
        m64 = rtmp(SPLITS)
        g_eq = rtmp(TILES, NG)
        g_e = rtmp(TILES, NG)
        g_m = rtmp(12, TILES)
        ml = rtmp(TILES, NE)
        e_eq = rtmp(TILES, NE)
        OH = rtmp(TILES, 2, NE)
        M = rtmp(TILES, NE)
        rank = rtmp(TILES, NE)
        before = rtmp(TILES + 1, NE)
        cnt = rtmp(5, NE)
        hits = rtmp(NE)
        plan_f = rtmp(5)
        plan_i = rtmp(6).bitcast(I32)
        row = rtmp(2)
        place_no = rtmp(CAP)
        place = rtmp(TILES, 2)
        block_no = rtmp(TILES, 2)
        names = rtmp(2, TILES, 2)
        many = rtmp(NE, SPLITS)
        prod = rtmp(TILES, 2, NE)
        r1 = rtmp(TILES, 2)
        b1 = rtmp(TILES, 2)
        q1 = rtmp(TILES, 2)
        ge = rtmp(TILES * 2, SPLITS - 1)
        blk_f = rtmp(NBLK)
        iota_i = rtmp(64)
        plan = area(Z0 + 3720, 5 * NBLK + 4).bitcast(I32)
        BLK_SLOT, BLK_IN0, BLK_IN1, LD_EXPERT, LD_AFTER = (k * NBLK for k in range(5))
        N_BLK, N_LD, N_EVEN, N_ODD = (5 * NBLK + k for k in range(4))
        place_oh = area(Z0 + 1024, 2 * TILES, CAP)
        block_oh = area(Z0 + 1024 + 640, 2 * TILES, NBLK)
        named = area(Z0 + 1024 + 1120, 2 * TILES, NBLK, 2)
        idx = area(Z0 + 3584, TW, 2).bitcast(I32)
        gidx = [area(Z0 + 3700 + j, 1).bitcast(I32) for j in range(2)]
        sidx = [area(Z0 + 3702 + j, 1).bitcast(I32) for j in range(2)]
        outrow = area(6 * WT + 5120, 2, D)

        job_done = sem("job_done")
        slot_free = [sem(f"slot_free{s}") for s in range(3)]
        w_in_slot = [sem(f"w_in_slot{s}") for s in range(3)]
        w_used = sem("w_used")
        rows_clear = sem("rows_clear")
        pack_in = sem("pack_in")
        x_in = sem("x_in")
        bmod_in = sem("bmod_in")
        mod_w_in = sem("mod_w_in")
        mod_ready = sem("mod_ready")
        small_in = sem("small_in")
        bd_in = sem("bd_in")
        consts = sem("consts")
        pool_step = sem("pool_step")
        act_step = sem("act_step")
        dve_step = sem("dve_step")
        xn_ready = sem("xn_ready")
        rstd_q = sem("rstd_q")
        rstd_a = sem("rstd_a")
        cs_ready = sem("cs_ready")
        modT_ready = sem("modT_ready")
        hT_act = sem("hT_act")
        hT_dve = sem("hT_dve")
        lam_q = sem("lam_q")
        lam_a = sem("lam_a")
        lam_ready = sem("lam_ready")
        rx_ready = sem("rx_ready")
        ry_ready = sem("ry_ready")
        xc_ready = sem("xc_ready")
        gates_ready = sem("gates_ready")
        th_ready = sem("th_ready")
        sqrt_ready = sem("sqrt_ready")
        ya_ready = sem("ya_ready")
        al_ready = sem("al_ready")
        nabs_ready = sem("nabs_ready")
        log_ready = sem("log_ready")
        bcum_ready = sem("bcum_ready")
        e1_ready = sem("e1_ready")
        dexp_q = sem("dexp_q")
        e2_ready = sem("e2_ready")
        gla_in_ready = sem("gla_in_ready")
        vf_ready = sem("vf_ready")
        vt_ready = sem("vt_ready")
        kt_ready = sem("kt_ready")
        at_done = sem("at_done")
        attm_ready = sem("attm_ready")
        o_done = sem("o_done")
        o_copied = sem("o_copied")
        s_ready = sem("s_ready")
        st_in = [sem(f"st_in{j}") for j in range(2)]
        st_ready = sem("st_ready")
        vs_out = sem("vs_out")
        vb_in = sem("vb_in")
        st_out = [sem(f"st_out{j}") for j in range(2)]
        sq_ready = sem("sq_ready")
        var_ready = sem("var_ready")
        rms_ready = sem("rms_ready")
        mod_out = sem("mod_out")
        mod_back = sem("mod_back")
        yb_ready = sem("yb_ready")
        sig_ready = sem("sig_ready")
        z_ready = sem("z_ready")
        s_out = sem("s_out")
        mix_ready = sem("mix_ready")
        outs_ready = sem("outs_ready")
        lnp_in = sem("lnp_in")
        hf_ready = sem("hf_ready")
        hf_out = [sem(f"hf_out{j}") for j in range(2)]
        hfT_ready = sem("hfT_ready")
        ge_q = sem("ge_q")
        ge_a = sem("ge_a")
        m_ready = sem("m_ready")
        iotas = sem("iotas")
        plan_ready = sem("plan_ready")
        named_ready = sem("named_ready")
        idx_ready = sem("idx_ready")
        blocks_ready = sem("blocks_ready")
        pair = lambda name: [sem(f"{name}{j}") for j in range(2)]
        we_in = [sem(f"we_in{s}") for s in range(6)]
        gidx_copied = sem("gidx_copied")
        sidx_copied = sem("sidx_copied")
        xg_in = pair("xg_in")
        moved = pair("moved")
        xt_done = pair("xt_done")
        xT_ready = pair("xT_ready")
        gu_done = sem("gu_done")
        sg_ready = pair("sg_ready")
        act_ready = pair("act_ready")
        tr_done = pair("tr_done")
        acT_ready = pair("acT_ready")
        dn_done = sem("dn_done")
        y_ready = pair("y_ready")
        started = sem("started")
        pe_turns = sem("pe_turns")
        pool_turns = sem("pool_turns")
        sp_turns = sem("sp_turns")
        yp_in = [sem(f"yp_in{i}") for i in range(TILES)]
        yw_ready = sem("yw_ready")
        fin_q = sem("fin_q")
        fin_a = sem("fin_a")
        norm_ready = sem("norm_ready")
        y_out_ready = sem("y_out_ready")
        out_sem = sem("out_sem")
        STARTS_AT_ONE = [s for l in (xt_done, xT_ready, act_ready, tr_done, acT_ready, y_ready)
                         for s in l]

        def rows(i):
            return P if i < 4 else NS

        def slot_banks(job):
            s = 2 * (INDEX[job] % 3)
            return ps[:, s:s + 2, :]

        def two_halves(job):
            return slot_banks(job)[:, :, 0:HALF]

        def halves(v):
            return v.rearrange("p (h n) -> p h n", h=2)

        def await_job(eng, job):
            eng.wait_ge(job_done, INDEX[job] + 1)

        def freed(job):
            return slot_free[INDEX[job] % 3]

        block = ctx.enter_context(nc.Block())

        @block.sync
        def _(sp):
            sp.dma_start(x_tok[0:NS, 4, :], t["x_sample"].rearrange("b o d -> (b o) d")).then_inc(x_in, 16)
            sp.dma_start(x_tok[:, 0:4, :], t["x_prompt"][0].rearrange("(i p) d -> p i d", p=P)).then_inc(x_in, 16)

            def load_tile(n):
                name, col = WTILES[n]
                s, before, _ = RING[n]
                if before is not None:
                    sp.wait_ge(w_used, before + 1)
                sp.dma_start(ring[s], t[name][0][:, col:col + 512].rearrange("(k p) n -> p k n", p=P))\
                  .then_inc(w_in_slot[s], 16)

            def load_late_mod(m):
                if m > EARLY_MOD:
                    sp.wait_ge(job_done, INDEX[("mod", m - 1)] + 1)
                sp.dma_start(mod_w[:], t["w_mod"][0][:, m * 512:(m + 1) * 512].rearrange("(k p) n -> p k n", p=P))\
                  .then_inc(mod_w_in, 16)

            sp.wait_ge(pack_in, 16 * 14)
            for n in range(MOD_TILES + 2):
                load_tile(n)
            load_late_mod(EARLY_MOD)
            for n in range(3):
                load_late_mod(EARLY_MOD + 1 + 2 * n)
                load_tile(MOD_TILES + 2 + n)
                load_late_mod(EARLY_MOD + 2 + 2 * n)
            load_late_mod(11)
            for n in range(MOD_TILES + 5, MOD_TILES + 8):
                load_tile(n)

            def load_state(b):
                if b >= 2:
                    sp.wait_ge(st_out[b % 2], 16 * (b // 2))
                    sp.wait_ge(job_done, INDEX[("os", b - 2)] + 1)
                else:
                    sp.wait_ge(job_done, INDEX[("kt", 3)] + 1)
                    sp.wait_ge(kt_ready, 1)
                sp.dma_start(st[b % 2], t["state_gla"][0, b].rearrange("h k v -> k h v")).then_inc(st_in[b % 2], 16)

            sp.wait_ge(mod_ready, 4 * 12)
            sp.dma_start(mod_dram, mod_sb[0:9, :]).then_inc(mod_out, 16)
            load_tile(MOD_TILES + 8)
            load_tile(MOD_TILES + 9)
            load_state(0)
            load_state(1)
            sp.wait_ge(vt_ready, 8)
            sp.dma_start(vs_dram, v_samp[0:NS, :]).then_inc(vs_out, 16)
            sp.wait_ge(vs_out, 16)

            def load_v(b):
                sp.dma_start(vb.rearrange("p h w -> p (h w)"), vs_dram[b:b + 1, :].to_broadcast([P, D])).then_inc(vb_in, 16)

            load_v(0)
            for b in range(NS):
                sp.wait_ge(st_ready, b + 1)
                if b + 1 < NS:
                    load_v(b + 1)
                sp.dma_start(new_gla_s[0, b].rearrange("h k v -> k h v"), st[b % 2]).then_inc(st_out[b % 2], 16)
                if b + 2 < NS:
                    load_state(b + 2)
                if b == 4:
                    load_tile(MOD_TILES + 10)
            sp.wait_ge(s_ready, NCH)
            sp.dma_start(new_gla_p[0, 0].rearrange("h k v -> k h v"), S[NCH % 2]).then_inc(s_out, 16)
            load_tile(MOD_TILES + 11)
            load_tile(MOD_TILES + 12)
            load_tile(MOD_TILES + 13)
            sp.wait_ge(yb_ready, KD)
            sp.wait_ge(mod_out, 16)
            sp.dma_start(mod_sb[0:NS, 2 * D:6 * D], mod_dram[0:NS, 2 * D:6 * D]).then_inc(mod_back, 16)
            load_tile(MOD_TILES + 14)
            sp.wait_ge(job_done, INDEX[("pa", 7)] + 1)
            sp.dma_start(bc.rearrange("p v d -> p (v d)"), mod_dram[8:9, 2 * D:6 * D].to_broadcast([P, 4 * D]))\
              .then_inc(mod_back, 16)
            sp.wait_ge(o_done, NCH)
            load_tile(len(WTILES) - 1)
            for n in range(MOD_TILES + 15, len(WTILES) - 1):
                load_tile(n)
            sp.wait_ge(outs_ready, 1)
            sp.dma_start(new_conv_p[0, 0], outrow[0:3, 0, :]).then_inc(out_sem, 16)
            sp.dma_start(new_conv_s[0, :, 2, :], outrow[3:11, 0, :]).then_inc(out_sem, 16)
            sp.wait_ge(outs_ready, 2)
            sp.dma_start(new_rg_p[0], outrow[0:1, 1, :]).then_inc(out_sem, 16)
            sp.dma_start(new_rg_s[0], outrow[1:9, 1, :]).then_inc(out_sem, 16)
            for m in range(3):
                sp.sem_inc(we_in[3 + m], 16)

            def load_expert(slot, m, e):
                w = t[("we_gate", "we_up", "we_down")[m]][0, bass.ds(e, 1) if not isinstance(e, int) else slice(e, e + 1)]
                to = ring[3 * slot + m]
                if m < 2:
                    sp.dma_start(to, w.rearrange("o (p k) n -> p (o k) n", p=P)).then_inc(we_in[3 * slot + m], 16)
                else:
                    sp.dma_start(to.rearrange("p k n -> p (k n)"), w.rearrange("o (p k) n -> p (o k n)", p=P))\
                      .then_inc(we_in[3 * slot + m], 16)

            def store_hf(p):
                i = ORDER[p]
                sp.wait_ge(hf_ready, p + 1)
                sp.dma_start(hf_dram[i * P:i * P + rows(i), :], hf[p % 2][0:rows(i), :]).then_inc(hf_out[p % 2], 16)

            for p in range(4):
                store_hf(p)
            sp.wait_ge(job_done, INDEX[("wo", ORDER[4])] + 1)
            load_expert(0, 0, 0)
            load_expert(0, 1, 0)
            load_expert(0, 2, 0)
            load_expert(1, 0, 1)
            store_hf(4)
            sp.wait_ge(job_done, INDEX[("lg", ORDER[4])] + 1)
            load_expert(1, 1, 1)
            sp.wait_ge(blocks_ready, 1)
            for j in range(2):
                sp.wait_ge(xg_in[j], 16)
            load_expert(1, 2, 1)
            sp.wait_ge(started, 1)
            n = sp.value_load(plan[0:1, N_LD:N_LD + 1], min_val=0, max_val=NE)
            with sp.Fori(1, NE // 2) as i:
                for j in range(2):
                    with sp.If(n > i * 2 + j):
                        e = sp.value_load(plan[0:1, bass.ds(i * 2 + (j + LD_EXPERT), 1)], min_val=0, max_val=NE - 1)
                        after = sp.value_load(plan[0:1, bass.ds(i * 2 + (j + LD_AFTER), 1)], min_val=0, max_val=NBLK)
                        for m in range(3):
                            if m != 1:
                                sp.wait_ge(gu_done if m == 0 else dn_done, after + 2)
                                sp.sem_inc(sp_turns, 1)
                            sp.wait_ge(we_in[3 * j + m], i * 16 + 16 * j)
                            load_expert(j, m, e)
            for j, at in ((0, N_EVEN), (1, N_ODD)):
                m = sp.value_load(plan[0:1, at:at + 1], min_val=0, max_val=NBLK // 2)
                sp.wait_ge(moved[j], m * 16 + 16)
                sp.sem_inc(sp_turns, 1)
            for i in ORDER:
                r = rows(i)
                sp.dma_start(yp[i][0:r], pair_dram[2 * P * i:2 * P * i + 2 * r, :].rearrange("(p k) d -> p k d", k=2))\
                  .then_inc(yp_in[i], 16)
            for p, i in enumerate(ORDER):
                sp.wait_ge(y_out_ready, p + 1)
                r = rows(i)
                dst = y_prompt[0][i * P:i * P + r, :] if i < 4 else y_sample.rearrange("b o d -> (b o) d")
                sp.dma_start(dst, ft[i][0:r, :]).then_inc(out_sem, 16)
            sp.wait_ge(out_sem, 16 * (4 + TILES))
            sp.wait_ge(s_out, 16)
            for j in range(2):
                sp.wait_ge(st_out[j], 16 * (NS // 2))

        @block.gpsimd
        def _(pool):
            steps = [0]

            def link(ins):
                steps[0] += 1
                ins.then_inc(pool_step, 1)
                pool.wait_ge(pool_step, steps[0])

            link(pool.memset(packrows[0:ROWS, :], 0.0))
            pool.sem_inc(rows_clear, 1)
            link(pool.memset(ident[:], 0.0))
            link(pool.memset(ones[:], 1.0))
            link(pool.memset(maskT[:], 1.0))
            link(pool.affine_select(out=ident[:], in_=ident[:], compare_op=ALU.not_equal, fill=1.0, base=0,
                               pattern=[[-1, P]], channel_multiplier=1))
            link(pool.affine_select(out=upper[:], in_=ones[:], compare_op=ALU.is_ge, fill=0.0, base=-1,
                               pattern=[[1, P]], channel_multiplier=-1))
            link(pool.affine_select(out=sel8[0:9, :], in_=ones[0:9, :], compare_op=ALU.is_ge, fill=0.0, base=-8,
                               pattern=[[0, P]], channel_multiplier=1))
            for q in range(2):
                m = maskT[64 * q:64 * q + 64, :]
                link(pool.affine_select(out=m, in_=m, compare_op=ALU.is_ge, fill=0.0, base=0,
                                   pattern=[[1, CH]], channel_multiplier=-1))
            pool.sem_inc(consts, 1)
            pool.wait_ge(w_used, MOD_TILES)
            link(pool.memset(bd[0], 0.0))
            link(pool.memset(bd[1], 0.0))
            for g, name in enumerate(("rg_wa", "rg_wx")):
                w = t[name][0].rearrange("(c two) i j -> two i c j", two=2)
                for q in range(2):
                    pool.dma_start(bd[g][64 * q:64 * q + 64, :, 64 * q:64 * q + 64], w[q]).then_inc(bd_in, 16)
            pool.dma_start(wa2[0:RANK, :], t["gla_wa2"][0]).then_inc(bd_in, 16)
            link(pool.memset(scan_mask[:], 1.0))
            link(pool.memset(scan_mask[:, 0:T:CH], 0.0))
            link(pool.memset(scan_mask[:, T:NT], 0.0))
            pool.sem_inc(consts, 1)

            pool.wait_ge(yb_ready, KD)
            ii = iota_i.bitcast(I32)
            link(pool.iota(ii[:, 0:NG], pattern=[[1, NG]], base=-99, channel_multiplier=0))
            link(pool.tensor_copy(j4[:], ii[:, 0:NG]))
            link(pool.iota(ii[:, 0:NE], pattern=[[1, NE]], base=-99, channel_multiplier=0))
            link(pool.tensor_copy(j32[:], ii[:, 0:NE]))
            link(pool.iota(ii[:, 0:SPLITS], pattern=[[CAP, SPLITS]], base=0, channel_multiplier=0))
            link(pool.tensor_copy(m64[:], ii[:, 0:SPLITS]))
            link(pool.iota(ii[:, 0:NBLK], pattern=[[1, NBLK]], base=0, channel_multiplier=0))
            link(pool.tensor_copy(blk_f[:], ii[:, 0:NBLK]))
            link(pool.iota(ii[:, 0:CAP], pattern=[[1, CAP]], base=0, channel_multiplier=0))
            link(pool.tensor_copy(place_no[:], ii[:, 0:CAP]))
            link(pool.iota(ii[:, 0:2], pattern=[[-1, 2]], base=0, channel_multiplier=1))
            link(pool.tensor_copy(row[:], ii[:, 0:2]))
            for k in range(2):
                link(pool.iota(ii[:, 0:TILES], pattern=[[P, TILES]], base=-OOB, channel_multiplier=1))
                link(pool.tensor_copy(names[:, 0, :, k], ii[:, 0:TILES]))
                link(pool.iota(ii[:, 0:TILES], pattern=[[2 * P, TILES]], base=k - OOB, channel_multiplier=2))
                link(pool.tensor_copy(names[:, 1, :, k], ii[:, 0:TILES]))
            link(pool.memset(LG[:, 4, :], 0.0))
            link(pool.memset(before[:, 0, :], 0.0))
            pool.sem_inc(iotas, 1)
            for s in STARTS_AT_ONE:
                pool.sem_inc(s, 1)
            pool.sem_inc(gu_done, 2)
            pool.sem_inc(dn_done, 2)
            pool.sem_inc(started, 1)
            pool.wait_ge(hf_ready, TILES)
            for j, name in enumerate(("ln2_g", "ln2_b")):
                pool.dma_start(ln2[:, j, :], t[name][0:1, :].to_broadcast([P, D])).then_inc(moved[j], 16)
            for j in range(2):
                link(pool.memset(xg[j][0:CAP, :], 0.0))
            pool.wait_ge(idx_ready, 1)
            for j in range(2):
                pool.wait_ge(hf_out[j], 16 * (3 - j))

            def gather(j):
                pool.sem_inc(pool_turns, 1)
                pool.indirect_dma_start(xg[j][0:CAP, :], None, hf_dram,
                                        bass.IndirectOffsetOnAxis(ap=gidx[j][0:CAP, 0:1], axis=0),
                                        bounds_check=NT - 1, oob_is_err=False).then_inc(xg_in[j], 16)

            for j in range(2):
                pool.tensor_copy(gidx[j][0:CAP, :], idx[0:CAP, j, 0:1]).then_inc(gidx_copied, 1)
                pool.wait_ge(gidx_copied, j + 1)
                gather(j)
            pool.wait_ge(blocks_ready, 1)
            n = pool.value_load(plan[0:1, N_BLK:N_BLK + 1], min_val=0, max_val=NBLK)

            def column(b, c):
                return idx[0:CAP, bass.ds(b, 1), c:c + 1].rearrange("p o c -> p (o c)")

            def scatter(i, j):
                pool.wait_ge(moved[j], i * 16 + 16)
                pool.tensor_copy(sidx[j][0:CAP, :], column(i * 2 + j, 1)).then_inc(sidx_copied, 1)
                pool.wait_ge(sidx_copied, i * 2 + (j + 1))
                pool.wait_ge(y_ready[j], i * 2 + 3)
                pool.sem_inc(pool_turns, 1)
                pool.indirect_dma_start(
                    pair_dram, bass.IndirectOffsetOnAxis(ap=sidx[j][0:CAP, 0:1], axis=0),
                    yb[j][0:CAP, :], None, bounds_check=PAIRS - 1, oob_is_err=False).then_inc(moved[j], 16)

            def two_blocks(i):
                for j in range(2):
                    with pool.If(n > i * 2 + j):
                        pool.wait_ge(xt_done[j], i + 2)
                        pool.tensor_copy(gidx[j][0:CAP, :], column(i * 2 + (j + 2), 0)).then_inc(gidx_copied, 1)
                        pool.wait_ge(gidx_copied, i * 2 + (j + 3))
                        gather(j)
                    if j == 1:
                        with pool.If(n > i * 2):
                            scatter(i, 0)
                    elif not isinstance(i, int):
                        with pool.If(n > i * 2 - 1):
                            scatter(i - 1, 1)

            two_blocks(0)
            with pool.Fori(1, NBLK // 2) as i:
                two_blocks(i)
            for j in range(2):
                pool.wait_ge(moved[j], 16)
            for p, i in enumerate(ORDER):
                r = rows(i)
                pool.wait_ge(norm_ready, p + 1)
                link(pool.tensor_tensor(yp[i][0:r, 1, :], yp[i][0:r, 1, :], ln2[0:r, 0, :], ALU.mult))
                pool.tensor_tensor(ft[i][0:r, :], yp[i][0:r, 1, :], ln2[0:r, 1, :], ALU.add).then_inc(y_out_ready, 1)

        @block.scalar
        def _(sc):
            steps = [0]

            def link(ins):
                steps[0] += 1
                ins.then_inc(act_step, 1)
                sc.wait_ge(act_step, steps[0])

            b_in = t["b_in"]
            sc.wait_ge(rows_clear, 1)
            packs = [(R_C, 8, t["c_sample"]), (R_C + 8, 1, t["c_prompt"]),
                     (R_CONVST, 24, t["state_conv"][0].rearrange("b w d -> (b w) d")),
                     (R_H0, 8, t["state_rglru"][0]), (R_CONVW, CONV, t["conv_w"][0]), (R_CONVB, 1, t["conv_b"]),
                     (R_BA, 1, t["rg_ba"]), (R_BX, 1, t["rg_bx"]), (R_LAM, 1, t["rg_lambda"]),
                     (R_BIN, 5, b_in[:, 0:5120].rearrange("o (r d) -> (o r) d", d=D)),
                     (R_BIN + 5, 2, b_in[:, 5136:7184].rearrange("o (r d) -> (o r) d", d=D))]
            for r, m, src in packs:
                sc.dma_start(packrows[r:r + m, :], src).then_inc(pack_in, 16)
            for c0, m, src in ((0, 512, t["gla_ba"]), (512, 256, t["gla_norm_g"]), (768, RANK, b_in[:, 5120:5136])):
                sc.dma_start(packrows[R_MISC:R_MISC + 1, c0:c0 + m], src).then_inc(pack_in, 16)
            sc.dma_start(mod_sb[0:1, :], t["b_mod"][0:1, :]).then_inc(bmod_in, 16)
            sc.dma_start(alpha_w[:], t["w_in"][0][:, 5120:5136].rearrange("(k p) n -> p k n", p=P)).then_inc(small_in, 16)
            sc.dma_start(route_w[:, :, 0:NG], t["w_grp"][0].rearrange("(k p) n -> p k n", p=P)).then_inc(small_in, 16)
            sc.dma_start(route_w[:, :, NG:NG + NE], t["w_exp"][0].rearrange("(k p) n -> p k n", p=P)).then_inc(small_in, 16)
            sc.dma_start(route_b[:, 0:NG], t["b_grp"][0:1, :].to_broadcast([P, NG])).then_inc(small_in, 16)
            sc.dma_start(route_b[:, NG:NG + NE], t["b_exp"][0:1, :].to_broadcast([P, NE])).then_inc(small_in, 16)
            sc.dma_start(new_conv_s[0, :, 0:2, :], t["state_conv"][0][:, 1:3, :]).then_inc(s_out, 16)

            def root_x(i):
                sc.wait_ge(rstd_q, i + 1)
                sc.activation(mv[0:rows(i), 2:3], mv[0:rows(i), 1:2], ACT.Sqrt).then_inc(rstd_a, 1)

            root_x(0)
            await_job(sc, ("pack", 0))
            link(sc.activation(fp[:], slot_banks(("pack", 0))[:, 0, :].rearrange("p (k r) -> p k r", r=64)[:, :, 0:ROWS],
                               ACT.Copy))
            sc.sem_inc(slot_free[0], 1)
            sc.activation(cs[:], fp[:, :, R_C:R_C + 9], ACT.Silu).then_inc(cs_ready, 1)

            def copy_mod(m):
                await_job(sc, ("mod", m))
                for g in range(4):
                    ins = sc.activation(mod_sb[0:9, m * 512 + g * P:m * 512 + (g + 1) * P],
                                        slot_banks(("mod", m))[32 * g:32 * g + 9, 0, 0:P], ACT.Copy)
                    if g < 3:
                        ins.then_inc(mod_ready, 1)
                    else:
                        link(ins)
                sc.sem_inc(mod_ready, 1)
                sc.sem_inc(freed(("mod", m)), 1)

            for i in range(TILES + 1):
                if 0 < i < TILES:
                    root_x(i)
                if i >= 1:
                    k = i - 1
                    await_job(sc, ("xt", k))
                    v = slot_banks(("xt", k)).rearrange("p h (k n) -> p (h k) n", k=4)[:, :, 0:rows(k)]
                    ins = sc.activation(hT[:, :, k * P:k * P + rows(k)], v, ACT.Copy)
                    ins.then_inc(freed(("xt", k)), 1)
                    if k >= 1:
                        copy_mod(k - 1)
            sc.wait_ge(modT_ready, 1)
            sc.wait_ge(slot_free[INDEX[("xt", 4)] % 3], INDEX[("xt", 4)] // 3 + 1)
            for k in range(0, KD, 2):
                sc.activation(hT[:, k, 0:T], hT[:, k, 0:T], ACT.Identity, bias=modT[:, k, 8:9],
                              scale=modT[:, 8 + k, 8:9]).then_inc(hT_act, 1)
            sc.wait_ge(lam_q, 1)
            link(sc.activation(lam[:, 2, :], lam[:, 1, :], ACT.Exp))
            sc.activation(lam[:, 3, :], lam[:, 2, :], ACT.Ln, bias=1.0).then_inc(lam_a, 1)

            def sqrt_step(c):
                sc.wait_ge(th_ready, c + 1)
                sc.activation(rg["sq"][c % 2], rg["th"][c % 2], ACT.Sqrt).then_inc(sqrt_ready, 1)

            for g in range(2):
                for c in range(4 * g, 4 * g + 4):
                    await_job(sc, ("rx", c))
                    link(sc.activation(halves(A[:, c, :]), two_halves(("rx", c)), ACT.Identity,
                                       bias=fp[:, c, R_BIN:R_BIN + 1]))
                    sc.sem_inc(freed(("rx", c)), 1)
                    sc.sem_inc(rx_ready, 1)
                    if c == 4:
                        sqrt_step(3)
                    if ("rx", c) in LATE_MOD:
                        copy_mod(LATE_MOD[("rx", c)])
                for c in range(4 * g, 4 * g + 4):
                    await_job(sc, ("ry", c))
                    link(sc.activation(halves(O[:, c, :]), two_halves(("ry", c)), ACT.Gelu_apprx_tanh,
                                       bias=fp[:, c, R_BIN + 1:R_BIN + 2]))
                    sc.sem_inc(freed(("ry", c)), 1)
                    sc.sem_inc(ry_ready, 1)
                    if c > 4 * g:
                        sqrt_step(c - 1)
                    if c == 0:
                        sc.wait_ge(lam_ready, 1)
                    if c >= 2:
                        sc.wait_ge(ya_ready, c - 1)
                    for name, job, row in (("r", "ra", R_BA), ("i", "ri", R_BX)):
                        await_job(sc, (job, c))
                        link(sc.activation(halves(rg[name][c % 2]), two_halves((job, c)), ACT.Sigmoid,
                                           bias=fp[:, c, row:row + 1]))
                        sc.sem_inc(freed((job, c)), 1)
                    sc.activation(rg["a"][c % 2], rg["r"][c % 2], ACT.Exp, scale=lam[:, 5, c:c + 1]).then_inc(gates_ready, 1)
                    sc.activation(rg["th"][c % 2], rg["r"][c % 2], ACT.Tanh, scale=lam[:, 4, c:c + 1]).then_inc(gates_ready, 1)
                    if ("ry", c) in LATE_MOD:
                        copy_mod(LATE_MOD[("ry", c)])
            sqrt_step(7)

            for c in range(8):
                await_job(sc, ("qk", c))
                sc.activation(halves(Q[:, c, :]), two_halves(("qk", c)), ACT.Identity,
                              bias=fp[:, c, R_BIN + 2:R_BIN + 3]).then_inc(freed(("qk", c)), 1)
            await_job(sc, ("al", 0))
            link(sc.activation(halves(al[0:RANK, :]), two_halves(("al", 0))[0:RANK], ACT.Identity,
                               bias=fp[0:RANK, 6, R_MISC:R_MISC + 1]))
            sc.sem_inc(freed(("al", 0)), 1)
            sc.sem_inc(al_ready, 1)
            sc.wait_ge(ya_ready, KD)
            for c in range(HEADS):
                await_job(sc, ("la", c))
                sc.activation(halves(L[:, c, :]), two_halves(("la", c)), ACT.Identity,
                              bias=fp[:, c, R_MISC:R_MISC + 1]).then_inc(freed(("la", c)), 1)
            sc.wait_ge(nabs_ready, 1)
            link(sc.activation(EX[:], EX[:], ACT.Exp))
            sc.activation(EX[:], EX[:], ACT.Ln, bias=1.0).then_inc(log_ready, 1)

            def copy_v(c):
                await_job(sc, ("v", c))
                if c >= 2:
                    await_job(sc, ("vt", c - 2))
                link(sc.activation(halves(vf[c % 2]), two_halves(("v", c)), ACT.Identity,
                                   bias=fp[:, c, R_BIN + 3:R_BIN + 4]))
                sc.sem_inc(freed(("v", c)), 1)
                sc.sem_inc(vf_ready, 1)

            copy_v(0)
            sc.wait_ge(bcum_ready, 1)
            sc.activation(L[:], EX[:], ACT.Exp, scale=1.0 / TAU).then_inc(e1_ready, 1)
            sc.activation(K2[:], EX[:], ACT.Exp, scale=-1.0 / TAU).then_inc(e1_ready, 1)
            copy_v(1)
            sc.wait_ge(dexp_q, 1)
            sc.activation(EX[:, :, 0:T], EX[:, :, 0:T], ACT.Exp, scale=1.0 / TAU).then_inc(e2_ready, 1)
            for c in range(2, 8):
                copy_v(c)

            for i in range(4):
                await_job(sc, ("kt", i))
                ins = sc.activation(kout_tok[:, i, :], slot_banks(("kt", i))[:, 0, :], ACT.Copy)
                ins.then_inc(freed(("kt", i)), 1)
            sc.sem_inc(kt_ready, 1)
            def gate(c):
                await_job(sc, ("gg", c))
                sc.activation(halves(G[:, c, :]), two_halves(("gg", c)), ACT.Silu, bias=fp[:, c, R_BIN + 4:R_BIN + 5])\
                  .then_inc(freed(("gg", c)), 1)

            sc.wait_ge(mod_out, 16)
            for n in range(NCH):
                gate(n)
                await_job(sc, ("os", n))
                sc.activation(O[:, :, T + n:T + n + 1], slot_banks(("os", n))[:, 0, 0:8].unsqueeze(2), ACT.Copy)\
                  .then_inc(freed(("os", n)), 1)
                sc.wait_ge(o_done, n + 1)
                sc.activation(O[:, :, n * CH:(n + 1) * CH], ps[:, 7, :].rearrange("p (a b) -> p a b", b=CH), ACT.Copy)\
                  .then_inc(o_copied, 1)
            def square(h):
                if h >= 2:
                    await_job(sc, ("ss", h - 2))
                sc.activation(sq[h % 2], O[:, 2 * h:2 * h + 2, :], ACT.Square).then_inc(sq_ready, 1)

            def root(h):
                sc.wait_ge(var_ready, h + 1)
                sc.activation(rms[h % 2], rms[h % 2], ACT.Sqrt).then_inc(rms_ready, 1)

            def merge_gate(job, c):
                dst, row = (Z, 5) if job == "ga" else (Q, 6)
                await_job(sc, (job, c))
                link(sc.activation(halves(dst[:, c, :]), two_halves((job, c)), ACT.Sigmoid,
                                   bias=fp[:, c, R_BIN + row:R_BIN + row + 1]))
                sc.sem_inc(freed((job, c)), 1)
                sc.sem_inc(sig_ready, 1)

            sc.wait_ge(o_copied, NCH)
            sc.wait_ge(freed(("os", 7)), INDEX[("os", 7)] // 3 + 1)
            for j in range(2):
                sc.wait_ge(st_out[j], 16 * (NS // 2))
            square(0)
            sc.wait_ge(s_out, 32)
            merge_gate("ga", 0)
            square(1)
            for h in range(3):
                root(h)
                merge_gate("ga", h + 1)
                if h < 2:
                    square(h + 2)
            root(3)
            for c in range(4, 8):
                merge_gate("ga", c)
            for c in range(8):
                merge_gate("gb", c)
            for k, (job, m) in enumerate((("rlT", 11), ("hlT", 9))):
                await_job(sc, (job, 0))
                link(sc.activation(outrow[0:m, k, :].rearrange("p (h n) -> p h n", h=2), slot_banks((job, 0))[0:m], ACT.Copy))
                sc.sem_inc(freed((job, 0)), 1)
                sc.sem_inc(outs_ready, 1)
            sc.wait_ge(z_ready, KD)
            for v, name in enumerate(("ln1_g", "ln1_b")):
                sc.dma_start(lnp[:, v, :], t[name][0:1, :].to_broadcast([P, D])).then_inc(lnp_in, 16)
            await_job(sc, ("wo", 4))
            for g in range(4):
                ins = sc.activation(lt[0:NS, g * 256:(g + 1) * 256], slot_banks(("wo", 4))[32 * g:32 * g + NS, 0, 0:256], ACT.Copy)
                if g < 3:
                    ins.then_inc(mix_ready, 1)
                else:
                    link(ins)
            sc.sem_inc(mix_ready, 1)
            sc.sem_inc(freed(("wo", 4)), 1)
            for p, i in enumerate(ORDER):
                for k in range(2):
                    sc.wait_ge(rstd_q, TILES + 2 * p + k + 1)
                    sc.activation(mv[0:rows(i), 2:3], mv[0:rows(i), 1:2], ACT.Sqrt).then_inc(rstd_a, 1)
                await_job(sc, ("ht", i))
                if p >= 2:
                    await_job(sc, ("lg", ORDER[p - 2]))
                v = slot_banks(("ht", i)).rearrange("p h (k n) -> p (h k) n", k=4)[:, :, 0:rows(i)]
                link(sc.activation(hfT[p % 2][:, :, 0:rows(i)], v, ACT.Copy))
                sc.sem_inc(freed(("ht", i)), 1)
                sc.sem_inc(hfT_ready, 1)
            sc.wait_ge(ge_q, 1)
            sc.activation(g_e[:], g_e[:], ACT.Exp).then_inc(ge_a, 1)
            sc.wait_ge(ge_q, 2)
            sc.activation(g_m[:, 6, :], g_m[:, 5, :], ACT.Exp).then_inc(ge_a, 1)

            sc.wait_ge(blocks_ready, 1)
            sc.wait_ge(started, 1)
            sc.wait_ge(xt_done[0], 2)
            sc.activation(xT[0], ps[:, 0, :].rearrange("p (k n) -> p k n", k=KD), ACT.Copy).then_inc(xT_ready[0], 1)
            n = sc.value_load(plan[0:1, N_BLK:N_BLK + 1], min_val=0, max_val=NBLK)
            with sc.Fori(0, NBLK // 2) as i:
                for j in range(2):
                    with sc.If(n > i * 2 + j):
                        sc.wait_ge(gu_done, i * 2 + (j + 3))
                        sc.wait_ge(act_ready[j], i + 1)
                        sc.activation(sg[j][CAP:2 * CAP, :], ps[0:CAP, 2 + j, :], ACT.Silu).then_inc(sg_ready[j], 1)
                        sc.wait_ge(xt_done[1 - j], i + (2 + j))
                        sc.wait_ge(gu_done, i * 2 + (j + 2))
                        sc.activation(xT[1 - j], ps[:, 1 - j, :].rearrange("p (k n) -> p k n", k=KD), ACT.Copy)\
                          .then_inc(xT_ready[1 - j], 1)
                        sc.wait_ge(tr_done[j], i + 2)
                        sc.wait_ge(dn_done, i * 2 + (j + 1))
                        sc.activation(acT[j], ps[:, 6 + j, 0:4 * CAP].rearrange("p (k n) -> p k n", k=4), ACT.Copy)\
                          .then_inc(acT_ready[j], 1)
            def weigh(i):
                r = rows(i)
                sc.wait_ge(yp_in[i], 16)
                sc.activation(yp[i][0:r, 0, :], yp[i][0:r, 0, :], ACT.Copy, scale=wpair[0:r, i, 0:1]).then_inc(yw_ready, 1)

            weigh(ORDER[0])
            for p, i in enumerate(ORDER):
                r = rows(i)
                if p + 1 < TILES:
                    weigh(ORDER[p + 1])
                sc.wait_ge(fin_q, 2 * p + 1)
                sc.activation(fmv[0:r, i, 2:3], fmv[0:r, i, 1:2], ACT.Sqrt).then_inc(fin_a, 1)
                sc.wait_ge(fin_q, 2 * p + 2)
                sc.activation(yp[i][0:r, 1, :], yp[i][0:r, 0, :], ACT.Identity, bias=fmv[0:r, i, 2:3],
                              scale=fmv[0:r, i, 3:4]).then_inc(norm_ready, 1)

        @block.vector
        def _(v):
            steps = [0]

            def link(ins):
                steps[0] += 1
                ins.then_inc(dve_step, 1)
                v.wait_ge(dve_step, steps[0])

            roots = [0]

            def layer_stats(x, r, ask, answer):
                link(v.bn_stats(stats[0:r, 0, :], x[:, 0:512]))
                link(v.bn_stats(stats[0:r, 1, :], x[:, 512:1024]))
                link(v.bn_aggr(mv[0:r, 0:2], stats[0:r].rearrange("p a b -> p (a b)")))
                v.tensor_scalar_add(mv[0:r, 1:2], mv[0:r, 1:2], LN_EPS).then_inc(ask, 1)
                roots[0] += 1
                v.wait_ge(answer, roots[0])
                link(v.reciprocal(mv[0:r, 3:4], mv[0:r, 2:3]))

            def normalise(out, x, r):
                return v.tensor_scalar(out, x, mv[0:r, 0:1], mv[0:r, 3:4], ALU.subtract, ALU.mult)

            v.wait_ge(x_in, 32)
            for i in range(TILES):
                r = rows(i)
                layer_stats(x_tok[0:r, i, :], r, rstd_q, rstd_a)
                if i >= 2:
                    await_job(v, ("xt", i - 2))
                link(normalise(xn[i % 2][0:r, :], x_tok[0:r, i, :], r))
                v.sem_inc(xn_ready, 1)
            await_job(v, ("modT", 0))
            mt = slot_banks(("modT", 0))[:, 0, 0:144].rearrange("p (a b) -> p a b", b=9)
            link(v.tensor_copy(modT[:, 0:8, :], mt[:, 0:8, :]))
            link(v.tensor_scalar_add(modT[:, 8:16, :], mt[:, 8:16, :], 1.0))
            v.sem_inc(freed(("modT", 0)), 1)
            v.sem_inc(modT_ready, 1)
            v.wait_ge(slot_free[INDEX[("xt", 4)] % 3], INDEX[("xt", 4)] // 3 + 1)
            hs = hT[:, :, T:NT]
            link(v.tensor_tensor(hs, hs, modT[:, 8:16, 0:8], ALU.mult))
            v.tensor_tensor(hs, hs, modT[:, 0:8, 0:8], ALU.add).then_inc(hT_dve, 1)
            for k in range(1, KD, 2):
                v.tensor_scalar(hT[:, k, 0:T], hT[:, k, 0:T], modT[:, 8 + k, 8:9], modT[:, k, 8:9], ALU.mult, ALU.add)\
                 .then_inc(hT_dve, 1)
            lm = fp[:, :, R_LAM]
            link(v.tensor_scalar(lam[:, 0, :], lm, -1.0, 0.0, ALU.mult, ALU.max))
            v.scalar_tensor_tensor(lam[:, 1, :], lm, -1.0, lm, ALU.mult, ALU.min).then_inc(lam_q, 1)
            v.wait_ge(lam_a, 1)
            link(v.tensor_tensor(lam[:, 3, :], lam[:, 3, :], lam[:, 0, :], ALU.add))
            link(v.tensor_scalar_mul(lam[:, 4, :], lam[:, 3, :], 8.0))
            v.tensor_scalar_mul(lam[:, 5, :], lam[:, 3, :], -8.0).then_inc(lam_ready, 1)

            def conv(c):
                v.wait_ge(rx_ready, c + 1)
                if c >= 2:
                    await_job(v, ("ri", c - 2))
                xc = rg["xc"][c % 2]
                w = [fp[:, c, R_CONVW + k:R_CONVW + k + 1] for k in range(CONV)]
                link(v.tensor_copy(rl[:, c, :], A[:, c, 509:520]))
                link(v.tensor_scalar(xc[:], A[:, c, :], w[3], fp[:, c, R_CONVB:R_CONVB + 1], ALU.mult, ALU.add))
                for k in range(1, CONV):
                    link(v.scalar_tensor_tensor(xc[:, k:T], A[:, c, 0:T - k], w[3 - k], xc[:, k:T], ALU.mult, ALU.add))
                for k in range(3):
                    s = fp[:, c, R_CONVST + k:R_CONVST + 24:3]
                    link(v.scalar_tensor_tensor(xc[:, T:NT], s, w[k], xc[:, T:NT], ALU.mult, ALU.add))
                v.sem_inc(xc_ready, 1)

            def recur(c):
                j = c % 2
                a, th, u, h = rg["a"][j], rg["th"][j], rg["i"][j], rg["r"][j]
                v.wait_ge(gates_ready, 2 * c + 2)
                link(v.tensor_tensor(u[:], u[:], rg["xc"][j][:], ALU.mult))
                link(v.tensor_tensor(rg["sq"][j][:], a[:], a[:], ALU.mult))
                link(v.scalar_tensor_tensor(th[:], rg["sq"][j][:], 1.0, th[:], ALU.add, ALU.mult))
                v.sem_inc(th_ready, 1)
                v.wait_ge(sqrt_ready, c + 1)
                link(v.tensor_tensor(u[:], u[:], rg["sq"][j][:], ALU.mult))
                link(v.tensor_tensor(tmp8[:, 0, :], a[:, T:NT], fp[:, c, R_H0:R_H0 + 8], ALU.mult))
                link(v.tensor_tensor_scan(h[:, 0:T], a[:, 0:T], u[:, 0:T], 0.0, ALU.mult, ALU.add))
                link(v.tensor_tensor(h[:, T:NT], u[:, T:NT], tmp8[:, 0, :], ALU.add))
                link(v.tensor_copy(hl[:, c, :], h[:, T - 1:NT]))
                v.wait_ge(ry_ready, c + 1)
                link(v.tensor_tensor(A[:, c, :], h[:], O[:, c, :], ALU.mult))
                v.sem_inc(ya_ready, 1)

            for c in range(KD):
                conv(c)
                if c:
                    recur(c - 1)
            recur(KD - 1)

            v.wait_ge(freed(("la", 3)), INDEX[("la", 3)] // 3 + 1)
            v.wait_ge(freed(("la", 2)), INDEX[("la", 2)] // 3 + 1)
            v.wait_ge(freed(("la", 1)), INDEX[("la", 1)] // 3 + 1)
            link(v.scalar_tensor_tensor(EX[:], L[:], -1.0, L[:], ALU.mult, ALU.min))
            v.sem_inc(nabs_ready, 1)
            v.wait_ge(log_ready, 1)
            link(v.scalar_tensor_tensor(L[:], L[:], 0.0, EX[:], ALU.min, ALU.subtract))
            v.wait_ge(consts, 2)
            for h in range(HEADS):
                link(v.tensor_tensor_scan(EX[:, h, :], scan_mask[:], L[:, h, :], 0.0, ALU.mult, ALU.add))
            v.sem_inc(bcum_ready, 1)
            v.tensor_copy(bt[:], EX[:, :, CH - 1:T:CH])
            v.wait_ge(e1_ready, 2)
            link(v.tensor_copy(ela[:], L[:, :, T:NT]))
            link(v.tensor_copy(dec[:], L[:, :, CH - 1:T:CH]))
            for h in range(HEADS):
                e = EX[:, h, 0:T].rearrange("p (n c) -> p n c", c=CH)
                link(v.tensor_tensor(e, bt[:, h, :].unsqueeze(2).to_broadcast([P, NCH, CH]), e, ALU.subtract))
            v.sem_inc(dexp_q, 1)

            def copy_vt(c):
                await_job(v, ("vt", c))
                b = slot_banks(("vt", c))
                link(v.tensor_copy(v_tok[:, :, c * P:(c + 1) * P], b[:, 0, :].rearrange("p (i n) -> p i n", i=4)))
                link(v.tensor_copy(v_samp[0:NS, c * P:(c + 1) * P], b[0:NS, 1, 0:P]))
                v.sem_inc(freed(("vt", c)), 1)
                v.sem_inc(vt_ready, 1)

            copy_vt(0)
            link(v.tensor_scalar_mul(qs[:], Q[:, 0:HEADS, T:NT], DKH ** -0.5))
            link(v.scalar_tensor_tensor(Q[:, 0:HEADS, 0:T], Q[:, 0:HEADS, 0:T], DKH ** -0.5, L[:, :, 0:T],
                                        ALU.mult, ALU.mult))
            v.wait_ge(e2_ready, 1)
            link(v.tensor_tensor(EX[:, :, 0:T], EX[:, :, 0:T], Q[:, HEADS:8, 0:T], ALU.mult))
            copy_vt(1)
            link(v.tensor_tensor(Q[:, HEADS:8, 0:T], Q[:, HEADS:8, 0:T], K2[:, :, 0:T], ALU.mult))
            v.sem_inc(gla_in_ready, 1)
            for c in range(2, 8):
                copy_vt(c)
            for n in range(NCH):
                q = 64 * (n % 2)
                v.wait_ge(at_done, n + 1)
                if n >= 2:
                    v.wait_ge(o_done, n - 1)
                if n == 0:
                    v.wait_ge(kt_ready, 1)
                am = attm[n % 2][q:q + 64]
                link(v.tensor_scalar(am, ps[q:q + 64, 6, 0:256].rearrange("p (h i) -> p h i", h=HEADS), MAX, -MAX,
                                     ALU.min, ALU.max))
                link(v.tensor_tensor(am, am, maskT[q:q + 64, :].unsqueeze(1).to_broadcast([64, HEADS, CH]), ALU.mult))
                v.sem_inc(attm_ready, 1)
                await_job(v, ("ds", n))
                if n >= 1:
                    v.wait_ge(o_done, n)
                ds = slot_banks(("ds", n)).rearrange("p b (h w) -> p (b h) w", w=DVH)
                new = S[(n + 1) % 2]
                for h in range(HEADS):
                    if n == 0:
                        link(v.tensor_copy(new[:, h, :], ds[:, h, :]))
                    else:
                        link(v.scalar_tensor_tensor(new[:, h, :], S[n % 2][:, h, :], dec[:, h, n:n + 1], ds[:, h, :],
                                                    ALU.mult, ALU.add))
                v.sem_inc(freed(("ds", n)), 1)
                v.sem_inc(s_ready, 1)
                v.wait_ge(st_in[n % 2], 16 * (n // 2 + 1))
                for h in range(HEADS):
                    link(v.tensor_scalar_mul(st[n % 2][:, h, :], st[n % 2][:, h, :], ela[:, h, n:n + 1]))
                v.wait_ge(vb_in, 16 * (n + 1))
                for h in range(HEADS):
                    link(v.scalar_tensor_tensor(st[n % 2][:, h, :], vb[:, h, :], Q[:, HEADS + h, T + n:T + n + 1],
                                                st[n % 2][:, h, :], ALU.mult, ALU.add))
                v.sem_inc(st_ready, 1)

            def variance(h):
                await_job(v, ("ss", h))
                link(v.tensor_scalar(halves(rms[h % 2]), two_halves(("ss", h)), 1.0 / DVH, RMS_EPS, ALU.mult, ALU.add))
                v.sem_inc(freed(("ss", h)), 1)
                v.sem_inc(var_ready, 1)

            def rescale(h):
                v.wait_ge(rms_ready, h + 1)
                link(v.reciprocal(rms[h % 2][:], rms[h % 2][:]))
                for d in range(2):
                    link(v.scalar_tensor_tensor(O[:, 2 * h + d, :], O[:, 2 * h + d, :], fp[:, 4 + d, R_MISC:R_MISC + 1],
                                                rms[h % 2][:], ALU.mult, ALU.mult))

            def gate(c):
                link(v.tensor_tensor(O[:, c, :], O[:, c, :], G[:, c, :], ALU.mult))
                v.sem_inc(yb_ready, 1)

            v.wait_ge(freed(("gg", 7)), INDEX[("gg", 7)] // 3 + 1)
            variance(0)
            variance(1)
            for h in range(HEADS):
                rescale(h)
                if h + 2 < HEADS:
                    variance(h + 2)
                gate(2 * h)
                gate(2 * h + 1)
            for c in range(KD):
                v.wait_ge(sig_ready, c + 1)
                await_job(v, ("pa", c))
                link(v.tensor_tensor(halves(Z[:, c, :]), halves(Z[:, c, :]), two_halves(("pa", c)), ALU.mult))
                v.sem_inc(freed(("pa", c)), 1)
            for c in range(KD):
                v.wait_ge(sig_ready, KD + c + 1)
                await_job(v, ("pb", c))
                link(v.tensor_tensor(halves(Q[:, c, :]), halves(Q[:, c, :]), two_halves(("pb", c)), ALU.mult))
                v.sem_inc(freed(("pb", c)), 1)
                link(v.tensor_tensor(Z[:, c, :], Z[:, c, :], Q[:, c, :], ALU.add))
                v.sem_inc(z_ready, 1)
            v.wait_ge(mod_back, 32)
            link(v.tensor_scalar_add(bc[:, 2, :], bc[:, 2, :], 1.0))
            link(v.tensor_scalar_add(mod_sb[0:NS, 4 * D:5 * D], mod_sb[0:NS, 4 * D:5 * D], 1.0))

            def modvec(k, i):
                return bc[:, k, :] if i < 4 else mod_sb[0:NS, (2 + k) * D:(3 + k) * D]

            def add_route_bias(i):
                r = rows(i)
                await_job(v, ("lg", i))
                if i == 4:
                    v.wait_ge(iotas, 1)
                link(v.tensor_tensor(LG[0:r, i, :], slot_banks(("lg", i))[0:r, 0, 0:NG + NE], route_b[0:r, :], ALU.add))
                v.sem_inc(freed(("lg", i)), 1)

            v.wait_ge(lnp_in, 32)
            for p, i in enumerate(ORDER):
                r = rows(i)
                u = lt[0:r, :]
                uh = u.rearrange("p (h n) -> p h n", h=2)
                x = x_tok[0:r, i, :]
                if i == 4:
                    v.wait_ge(mix_ready, 4)
                    link(v.tensor_tensor(u, u, modvec(0, i), ALU.mult))
                else:
                    await_job(v, ("wo", i))
                    link(v.tensor_tensor(uh, slot_banks(("wo", i))[0:r], modvec(0, i).rearrange("p (h n) -> p h n", h=2),
                                         ALU.mult))
                    v.sem_inc(freed(("wo", i)), 1)
                link(v.scalar_tensor_tensor(u, x, ALPHA, u, ALU.mult, ALU.add))
                layer_stats(u, r, rstd_q, rstd_a)
                link(normalise(u, u, r))
                link(v.tensor_tensor(u, u, lnp[0:r, 0, :], ALU.mult))
                link(v.tensor_tensor(x, u, lnp[0:r, 1, :], ALU.add))
                layer_stats(x, r, rstd_q, rstd_a)
                if p >= 2:
                    v.wait_ge(hf_out[p % 2], 16 * (p // 2))
                    await_job(v, ("ht", ORDER[p - 2]))
                h = hf[p % 2][0:r, :]
                link(normalise(h, x, r))
                link(v.tensor_tensor(h, h, modvec(2, i), ALU.mult))
                link(v.tensor_tensor(h, h, modvec(1, i), ALU.add))
                v.sem_inc(hf_ready, 1)
                if p >= 1:
                    add_route_bias(ORDER[p - 1])
            add_route_bias(ORDER[4])

            v.wait_ge(iotas, 1)
            GL = LG[:, :, 0:NG]
            EL = LG[:, :, NG:NG + NE].rearrange("p t (g e) -> p t g e", g=NG)
            bro = lambda a, n: a.unsqueeze(2).to_broadcast([P, TILES, n])
            j4b = j4.unsqueeze(1).to_broadcast([P, TILES, NG])
            j32b = j32.unsqueeze(1).to_broadcast([P, TILES, NE])

            def first_of(eq, jb, low, oh, n):
                link(v.tensor_tensor(eq, eq, jb, ALU.mult))
                link(v.tensor_reduce(low, eq, AX, ALU.min))
                link(v.tensor_tensor(oh, jb, bro(low, n), ALU.is_equal))

            link(v.tensor_reduce(g_m[:, 0, :], GL, AX, ALU.max))
            link(v.tensor_tensor(g_e[:], GL, bro(g_m[:, 0, :], NG), ALU.subtract))
            v.sem_inc(ge_q, 1)
            link(v.tensor_tensor(g_eq[:], GL, bro(g_m[:, 0, :], NG), ALU.is_equal))
            link(v.tensor_tensor(g_eq[:], g_eq[:], j4b, ALU.mult))
            link(v.tensor_reduce(g_m[:, 1, :], g_eq[:], AX, ALU.min))
            link(v.tensor_tensor(g_eq[:], j4b, bro(g_m[:, 1, :], NG), ALU.is_equal))
            v.wait_ge(ge_a, 1)
            link(v.tensor_reduce(g_m[:, 2, :], g_e[:], AX, ALU.add))
            link(v.reciprocal(g_m[:, 2, :], g_m[:, 2, :]))
            mlg = ml.rearrange("p t (g e) -> p t g e", g=NG)
            for i in range(TILES):
                gb = g_eq[:, i, :].unsqueeze(2).to_broadcast([P, NG, EPG])
                link(v.tensor_tensor(mlg[:, i], EL[:, i], gb, ALU.mult))
                link(v.tensor_scalar(e_eq[:, i, :].rearrange("p (g e) -> p g e", g=NG), gb, -1.0, BIG, ALU.add, ALU.mult))
            link(v.tensor_tensor(ml[:], ml[:], e_eq[:], ALU.add))
            for k in range(2):
                link(v.tensor_reduce(g_m[:, 3 + k, :], ml[:], AX, ALU.max))
                link(v.tensor_tensor(e_eq[:], ml[:], bro(g_m[:, 3 + k, :], NE), ALU.is_equal))
                first_of(e_eq[:], j32b, g_m[:, 7, :], OH[:, :, k, :], NE)
                if k == 0:
                    link(v.scalar_tensor_tensor(ml[:], OH[:, :, 0, :], -3.0 * BIG, ml[:], ALU.mult, ALU.add))
            link(v.tensor_tensor(g_m[:, 5, :], g_m[:, 4, :], g_m[:, 3, :], ALU.subtract))
            v.sem_inc(ge_q, 1)
            link(v.tensor_tensor(M[:], OH[:, :, 0, :], OH[:, :, 1, :], ALU.add))
            v.sem_inc(m_ready, 1)
            v.wait_ge(ge_a, 2)
            link(v.tensor_scalar_add(g_m[:, 8, :], g_m[:, 6, :], 1.0))
            link(v.reciprocal(g_m[:, 8, :], g_m[:, 8, :]))
            link(v.tensor_tensor(wpair[:, :, 0], g_m[:, 8, :], g_m[:, 2, :], ALU.mult))
            link(v.tensor_tensor(wpair[:, :, 1], wpair[:, :, 0], g_m[:, 6, :], ALU.mult))
            await_job(v, ("rk", 0))
            rk = slot_banks(("rk", 0))[:, :, 0:TILES * NE].rearrange("p h (t e) -> p h t e", e=NE)
            for i in range(TILES):
                link(v.tensor_tensor(before[:, i + 1, :], before[:, i, :], rk[:, 1, i, :], ALU.add))
            link(v.tensor_tensor(rank[:], rk[:, 0], before[:, 0:TILES, :], ALU.add))
            cb = before[:, TILES, :].unsqueeze(2).to_broadcast([P, NE, SPLITS])
            link(v.tensor_tensor(many[:], cb, m64.unsqueeze(1).to_broadcast([P, NE, SPLITS]), ALU.is_gt))
            link(v.tensor_reduce(cnt[:, 0, :], many[:], AX, ALU.add))
            link(v.tensor_tensor_scan(cnt[:, 1, :], ones[:, 0:NE], cnt[:, 0, :], 0.0, ALU.mult, ALU.add))
            link(v.tensor_tensor(cnt[:, 2, :], cnt[:, 1, :], cnt[:, 0, :], ALU.subtract))
            for k in range(2):
                link(v.tensor_tensor(prod[:, :, k, :], OH[:, :, k, :], rank[:], ALU.mult))
            link(v.tensor_reduce(r1[:], prod[:], AX, ALU.add))
            for k in range(2):
                link(v.tensor_tensor(prod[:, :, k, :], OH[:, :, k, :],
                                     cnt[:, 2, :].unsqueeze(1).to_broadcast([P, TILES, NE]), ALU.mult))
            link(v.tensor_reduce(b1[:], prod[:], AX, ALU.add))
            flat = lambda a: a.rearrange("p t k -> p (t k)")
            wide = lambda a, m: flat(a).unsqueeze(2).to_broadcast([P, 2 * TILES, m])
            link(v.tensor_tensor(ge[:], wide(r1, SPLITS - 1),
                                 m64[:, 1:SPLITS].unsqueeze(1).to_broadcast([P, 2 * TILES, SPLITS - 1]), ALU.is_ge))
            link(v.tensor_reduce(flat(q1), ge[:], AX, ALU.add))
            link(v.scalar_tensor_tensor(place[:], q1[:], -float(CAP), r1[:], ALU.mult, ALU.add))
            link(v.tensor_tensor(block_no[:], b1[:], q1[:], ALU.add))
            link(v.tensor_tensor(place_oh[:], wide(place, CAP), place_no.unsqueeze(1).to_broadcast([P, 2 * TILES, CAP]),
                                 ALU.is_equal))
            link(v.tensor_tensor(block_oh[:], wide(block_no, NBLK), blk_f.unsqueeze(1).to_broadcast([P, 2 * TILES, NBLK]),
                                 ALU.is_equal))
            for m in range(2):
                link(v.tensor_tensor(named[:, :, :, m], block_oh[:], wide(names[:, m], NBLK), ALU.mult))
            v.sem_inc(named_ready, 1)
            link(v.tensor_scalar_min(cnt[:, 3, :], cnt[:, 0, :], 1.0))
            link(v.tensor_scalar(cnt[:, 3, 0:2], cnt[:, 0, 0:2], 0.0, 1.0, ALU.mult, ALU.add))
            link(v.tensor_tensor_scan(cnt[:, 4, :], ones[:, 0:NE], cnt[:, 3, :], 0.0, ALU.mult, ALU.add))
            for k, value, limit, weight in (
                    (0, cnt[:, 1, :], row[:, 0:1], cnt[:, 3, :]),
                    (3, cnt[:, 4, :], row[:, 0:1], ones[:, 0:NE]),
                    (4, cnt[:, 4, :], row[:, 1:2], cnt[:, 0, :])):
                link(v.scalar_tensor_tensor(hits[:], value, limit, weight, ALU.is_le, ALU.mult))
                link(v.tensor_reduce(plan_f[:, k:k + 1], hits[:], AX, ALU.add))
            link(v.tensor_scalar_min(plan_f[:, 3:4], plan_f[:, 3:4], float(NE - 1)))
            link(v.tensor_copy(plan_i[:, 0:1], plan_f[:, 0:1]))
            link(v.tensor_single_scalar(plan_i[:, 1:2], plan_i[:, 0:1], 1, ALU.bitwise_and))
            link(v.tensor_scalar_mul(plan_f[:, 0:1], plan_i[:, 1:2], float(3 * WT)))
            for k in range(2):
                link(v.tensor_scalar_add(plan_i[:, 2 + k:3 + k], plan_i[:, 0:1], 2 + k))
            link(v.tensor_single_scalar(plan_i[:, 4:6], plan_i[:, 2:4], 1, ALU.logical_shift_right))
            link(v.tensor_copy(plan_f[:, 1:3], plan_i[:, 4:6]))
            v.sem_inc(plan_ready, 1)
            await_job(v, ("table", 0))
            link(v.tensor_scalar_add(idx[0:CAP, 0:NBLK, :],
                                     slot_banks(("table", 0))[0:CAP, 0, 0:2 * NBLK].rearrange("p (b c) -> p b c", c=2), float(OOB)))
            link(v.tensor_scalar(idx[0:CAP, NBLK:TW, :], blk_f[0:CAP, 0:2 * (TW - NBLK)].rearrange("p (b c) -> p b c", c=2),
                                 0.0, float(OOB), ALU.mult, ALU.add))
            v.sem_inc(idx_ready, 1)
            await_job(v, ("plan", 0))
            link(v.tensor_copy(plan[0:1, 0:5 * NBLK], slot_banks(("plan", 0))[0:1, 0, 0:5 * NBLK]))
            link(v.tensor_copy(plan[0:1, N_BLK:N_BLK + 1], cnt[0:1, 1, NE - 1:NE]))
            link(v.tensor_copy(plan[0:1, N_LD:N_LD + 1], cnt[0:1, 4, NE - 1:NE]))
            for k in range(2):
                link(v.tensor_scalar_add(plan_i[0:1, k:k + 1], plan[0:1, N_BLK:N_BLK + 1], 1 - k))
            link(v.tensor_single_scalar(plan[0:1, N_EVEN:N_EVEN + 2], plan_i[0:1, 0:2], 1, ALU.logical_shift_right))
            v.sem_inc(blocks_ready, 1)

            n = v.value_load(plan[0:1, N_BLK:N_BLK + 1], min_val=0, max_val=NBLK)

            def take_result(i, j):
                v.wait_ge(dn_done, i * 2 + (j + 3))
                v.wait_ge(moved[j], i * 16 + 16)
                for q in range(2):
                    v.tensor_copy(yb[j][0:CAP, q * 512:(q + 1) * 512], ps[CAP * q:CAP * q + CAP, 4 + j, :])\
                     .then_inc(y_ready[j], 1)

            def two_blocks(i):
                for j in range(2):
                    with v.If(n > i * 2 + j):
                        v.wait_ge(sg_ready[j], i + 1)
                        v.wait_ge(tr_done[j], i + 1)
                        v.tensor_tensor(act[j][0:CAP, :], sg[j][CAP:2 * CAP, :], ps[CAP:2 * CAP, 2 + j, :], ALU.mult)\
                         .then_inc(act_ready[j], 1)
                    if j == 1:
                        with v.If(n > i * 2):
                            take_result(i, 0)
                    elif not isinstance(i, int):
                        with v.If(n > i * 2 - 1):
                            take_result(i - 1, 1)

            two_blocks(0)
            with v.Fori(1, NBLK // 2) as i:
                two_blocks(i)

            for p, i in enumerate(ORDER):
                r = rows(i)
                x = x_tok[0:r, i, :]
                v.wait_ge(yw_ready, p + 1)
                y0 = yp[i][0:r, 0, :]
                link(v.scalar_tensor_tensor(y0, yp[i][0:r, 1, :], wpair[0:r, i, 1:2], y0, ALU.mult, ALU.add))
                link(v.tensor_tensor(y0, y0, modvec(3, i), ALU.mult))
                link(v.scalar_tensor_tensor(y0, x, ALPHA, y0, ALU.mult, ALU.add))
                link(v.bn_stats(stats[0:r, 0, :], y0[:, 0:512]))
                link(v.bn_stats(stats[0:r, 1, :], y0[:, 512:1024]))
                link(v.bn_aggr(fmv[0:r, i, 0:2], stats[0:r].rearrange("p a b -> p (a b)")))
                link(v.tensor_scalar_add(fmv[0:r, i, 1:2], fmv[0:r, i, 1:2], LN_EPS))
                v.sem_inc(fin_q, 1)
                v.wait_ge(fin_a, p + 1)
                link(v.reciprocal(fmv[0:r, i, 3:4], fmv[0:r, i, 2:3]))
                link(v.scalar_tensor_tensor(fmv[0:r, i, 2:3], fmv[0:r, i, 0:1], -1.0, fmv[0:r, i, 3:4], ALU.mult, ALU.mult))
                v.sem_inc(fin_q, 1)

        @block.tensor
        def _(pe):
            def start(job):
                n = INDEX[job]
                if n >= 3:
                    pe.wait_ge(slot_free[n % 3], n // 3)
                return slot_banks(job)

            def done(ins):
                ins.then_inc(job_done, 1)

            tiles = [0]

            def weight_tile():
                s, _, turn = RING[tiles[0]]
                tiles[0] += 1
                pe.wait_ge(w_in_slot[s], 16 * turn)
                return ring[s]

            def tile_used():
                pe.sem_inc(w_used, 1)

            def project_half(out, h, w, col, m, src):
                for k in range(KD):
                    ins = pe.matmul(out[0:m, h, 0:HALF], w[:, k, col:col + m], src[:, k, h * HALF:(h + 1) * HALF],
                                    start=(k == 0), stop=(k == KD - 1))
                return ins

            def project(job, w, col, m, src):
                out = start(job)
                for h in range(2):
                    ins = project_half(out, h, w, col, m, src)
                done(ins)

            pe.wait_ge(pack_in, 16 * 14)
            pe.wait_ge(consts, 1)
            out = start(("pack", 0))
            for k in range(KD):
                ins = pe.transpose(out[:, 0, k * 64:k * 64 + ROWS], packrows[0:ROWS, k * P:(k + 1) * P], ident[0:ROWS, 0:ROWS])
            done(ins)

            def transpose_x(i):
                out = start(("xt", i))
                pe.wait_ge(xn_ready, i + 1)
                r = rows(i)
                for k in range(KD):
                    ins = pe.transpose(out[:, k // 4, (k % 4) * P:(k % 4) * P + r], xn[i % 2][0:r, k * P:(k + 1) * P],
                                       ident[0:r, 0:r])
                done(ins)

            def modulation(m, w):
                out = start(("mod", m))
                for k in range(KD + 1):
                    for g in range(4):
                        o = out[32 * g:32 * g + 9, 0, 0:P]
                        if k < KD:
                            pe.matmul(o, cs[:, k, :], w[:, k, g * P:(g + 1) * P], start=(k == 0), stop=False)
                        else:
                            ins = pe.matmul(o, ones[0:1, 0:9], mod_sb[0:1, m * 512 + g * P:m * 512 + (g + 1) * P],
                                            start=False, stop=True)
                done(ins)

            def late_modulation(job):
                if job in LATE_MOD:
                    m = LATE_MOD[job]
                    pe.wait_ge(mod_w_in, 16 * (m - EARLY_MOD + 1))
                    modulation(m, mod_w)

            transpose_x(0)
            transpose_x(1)
            pe.wait_ge(cs_ready, 1)
            pe.wait_ge(bmod_in, 16)
            for m in range(EARLY_MOD):
                modulation(m, weight_tile())
                pe.wait_ge(job_done, INDEX[("mod", m)] + 1)
                tile_used()
                if m < 3:
                    transpose_x(m + 2)
            pe.wait_ge(mod_ready, 4 * EARLY_MOD)
            out = start(("modT", 0))
            for c in range(16):
                ins = pe.transpose(out[:, 0, c * 9:c * 9 + 9], mod_sb[0:9, c * P:(c + 1) * P], ident[0:9, 0:9])
            done(ins)
            pe.wait_ge(hT_act, KD // 2)
            pe.wait_ge(hT_dve, 1 + KD // 2)

            def last_of_tile(job):
                pe.wait_ge(job_done, INDEX[job] + 1)
                tile_used()

            for g in range(2):
                w = weight_tile()
                for c in range(4 * g, 4 * g + 4):
                    project(("rx", c), w, (c % 4) * P, P, hT)
                    late_modulation(("rx", c))
                last_of_tile(("rx", 4 * g + 3))
                w = weight_tile()
                for c in range(4 * g, 4 * g + 4):
                    project(("ry", c), w, (c % 4) * P, P, hT)
                    if c == 4 * g + 3:
                        last_of_tile(("ry", c))
                    if c == 0:
                        pe.wait_ge(bd_in, 16 * 5)
                    pe.wait_ge(xc_ready, c + 1)
                    for job, gate in (("ra", bd[0]), ("ri", bd[1])):
                        out = start((job, c))
                        for h in range(2):
                            ins = pe.matmul(out[:, h, 0:HALF], gate[:, c, :], rg["xc"][c % 2][:, h * HALF:(h + 1) * HALF],
                                            start=True, stop=True)
                        done(ins)
                    late_modulation(("ry", c))
            for g in range(2):
                w = weight_tile()
                for c in range(4 * g, 4 * g + 4):
                    project(("qk", c), w, (c % 4) * P, P, hT)
                last_of_tile(("qk", 4 * g + 3))
            pe.wait_ge(small_in, 16 * 5)
            project(("al", 0), alpha_w, 0, RANK, hT)
            pe.wait_ge(al_ready, 1)
            for c in range(HEADS):
                out = start(("la", c))
                for h in range(2):
                    ins = pe.matmul(out[:, h, 0:HALF], wa2[0:RANK, c * P:(c + 1) * P], al[0:RANK, h * HALF:(h + 1) * HALF],
                                    start=True, stop=True)
                done(ins)

            def v_transpose(c):
                pe.wait_ge(vf_ready, c + 1)
                out = start(("vt", c))
                for i in range(4):
                    pe.transpose(out[:, 0, i * P:(i + 1) * P], vf[c % 2][:, i * P:(i + 1) * P], ident[:])
                done(pe.transpose(out[0:NS, 1, 0:P], vf[c % 2][:, T:NT], ident[:]))

            for c in range(8):
                if c % 4 == 0:
                    w = weight_tile()
                project(("v", c), w, (c % 4) * P, P, hT)
                if c % 4 == 3:
                    last_of_tile(("v", c))
                if c:
                    v_transpose(c - 1)
            v_transpose(7)
            pe.wait_ge(gla_in_ready, 1)
            for i in range(4):
                out = start(("kt", i))
                for h in range(HEADS):
                    ins = pe.transpose(out[:, 0, h * P:(h + 1) * P], EX[:, h, i * P:(i + 1) * P], ident[:])
                done(ins)
            pe.wait_ge(vt_ready, 8)
            pe.wait_ge(kt_ready, 1)
            for n in range(NCH):
                q, tile = 64 * (n % 2), n // 2
                cols = slice(n * CH, (n + 1) * CH)
                if n >= 1:
                    pe.wait_ge(attm_ready, n)
                for h in range(HEADS):
                    ins = pe.matmul(ps[q:q + 64, 6, h * CH:(h + 1) * CH], Q[:, HEADS + h, cols], Q[:, h, cols],
                                    start=True, stop=True)
                ins.then_inc(at_done, 1)
                out = start(("ds", n))
                for h in range(HEADS):
                    ins = pe.matmul(out[:, h // 2, (h % 2) * DVH:(h % 2 + 1) * DVH],
                                    kout_tok[q:q + 64, tile, h * P:(h + 1) * P],
                                    v_tok[q:q + 64, tile, h * DVH:(h + 1) * DVH], start=True, stop=True)
                done(ins)
                if n % 4 == 0:
                    w = weight_tile()
                gate = start(("gg", n))
                project_half(gate, 0, w, (n % 4) * P, P, hT)
                pe.wait_ge(attm_ready, n + 1)
                if n >= 1:
                    pe.wait_ge(s_ready, n)
                    pe.wait_ge(o_copied, n)
                for hd in range(8):
                    h, d = hd // 2, hd % 2
                    o = ps[:, 7, hd * CH:(hd + 1) * CH]
                    ins = pe.matmul(o, v_tok[q:q + 64, tile, hd * P:(hd + 1) * P], attm[n % 2][q:q + 64, h, :],
                                    start=True, stop=(n == 0))
                    if n:
                        ins = pe.matmul(o, S[n % 2][:, h, d * P:(d + 1) * P], Q[:, h, cols], start=False, stop=True)
                ins.then_inc(o_done, 1)
                done(project_half(gate, 1, w, (n % 4) * P, P, hT))
                if n % 4 == 3:
                    last_of_tile(("gg", n))
                pe.wait_ge(st_ready, n + 1)
                out = start(("os", n))
                for hd in range(8):
                    ins = pe.matmul(out[:, 0, hd:hd + 1], st[n % 2][:, hd // 2, (hd % 2) * P:(hd % 2 + 1) * P],
                                    qs[:, hd // 2, n:n + 1], start=True, stop=True)
                done(ins)

            def squares(h):
                pe.wait_ge(sq_ready, h + 1)
                out = start(("ss", h))
                for half in range(2):
                    for d in range(2):
                        ins = pe.matmul(out[:, half, 0:HALF], ones[:], sq[h % 2][:, d, half * HALF:(half + 1) * HALF],
                                        start=(d == 0), stop=(d == 1))
                done(ins)

            for a, b, src, ready in (("ga", "pa", A, ya_ready), ("gb", "pb", O, yb_ready)):
                for g in range(2):
                    w = weight_tile()
                    for c in range(4 * g, 4 * g + 4):
                        project((a, c), w, (c % 4) * P, P, hT)
                        if a == "ga" and c < 4:
                            squares(c)
                    last_of_tile((a, 4 * g + 3))
                    w = weight_tile()
                    pe.wait_ge(ready, KD)
                    for c in range(4 * g, 4 * g + 4):
                        project((b, c), w, (c % 4) * P, P, src)
                    last_of_tile((b, 4 * g + 3))
            for job, src, m in (("rlT", rl, 11), ("hlT", hl, 9)):
                out = start((job, 0))
                for k in range(KD):
                    ins = pe.transpose(out[0:m, k // 4, (k % 4) * P:(k % 4 + 1) * P], src[:, k, :], ident[:])
                done(ins)

            def route(p):
                i = ORDER[p]
                r = rows(i)
                pe.wait_ge(hf_ready, p + 1)
                out = start(("ht", i))
                for k in range(KD):
                    ins = pe.transpose(out[:, k // 4, (k % 4) * P:(k % 4) * P + r], hf[p % 2][0:r, k * P:(k + 1) * P],
                                       ident[0:r, 0:r])
                done(ins)
                pe.wait_ge(hfT_ready, p + 1)
                out = start(("lg", i))
                for k in range(KD):
                    ins = pe.matmul(out[0:r, 0, 0:NG + NE], hfT[p % 2][:, k, 0:r], route_w[:, k, :],
                                    start=(k == 0), stop=(k == KD - 1))
                done(ins)

            pe.wait_ge(z_ready, KD)
            wo = [weight_tile(), weight_tile()]
            for p, i in enumerate(ORDER):
                r = rows(i)
                out = start(("wo", i))
                if i == 4:
                    for k in range(KD):
                        for g in range(4):
                            ins = pe.matmul(out[32 * g:32 * g + NS, 0, 0:256], Z[:, k, T:NT],
                                            wo[g // 2][:, k, (g % 2) * 256:(g % 2 + 1) * 256],
                                            start=(k == 0), stop=(k == KD - 1))
                for h in range(2 if i < 4 else 0):
                    for k in range(KD):
                        ins = pe.matmul(out[0:r, h, :], Z[:, k, i * P:i * P + r], wo[h][:, k, :],
                                        start=(k == 0), stop=(k == KD - 1))
                done(ins)
                if p >= 1:
                    route(p - 1)
            route(4)
            pe.wait_ge(m_ready, 1)
            out = start(("rk", 0))
            for h, w in enumerate((upper, ones)):
                pe.matmul(out[:, h, 0:4 * NE], w[:], M[:, 0:4, :].rearrange("p t e -> p (t e)"), start=True, stop=True)
                ins = pe.matmul(out[:, h, 4 * NE:5 * NE], w[0:NS, :], M[0:NS, 4, :], start=True, stop=True)
            done(ins)
            pe.wait_ge(named_ready, 1)
            out = start(("table", 0))
            for n in range(2 * TILES):
                r = rows(n // 2)
                ins = pe.matmul(out[0:CAP, 0, 0:2 * NBLK], place_oh[0:r, n, :], named[0:r, n].rearrange("p b c -> p (b c)"),
                                start=(n == 0), stop=(n == 2 * TILES - 1))
            done(ins)
            pe.wait_ge(plan_ready, 1)
            out = start(("plan", 0))
            for k in range(5):
                ins = pe.matmul(out[0:1, 0, k * NBLK:(k + 1) * NBLK], plan_f[:, k:k + 1], ident[:, 0:NBLK],
                                start=True, stop=True)
            done(ins)

            def transpose_rows(j):
                pe.sem_inc(pe_turns, 1)
                for k in range(KD):
                    ins = pe.transpose(ps[:, j, k * CAP:(k + 1) * CAP],
                                       xg[j][0:CAP, :].rearrange("s (p k) -> s k p", k=KD)[:, k, :], ident[0:CAP, 0:CAP])
                ins.then_inc(xt_done[j], 1)

            def gate_up(j, slot):
                for k in range(KD):
                    for q in range(2):
                        ins = pe.matmul(ps[CAP * q:CAP * q + CAP, 2 + j, :], xT[j][:, k, :], ring[3 * slot + q][:, k, :],
                                        start=(k == 0), stop=(k == KD - 1))
                ins.then_inc(gu_done, 1)

            def down(j, slot):
                wd = ring[3 * slot + 2].rearrange("p k n -> p (k n)").rearrange("p (k n) -> p k n", k=4)
                for k in range(4):
                    for q in range(2):
                        ins = pe.matmul(ps[CAP * q:CAP * q + CAP, 4 + j, :], acT[j][:, k, :],
                                        wd[:, k, q * 512:(q + 1) * 512], start=(k == 0), stop=(k == 3))
                ins.then_inc(dn_done, 1)

            pe.wait_ge(started, 1)
            pe.wait_ge(blocks_ready, 1)
            pe.wait_ge(xg_in[0], 16)
            transpose_rows(0)
            n = pe.value_load(plan[0:1, N_BLK:N_BLK + 1], min_val=0, max_val=NBLK)

            def weights_of(b):
                return (pe.value_load(plan[0:1, bass.ds(b + BLK_SLOT, 1)], min_val=0, max_val=3 * WT),
                        pe.value_load(plan[0:1, bass.ds(b + BLK_IN0, 1)], min_val=1, max_val=NE),
                        pe.value_load(plan[0:1, bass.ds(b + BLK_IN1, 1)], min_val=1, max_val=NE))

            def finish(i, j):
                pe.wait_ge(acT_ready[j], i + 2)
                pe.wait_ge(y_ready[j], i * 2 + 1)
                lies, in0, in1 = weights_of(i * 2 + j)
                pe.wait_ge(we_in[2], in0 * 16)
                pe.wait_ge(we_in[5], in1 * 16)
                for slot in range(2):
                    with pe.If(lies < 1 if slot == 0 else lies > 0):
                        down(j, slot)

            def two_blocks(i):
                for j in range(2):
                    with pe.If(n > i * 2 + j):
                        pe.wait_ge(xT_ready[j], i + 2)
                        pe.wait_ge(act_ready[j], i + 1)
                        lies, in0, in1 = weights_of(i * 2 + j)
                        for m in range(2):
                            pe.wait_ge(we_in[m], in0 * 16)
                            pe.wait_ge(we_in[3 + m], in1 * 16)
                        for slot in range(2):
                            with pe.If(lies < 1 if slot == 0 else lies > 0):
                                gate_up(j, slot)
                        pe.wait_ge(xg_in[1 - j], i * 16 + 16 * (1 + j))
                        pe.wait_ge(xT_ready[1 - j], i + (1 + j))
                        transpose_rows(1 - j)
                    if j == 1:
                        with pe.If(n > i * 2):
                            finish(i, 0)
                    elif not isinstance(i, int):
                        with pe.If(n > i * 2 - 1):
                            finish(i - 1, 1)
                    with pe.If(n > i * 2 + j):
                        pe.wait_ge(act_ready[j], i + 2)
                        pe.wait_ge(acT_ready[j], i + 1)
                        pe.sem_inc(pe_turns, 1)
                        for k in range(4):
                            ins = pe.transpose(ps[:, 6 + j, k * CAP:(k + 1) * CAP],
                                               act[j][0:CAP, :].rearrange("s (p k) -> s k p", k=4)[:, k, :],
                                               ident[0:CAP, 0:CAP])
                        ins.then_inc(tr_done[j], 1)

            two_blocks(0)
            with pe.Fori(1, NBLK // 2) as i:
                two_blocks(i)


_INS = ["x_prompt", "x_sample", "state_conv", "state_rglru", "state_gla", "c_prompt", "c_sample", "w_mod", "b_mod",
        "w_in", "b_in", "conv_w", "conv_b", "rg_wa", "rg_ba", "rg_wx", "rg_bx", "rg_lambda", "gla_wa2", "gla_ba",
        "gla_norm_g", "p_a", "p_b", "w_o", "ln1_g", "ln1_b", "w_grp", "b_grp", "w_exp", "b_exp", "we_gate", "we_up",
        "we_down", "ln2_g", "ln2_b"]
_OUTS = [(1, T, D), (NS, 1, D), (1, 1, CONV - 1, D), (1, 1, D), (1, 1, HEADS, DKH, DVH), (1, NS, CONV - 1, D),
         (1, NS, D), (1, NS, HEADS, DKH, DVH)]


def kernel(**inputs):
    import numpy as np
    import concourse.bacc as bacc
    from concourse.bass_utils import run_bass_kernel_spmd as run

    nc = bacc.Bacc("TRN2", target_bir_lowering=False, num_devices=1)
    arrays, t = {}, {}
    for name in _INS:
        a = np.ascontiguousarray(inputs[name])
        arrays[f"in_{name}"] = a
        t[name] = nc.dram_tensor(f"in_{name}", a.shape, mybir.dt.from_np(a.dtype), kind="ExternalInput").ap()
    outs = [nc.dram_tensor(f"out_{i}", s, F32, kind="ExternalOutput").ap() for i, s in enumerate(_OUTS)]
    build(nc, t, outs)
    r = run(nc, [arrays], core_ids=[0])
    return tuple(r.results[0][f"out_{i}"] for i in range(len(_OUTS)))
```
